# Optimizing a Trainium2 kernel written in Bass

```python
import math
import jax, jax.numpy as jnp
from jax import lax
import numpy as np

D_MODEL = 2048
BATCH = 1
SEQ = 256
DEPTH = 2

D_MIX = D_MODEL
ATTN_WIDTH = D_MIX // 2
ATTN_HEAD_DIM = 128
ATTN_HEADS = ATTN_WIDTH // ATTN_HEAD_DIM
ROPE_DIM = ATTN_HEAD_DIM // 4
ROPE_THETA = 500000.0
MOBA_BLOCK = 256
MOBA_TOPK = 3
Q_CHUNK = 16

SSD_WIDTH = D_MIX - ATTN_WIDTH
SSD_HEAD_DIM = 64
SSD_HEADS = SSD_WIDTH // SSD_HEAD_DIM
SSD_GROUPS = 2
SSD_STATE = 128
SSD_CONV = 4
SSD_CHUNK = 128
CONV_DIM = SSD_WIDTH + 2 * SSD_GROUPS * SSD_STATE
IN_DIM = 3 * ATTN_WIDTH + SSD_WIDTH + CONV_DIM + SSD_HEADS

D_FF = 4 * D_MODEL
NORM_EPS = 1e-6

kernel_name = "hymba_moba_ssd_sandwich_trunk"

def rms_norm(x, gain):
    xf = x.astype(jnp.float32)
    inv = lax.rsqrt(jnp.mean(xf * xf, axis=-1, keepdims=True) + NORM_EPS)
    return (xf * inv).astype(x.dtype) * gain

def partial_rope(t, positions):
    half = ROPE_DIM // 2
    inv_freq = ROPE_THETA ** (-jnp.arange(half, dtype=jnp.float32) / half)
    ang = positions.astype(jnp.float32)[:, None, :, None] * inv_freq
    cos, sin = jnp.cos(ang), jnp.sin(ang)
    x1 = t[..., :half]
    x2 = t[..., half:ROPE_DIM]
    rot = jnp.concatenate([x1 * cos - x2 * sin, x2 * cos + x1 * sin], axis=-1).astype(t.dtype)
    return jnp.concatenate([rot, t[..., ROPE_DIM:]], axis=-1)

def moba_attention(q, k, v, positions):
    B_, H, S, Dh = q.shape
    n_blocks = -(-S // MOBA_BLOCK)
    pad = n_blocks * MOBA_BLOCK - S
    q = partial_rope(q, positions) * (Dh ** -0.5)
    k = partial_rope(k, positions)
    kb = jnp.pad(k, ((0, 0), (0, 0), (0, pad), (0, 0))).reshape(B_, H, n_blocks, MOBA_BLOCK, Dh)
    vb = jnp.pad(v, ((0, 0), (0, 0), (0, pad), (0, 0))).reshape(B_, H, n_blocks, MOBA_BLOCK, Dh)
    k_mean = jnp.mean(kb.astype(jnp.float32), axis=3)
    gate = jnp.einsum('bhsd,bhnd->bhsn', q.astype(jnp.float32), k_mean)
    q_block = jnp.arange(S) // MOBA_BLOCK
    past = jnp.arange(n_blocks)[None, :] < q_block[:, None]
    gate = jnp.where(past, gate, -jnp.inf)
    k_sel = min(MOBA_TOPK, n_blocks)
    _, idx = lax.top_k(gate, k_sel)
    valid = idx < q_block[None, None, :, None]

    n_chunks = S // Q_CHUNK
    q_c = q.reshape(B_, H, n_chunks, Q_CHUNK, Dh).transpose(2, 0, 1, 3, 4)
    idx_c = idx.reshape(B_, H, n_chunks, Q_CHUNK, k_sel).transpose(2, 0, 1, 3, 4)
    val_c = valid.reshape(B_, H, n_chunks, Q_CHUNK, k_sel).transpose(2, 0, 1, 3, 4)
    starts = jnp.arange(n_chunks, dtype=jnp.int32) * Q_CHUNK
    b_ix = jnp.arange(B_)[:, None, None, None]
    h_ix = jnp.arange(H)[None, :, None, None]
    key_off = jnp.arange(MOBA_BLOCK)

    def attend_chunk(args):
        qc, ic, vc, start = args
        own = start // MOBA_BLOCK
        k_g = kb[b_ix, h_ix, ic]
        v_g = vb[b_ix, h_ix, ic]
        k_own = lax.dynamic_index_in_dim(kb, own, axis=2, keepdims=False)
        v_own = lax.dynamic_index_in_dim(vb, own, axis=2, keepdims=False)
        s_sel = jnp.einsum('bhqd,bhqjkd->bhqjk', qc, k_g).astype(jnp.float32)
        s_sel = jnp.where(vc[..., None], s_sel, -jnp.inf).reshape(B_, H, Q_CHUNK, k_sel * MOBA_BLOCK)
        s_own = jnp.einsum('bhqd,bhkd->bhqk', qc, k_own).astype(jnp.float32)
        q_pos = start + jnp.arange(Q_CHUNK)
        k_pos = own * MOBA_BLOCK + key_off
        s_own = jnp.where(k_pos[None, :] <= q_pos[:, None], s_own, -jnp.inf)
        p = jax.nn.softmax(jnp.concatenate([s_sel, s_own], axis=-1), axis=-1).astype(v.dtype)
        p_sel = p[..., :k_sel * MOBA_BLOCK].reshape(B_, H, Q_CHUNK, k_sel, MOBA_BLOCK)
        p_own = p[..., k_sel * MOBA_BLOCK:]
        return (jnp.einsum('bhqjk,bhqjkd->bhqd', p_sel, v_g)
                + jnp.einsum('bhqk,bhkd->bhqd', p_own, v_own))

    out = lax.map(attend_chunk, (q_c, idx_c, val_c, starts))
    return out.transpose(1, 2, 0, 3, 4).reshape(B_, H, S, Dh)

def causal_depthwise_conv(x, w, b):
    K, C = w.shape
    out = lax.conv_general_dilated(x, w[:, None, :], window_strides=(1,), padding=[(K - 1, 0)],
                                   dimension_numbers=('NWC', 'WIO', 'NWC'), feature_group_count=C)
    return out + b

def segsum(x):
    T = x.shape[-1]
    xr = jnp.broadcast_to(x[..., :, None], x.shape + (T,))
    xr = jnp.where(jnp.tril(jnp.ones((T, T), dtype=bool), -1), xr, 0.0)
    cs = jnp.cumsum(xr, axis=-2)
    return jnp.where(jnp.tril(jnp.ones((T, T), dtype=bool)), cs, -jnp.inf)

def ssd_scan(x, a_dt, Bm, Cm):
    B_, S, H, P = x.shape
    G, N = Bm.shape[2], Bm.shape[3]
    E = H // G
    L = SSD_CHUNK
    nc = S // L
    xc = x.reshape(B_, nc, L, G, E, P)
    Bc = Bm.reshape(B_, nc, L, G, N)
    Cc = Cm.reshape(B_, nc, L, G, N)
    a = a_dt.reshape(B_, nc, L, G, E).transpose(0, 3, 4, 1, 2)
    a_cs = jnp.cumsum(a, axis=-1)
    decay_in = jnp.exp(segsum(a)).astype(x.dtype)
    cb = jnp.einsum('bclgn,bcsgn->bcgls', Cc, Bc)
    y_diag = jnp.einsum('bcgls,bgecls,bcsgep->bclgep', cb, decay_in, xc)
    decay_to_end = jnp.exp(a_cs[..., -1:] - a_cs).astype(x.dtype)
    chunk_states = jnp.einsum('bclgn,bgecl,bclgep->bcgepn', Bc, decay_to_end, xc)
    chunk_decay = jnp.exp(a_cs[..., -1]).astype(x.dtype)

    def step(state, inp):
        dec, new = inp
        return state * dec[..., None, None] + new, state

    init = jnp.zeros((B_, G, E, P, N), x.dtype)
    _, prev = lax.scan(step, init, (chunk_decay.transpose(3, 0, 1, 2),
                                    chunk_states.transpose(1, 0, 2, 3, 4, 5)))
    prev = prev.transpose(1, 0, 2, 3, 4, 5)
    y_off = jnp.einsum('bclgn,bcgepn,bgecl->bclgep', Cc, prev, jnp.exp(a_cs).astype(x.dtype))
    return (y_diag + y_off).reshape(B_, S, H, P)

def hybrid_mixer(h, positions, w_in, conv_w, conv_b, dt_bias, a_log, d_skip,
                 attn_out_norm, ssd_out_norm, w_out):
    B_, S, _ = h.shape
    proj = h @ w_in
    o1 = ATTN_WIDTH
    o2 = 2 * ATTN_WIDTH
    o3 = 3 * ATTN_WIDTH
    o4 = o3 + SSD_WIDTH
    o5 = o4 + CONV_DIM
    q, k, v, z, xbc, dt = jnp.split(proj, [o1, o2, o3, o4, o5], axis=-1)

    def heads(t):
        return t.reshape(B_, S, ATTN_HEADS, ATTN_HEAD_DIM).transpose(0, 2, 1, 3)
    attn = moba_attention(heads(q), heads(k), heads(v), positions)
    attn = attn.transpose(0, 2, 1, 3).reshape(B_, S, ATTN_WIDTH)
    attn = rms_norm(attn, attn_out_norm)

    xbc = jax.nn.silu(causal_depthwise_conv(xbc, conv_w, conv_b))
    xs, Bm, Cm = jnp.split(xbc, [SSD_WIDTH, SSD_WIDTH + SSD_GROUPS * SSD_STATE], axis=-1)
    dt = jax.nn.softplus(dt.astype(jnp.float32) + dt_bias.astype(jnp.float32))
    a = -jnp.exp(a_log.astype(jnp.float32))
    xh = xs.reshape(B_, S, SSD_HEADS, SSD_HEAD_DIM)
    y = ssd_scan(xh * dt[..., None].astype(xh.dtype), dt * a,
                 Bm.reshape(B_, S, SSD_GROUPS, SSD_STATE), Cm.reshape(B_, S, SSD_GROUPS, SSD_STATE))
    y = y + d_skip[:, None] * xh
    y = y.reshape(B_, S, SSD_WIDTH) * jax.nn.silu(z)
    y = rms_norm(y.reshape(B_, S, SSD_GROUPS, SSD_WIDTH // SSD_GROUPS),
                 ssd_out_norm.reshape(SSD_GROUPS, SSD_WIDTH // SSD_GROUPS)).reshape(B_, S, SSD_WIDTH)

    mix = jnp.concatenate([attn, y], axis=-1)
    return mix @ w_out

def setup_inputs(seed: int = 0) -> dict:
    key = jax.random.key(seed)
    ks = jax.random.split(key, 18)
    f32 = jnp.float32

    def normal(k, shape, scale):
        return jax.random.normal(k, shape, f32) * scale

    def gain(k, shape):
        return 1.0 + 0.05 * jax.random.normal(k, shape, f32)

    x = jax.random.normal(ks[0], (BATCH, SEQ, D_MODEL), f32)
    offset = jax.random.randint(ks[1], (BATCH, 1), 0, 4096, dtype=jnp.int32)
    positions = offset + jnp.arange(SEQ, dtype=jnp.int32)[None, :]
    dt_init = jnp.exp(jax.random.uniform(ks[9], (DEPTH, SSD_HEADS), f32,
                                         math.log(1e-3), math.log(1e-1)))
    dt_bias = dt_init + jnp.log(-jnp.expm1(-dt_init))
    a_log = jnp.log(jax.random.uniform(ks[10], (DEPTH, SSD_HEADS), f32, 1.0, 16.0))
    return {
        "x": x,
        "positions": positions,
        "pre_mix_norm": gain(ks[2], (DEPTH, D_MODEL)),
        "post_mix_norm": gain(ks[3], (DEPTH, D_MODEL)),
        "pre_mlp_norm": gain(ks[4], (DEPTH, D_MODEL)),
        "post_mlp_norm": gain(ks[5], (DEPTH, D_MODEL)),
        "w_in": normal(ks[6], (DEPTH, D_MODEL, IN_DIM), D_MODEL ** -0.5),
        "conv_w": normal(ks[7], (DEPTH, SSD_CONV, CONV_DIM), SSD_CONV ** -0.5),
        "conv_b": normal(ks[8], (DEPTH, CONV_DIM), 0.01),
        "dt_bias": dt_bias,
        "a_log": a_log,
        "d_skip": gain(ks[11], (DEPTH, SSD_HEADS)),
        "attn_out_norm": gain(ks[12], (DEPTH, ATTN_WIDTH)),
        "ssd_out_norm": gain(ks[13], (DEPTH, SSD_WIDTH)),
        "w_out": normal(ks[14], (DEPTH, D_MIX, D_MODEL), D_MIX ** -0.5),
        "w_up": normal(ks[15], (DEPTH, D_MODEL, D_FF), D_MODEL ** -0.5),
        "w_down": normal(ks[16], (DEPTH, D_FF, D_MODEL), D_FF ** -0.5),
    }

def reference(x, positions, pre_mix_norm, post_mix_norm, pre_mlp_norm, post_mlp_norm,
              w_in, conv_w, conv_b, dt_bias, a_log, d_skip, attn_out_norm, ssd_out_norm,
              w_out, w_up, w_down):
    for l in range(DEPTH):
        h = rms_norm(x, pre_mix_norm[l])
        h = hybrid_mixer(h, positions, w_in[l], conv_w[l], conv_b[l], dt_bias[l], a_log[l],
                         d_skip[l], attn_out_norm[l], ssd_out_norm[l], w_out[l])
        x = x + rms_norm(h, post_mix_norm[l])
        h = rms_norm(x, pre_mlp_norm[l])
        h = jnp.square(jax.nn.relu(h @ w_up[l])) @ w_down[l]
        x = x + rms_norm(h, post_mlp_norm[l])
    return x


_drawn_inputs = setup_inputs


def setup_inputs(seed=0):
    import zlib

    import numpy as np

    out = dict(_drawn_inputs(seed))
    spreads = {}
    factors = {'conv_b': 6.096}
    for name, (base, spread) in spreads.items():
        noise = np.random.default_rng([zlib.crc32(name.encode()), seed]).standard_normal(out[name].shape)
        drawn = base * np.exp(spread * noise) if base else spread * noise
        out[name] = __import__('jax').numpy.asarray(drawn.astype(out[name].dtype))
    for name, factor in factors.items():
        out[name] = (out[name] * factor).astype(out[name].dtype)
    return out
```

```python
from contextlib import ExitStack

import numpy as np

import concourse.bass as bass
from concourse import mybir

ALU = mybir.AluOpType
ACT = mybir.ActivationFunctionType
AX = mybir.AxisListType
F32 = mybir.dt.float32
F32R = mybir.dt.float32r
I32 = mybir.dt.int32
BF16 = mybir.dt.bfloat16

P = 128
DEPTH, D, SEQ, DFF = 2, 2048, 256, 8192
TT = SEQ // P
KT = D // P
HEADS, DH, ROPE, THETA = 8, 128, 32, 500000.0
HALF = ROPE // 2
AW = HEADS * DH
SH, SP_, SG, SN, TAPS = 16, 64, 2, 128, 4
SW = SH * SP_
CONV = SW + 2 * SG * SN
EPS = 1e-6
NEG = -3e38

RING = 4
CK = 2
CB = 512
NC = KT // CK
W = CK * CB
AHEAD = 3

B_XBC, B_Q, B_K, B_V, B_Z, B_OUT, B_MLP = 0, 3, 5, 7, 9, 11, 15
QUARTERS = 4
QB = DFF // QUARTERS // CB
NB = B_MLP + QUARTERS * 2 * QB
MIX_SLOTS = B_MLP * NC

COL_Q, COL_K, COL_V, COL_Z, COL_XBC = 0, AW, 2 * AW, 3 * AW, 3 * AW + SW
COL_DT = COL_XBC + CONV

NCT = CONV // P
G_MIX, G_MLP, G_ATTN, G_SSD = 0, KT, 2 * KT, 2 * KT + AW // P
G_TAP = G_SSD + SW // P
G_BIAS = G_TAP + TAPS * NCT
NPRM = G_BIAS + NCT

PE_DT, PE_DT_TURN, PE_DECAY, PE_XTOK, PE_CB, PE_STATE = 7, 10, 17, 20, 28, 31
PE_SEG = [34 + 2 * i for i in range(8)]
PE_YD = [36 + 2 * i for i in range(8)]
PE_YOFF = [46, 50]
PE_SCORE = [59 + 5 * p for p in range(4)]
PE_PT = [s + 3 for s in PE_SCORE]
PE_PV = [s + 6 for s in PE_SCORE]
PE_ATTNT = [84, 85, 86, 87]
PE_SSDT = [83, 85, 90, 91]
AD_DIAG, AD_DTT, AD_DT, AD_DECAY, AD_XTOK, AD_XDT, AD_CB, AD_STATE = 5, 11, 14, 21, 24, 30, 32, 35
AD_SEG = [38 + 2 * i for i in range(8)]
AD_Y = [42 + 4 * j for j in range(4)]
AD_ROPE = [37, 39, 45, 47, 53, 55, 60, 62]
AD_SOFT = [s + 4 for s in PE_SCORE]
AD_PT = [s + 7 for s in PE_SCORE]
AD_O = [s + 10 for s in PE_SCORE]
AD_ATTN_NORM = 85
AD_ATTNT = [88, 89, 90, 91]
AD_SSDT = [87, 89, 94, 95]
ATTNT_BANK, SSDT_BANK = [0, 1, 3, 0], [2, 2, 2, 3]

X_SUM, X_MS, X_INV, X_INV2, Y_SUM, Y_MS, Y_INV, A_MS, A_INV, S0_MS, S0_INV, S1_MS, S1_INV = range(13)
NST = 13
DT_IN, DT_ABS, DT_EXP, DT_TMP, DT_S, DT_S2, DT, A_DT = range(8)

SQ_X0, SQ_S0, SQ_A, SQ_S1, SQ_Y0, SQ_X1 = 8, 10, 12, 14, 22, 30
SQ_Y1 = SQ_X1 + TT * QUARTERS * QB
DVE_LINKS, POOL_LINKS = 36, 1


def leaves(b):
    return NC * (b + 1) + AHEAD - 1


def trunk(nc, x, positions, pre_mix_norm, post_mix_norm, pre_mlp_norm, post_mlp_norm, w_in, conv_w,
          conv_b, dt_bias, a_log, d_skip, attn_out_norm, ssd_out_norm, w_out, w_up, w_down, out):
    ctx = ExitStack()
    with ctx:
        def sb(name, shape, dt=F32):
            return ctx.enter_context(nc.sbuf_tensor(name, shape, dt))

        raw = sb("raw", [P, RING, W])
        w_hi = sb("w_hi", [P, RING, W], F32R)
        w_lo = sb("w_lo", [P, RING, W], F32R)
        x_sb = sb("x_sb", [P, TT, D])
        a_hi = sb("a_hi", [P, KT, SEQ], F32R)
        a_lo = sb("a_lo", [P, KT, SEQ], F32R)
        u_hi = sb("u_hi", [P, KT, SEQ], F32R)
        u_lo = sb("u_lo", [P, KT, SEQ], F32R)
        ybuf = sb("ybuf", [P, TT * D])
        xbcT = sb("xbcT", [P, NCT, SEQ])
        x_tok = sb("x_tok", [P, TT, SW])
        v_tok = sb("v_tok", [P, TT, AW])
        zg = sb("zg", [P, D])
        b_tok = sb("b_tok", [P, SG, SN])
        convr = sb("convr", [P, 2, 2, TAPS - 1 + SEQ])
        wk = sb("wk", [P, 4, CB])
        cbm = sb("cbm", [P, TT * SG, P])
        wdt_hi = sb("wdt_hi", [P, KT * SH + P - SH], F32R)
        wdt_lo = sb("wdt_lo", [P, KT * SH + P - SH], F32R)
        ident = sb("ident", [P, P])
        tri = sb("tri", [P, P])
        low = sb("low", [P, P], F32R)
        cmask = sb("cmask", [P, P], BF16)
        ident_b = sb("ident_b", [P, P], BF16)
        ones = sb("ones", [P, P])
        cosT = sb("cosT", [ROPE, SEQ])
        sinT = sb("sinT", [ROPE, SEQ])
        inv_row = sb("inv_row", [P, SEQ])
        prm_all = sb("prm_all", [P, DEPTH, NPRM])
        row_all = sb("row_all", [P, DEPTH, 3, SH])
        prm = sb("prm", [P, NPRM])
        row = sb("row", [P, 3, SH])
        minus_half = sb("minus_half", [P, 2])
        pos = sb("pos", [P, TT], I32)
        sq = sb("sq", [P, TT, 4])
        ysq = sb("ysq", [P, TT, 4])
        st = sb("st", [P, NST, TT])
        dts = sb("dts", [P, 8, TT, SH])
        adt_hi = sb("adt_hi", [P, TT, SH], F32R)
        adt_lo = sb("adt_lo", [P, TT, SH], F32R)
        decay = sb("decay", [P, 2, SH])
        mx = sb("mx", [P, 4])
        rs = sb("rs", [P, 4])
        rinv = sb("rinv", [P, 4])
        ssq = sb("ssq", [P, 3, TT])

        acc = [[ctx.enter_context(nc.psum_tensor(f"acc{i}{j}", [P, CB], F32)) for j in range(2)]
               for i in range(2)]
        M = [ctx.enter_context(nc.psum_tensor(f"M{i}", [P, CB], F32)) for i in range(4)]

        qk = ybuf[:, :].rearrange("p (h s) -> p h s", s=SEQ)
        attn = ybuf[:, 0:TT * AW].rearrange("p (h t d) -> p h t d", t=TT, d=DH)
        y = ybuf[:, :].rearrange("p (t n) -> p t n", t=TT)
        ys = xbcT[:, 0:SW // P, :].rearrange("p a s -> p (a s)").rearrange("p (t n) -> p t n", t=TT)
        zs = zg[:, :].rearrange("p (t n) -> p t n", t=TT)
        rope_t = convr[0:ROPE, 0, :, TAPS - 1:]
        wdt = wk[:, 3, 0:KT * SH]
        dtT = wk[:, 0, 0:SEQ]
        seg_hi = [u_hi[:, 2 * i:2 * i + 2].rearrange("p k s -> p (k s)") for i in range(2)]
        seg_lo = [u_lo[:, 2 * i:2 * i + 2].rearrange("p k s -> p (k s)") for i in range(2)]
        seg_e = wk[:, 1]
        low_w, cmask_w, wdt_w = v_tok[:, 0, 0:P], v_tok[:, 0, P:2 * P], v_tok[:, 0, 2 * P:3 * P - SH]
        probs = wk[:, 0:2].rearrange("p a n -> p (a n)")
        probsT = wk[:, 2:4].rearrange("p a n -> p (a n)")
        diag = wk[:, 1, 0:SEQ].rearrange("p (t n) -> p t n", t=TT)
        junk = cbm[:, :, :].rearrange("p a n -> p (a n)")

        up_banks = 2 * QB * QUARTERS
        per = dict(
            hi_ready=NB * NC,
            split_done=NB * NC,
            mm_done=NB * NC,
            x_ready=16,
            xT_mm=16, xT_hi=16, xT_ready=16,
            x_ms=2, x_inv=2, x_inv2=1,
            diag_ready=1, diag_mm=1, inv_row_ready=1,
            prm_ready=1, wdt_landed=16, wdt_hi_ready=1, wdt_ready=1,
            dt_mm=1, dtT_ready=1, dt_turned=1, dt_abs=1, dt_exp=1, adt_hi_ready=1, adt_ready=1, decay_mm=1, decay_ready=1,
            conv_step=48, silu_ready=3,
            xtok_mm=4, xtok_ready=4, skip_done=4, xdt_ready=4, xdd_ready=2,
            btok_mm=1, btok_ready=1, cb_mm=1, cbm_ready=1, state_mm=1, state_ready=1,
            sega_hi=8, sega_ready=8, seg_mm=8, sege_ready=8, segm_ready=8, yd_mm=8, yoff_mm=2,
            y_added=4, yoff_mul=2, yoff_added=2,
            rope_swapped=8, rope_mul=8, rope_cos=8, rope_ready=8,
            score_mm=4, nmax_ready=4, probs_ready=4, pt_mm=4, pt_a=4, pt_v=4, pv_mm=4, attn_out=4,
            attn_ms=1, attn_inv=1, attn_ready=1, attnT_mm=4, attnT_hi=4, attnT_ready=4,
            gated=2, ssd_ms=2, ssd_inv=2, ssd_ready=2, ssdT_mm=4, ssdT_hi=4, ssdT_ready=4,
            squared=SQ_Y1,
            gain_landed=32, y_ms=2, y_pow=1, y_inv=2, y_scaled=16, y_zero=1,
            u_hi_ready=up_banks,
            u_sq=up_banks,
            u_ready=up_banks,
            dve_chain=DVE_LINKS, pool_chain=POOL_LINKS,
        )
        sem = {n: ctx.enter_context(nc.semaphore(n)) for n in per}
        raw_landed = [ctx.enter_context(nc.semaphore(f"raw_landed{s}")) for s in range(RING)]
        acc_free = [ctx.enter_context(nc.semaphore(f"acc_free{i}")) for i in range(2)]
        names = ["x_landed", "const_step", "const_ready", "typed_ready", "prm_landed", "row_landed", "row_exp", "row_ready",
                 "pos_landed", "table_step", "table_angle", "table_sin", "table_mm", "table_ready", "prm_mm",
                 "prm_copied", "out_landed"]
        once = {n: ctx.enter_context(nc.semaphore(n)) for n in names}

        def upto(name, l, n):
            return sem[name], l * per[name] + n

        def chunk(b, c):
            return b * NC + c

        def through(l, b):
            return sem["mm_done"], RING + chunk(l * NB + b + 1, 0)

        def left(l, b, n, pairs=0):
            return acc_free[b % 2], 2 * (l * ((NB + 1 - b % 2) // 2) + b // 2 + pairs) + 2 + n

        def heads8(a, t, g):
            return a[:, t, g * CB:(g + 1) * CB].rearrange("p (h n) -> p h n", h=SH // SG)

        def per_head(a, g):
            n = SH // SG
            return a[:, g * n:(g + 1) * n].unsqueeze(2).broadcast_to([P, n, SP_])

        def four(a):
            return a.rearrange("p (h n) -> p h n", h=4)

        block = ctx.enter_context(nc.Block())

        @block.sync
        def _(sp):
            for t in range(TT):
                sp.dma_start(x_sb[:, t], x[0, t * P:(t + 1) * P, :]).then_inc(once["x_landed"], 16)

            def load(b, c, src):
                sp.wait_ge(sem["split_done"], chunk(b, c) + 1)
                sp.dma_start(raw[:, c % RING].rearrange("p (k n) -> p k n", k=CK),
                             src.rearrange("(k p) n -> p k n", p=P)).then_inc(raw_landed[c % RING], 16)

            def load_block(b, w, l, r0, c0):
                for c in range(NC):
                    load(b, c, w[l, bass.ds(r0 + c * CK * P, CK * P), bass.ds(c0, CB)])

            with sp.Fori(0, DEPTH) as l:
                for b0, n, c0 in ((B_XBC, B_Q - B_XBC, COL_XBC), (B_Q, B_OUT - B_Q, COL_Q)):
                    with sp.Fori(0, n) as i:
                        load_block(l * NB + b0 + i, w_in, l, 0, i * CB + c0)
                with sp.Fori(0, B_MLP - B_OUT) as i:
                    load_block(l * NB + B_OUT + i, w_out, l, 0, i * CB)
                with sp.Fori(0, QUARTERS) as q:
                    with sp.Fori(0, QB) as i:
                        load_block(l * NB + q * (2 * QB) + i + B_MLP, w_up, l, 0, q * (QB * CB) + i * CB)
                    with sp.Fori(0, QB) as i:
                        load_block(l * NB + q * (2 * QB) + i + (B_MLP + QB), w_down, l, q * (QB * CB), i * CB)
            for c in range(AHEAD):
                load(DEPTH * NB, c, w_in[0, c * CK * P:(c + 1) * CK * P, COL_XBC:COL_XBC + CB])
            for c in range(4):
                sp.wait_ge(*upto("x_ready", DEPTH, 2 * (c + 1)))
                for t in range(TT):
                    sp.dma_start(out[0, t * P:(t + 1) * P, c * CB:(c + 1) * CB],
                                 x_sb[:, t, c * CB:(c + 1) * CB]).then_inc(once["out_landed"], 16)
            for s in range(RING):
                sp.wait_ge(raw_landed[s], 16 * (2 * DEPTH * NB + (1 if s < AHEAD else 0)))
            sp.wait_ge(once["out_landed"], 16 * 4 * TT)

        @block.gpsimd
        def _(pool):
            step, ready = once["const_step"], once["const_ready"]
            pool.memset(sq[:], 0.0).then_inc(sem["mm_done"], RING)
            pool.memset(ysq[:], 0.0).then_inc(acc_free[0], 2)
            pool.memset(minus_half[:], -0.5).then_inc(acc_free[1], 2)
            pool.memset(ident[:], 0.0).then_inc(step, 1)
            pool.memset(tri[:], 1.0).then_inc(step, 1)
            pool.memset(low_w[:], 1.0).then_inc(step, 1)
            pool.memset(cmask_w[:], 0.0).then_inc(step, 1)
            pool.memset(ones[:], 1.0).then_inc(ready, 1)
            pool.memset(convr[:, :, :, 0:TAPS - 1], 0.0).then_inc(ready, 1)
            pool.wait_ge(step, 4)
            pool.affine_select(out=ident[:], in_=ident[:], compare_op=ALU.not_equal, fill=1.0, base=0,
                               pattern=[[-1, P]], channel_multiplier=1).then_inc(ready, 1)
            pool.affine_select(out=tri[:], in_=tri[:], compare_op=ALU.is_ge, fill=0.0, base=0,
                               pattern=[[1, P]], channel_multiplier=-1).then_inc(ready, 1)
            pool.affine_select(out=low_w[:], in_=low_w[:], compare_op=ALU.is_gt, fill=0.0, base=0,
                               pattern=[[-1, P]], channel_multiplier=1).then_inc(step, 1)
            pool.affine_select(out=cmask_w[:], in_=cmask_w[:], compare_op=ALU.is_ge, fill=NEG, base=0,
                               pattern=[[-1, P]], channel_multiplier=1).then_inc(step, 1)
            pool.memset(wdt_w[:], 0.0).then_inc(step, 1)
            for i, a in enumerate((dt_bias, a_log, d_skip)):
                for l in range(DEPTH):
                    pool.dma_start(row_all[:, l, i], a[l].partition_broadcast(P))\
                        .then_inc(once["row_landed"], 16)

            with pool.Fori(0, DEPTH) as l:
                links = [0]

                def link(ins):
                    links[0] += 1
                    ins.then_inc(sem["pool_chain"], 1)
                    pool.wait_ge(*upto("pool_chain", l, links[0]))

                def power(name, n, k_out, k_in, waited, w_n):
                    pool.wait_ge(*upto(waited, l, w_n))
                    return pool.tensor_tensor(st[:, k_out], st[:, k_in], minus_half[:], ALU.pow)

                pool.wait_ge(once["prm_copied"], DEPTH)
                pool.wait_ge(once["row_ready"], 1)
                pool.wait_ge(*upto("x_ready", l, 8))
                pool.tensor_copy(row[:].rearrange("p i n -> p (i n)"),
                                 row_all[:].rearrange("p l i n -> p (l i n)")[:, bass.ds(l * (3 * SH), 3 * SH)])
                pool.tensor_copy(prm[:], prm_all[:].rearrange("p l n -> p (l n)")[:, bass.ds(l * NPRM, NPRM)])\
                    .then_inc(sem["prm_ready"], 1)
                pool.dma_start(wdt.rearrange("p (k n) -> p k n", n=SH), w_in[bass.ds(l, 1), :, COL_DT:COL_DT + SH]
                               .rearrange("a (k p) n -> p (a k) n", p=P)).then_inc(sem["wdt_landed"], 16)
                power("x_inv", 1, X_INV, X_MS, "x_ms", 1).then_inc(sem["x_inv"], 1)
                pool.wait_ge(*upto("xtok_ready", l, 4))
                for i in range(TT * SG):
                    t, g = divmod(i, SG)
                    pool.tensor_tensor(heads8(ys, t, g), heads8(x_tok, t, g), per_head(row[:, 2], g),
                                       ALU.mult).then_inc(sem["skip_done"], 1)

                def seg_weights(i):
                    t, g, hh = i // 4, i // 2 % 2, i % 2
                    h0 = g * 8 + hh * 4
                    if i >= 2:
                        pool.wait_ge(*upto("seg_mm", l, i - 1))
                    for dst, a, done in ((seg_hi, adt_hi, "sega_hi"), (seg_lo, adt_lo, "sega_ready")):
                        pool.tensor_tensor(four(dst[i % 2]), tri[:].unsqueeze(1).broadcast_to([P, 4, P]),
                                           a[:, t, h0:h0 + 4].bitcast(F32).unsqueeze(2)
                                           .broadcast_to([P, 4, P]), ALU.mult).then_inc(sem[done], 1)

                def rope_cos(r):
                    pool.wait_ge(*upto("rope_swapped", l, r + 1))
                    pool.tensor_tensor(qk[0:ROPE, 2 * r:2 * r + 2], qk[0:ROPE, 2 * r:2 * r + 2],
                                       cosT[:].unsqueeze(1).broadcast_to([ROPE, 2, SEQ]),
                                       ALU.mult).then_inc(sem["rope_cos"], 1)

                for slot in range(PE_SEG[0] - 3, AD_ROPE[-1] + 1):
                    if slot + 3 in PE_SEG:
                        seg_weights(PE_SEG.index(slot + 3))
                    if slot + 2 in AD_ROPE:
                        rope_cos(AD_ROPE.index(slot + 2))
                power("ssd", 1, S0_INV, S0_MS, "ssd_ms", 1).then_inc(sem["ssd_inv"], 1)
                power("attn", 1, A_INV, A_MS, "attn_ms", 1).then_inc(sem["attn_inv"], 1)
                power("ssd", 2, S1_INV, S1_MS, "ssd_ms", 2).then_inc(sem["ssd_inv"], 1)
                power("y", 1, Y_INV, Y_MS, "y_ms", 1).then_inc(sem["y_inv"], 1)
                power("x_inv", 2, X_INV, X_MS, "x_ms", 2).then_inc(sem["x_inv"], 1)
                pool.wait_ge(*upto("x_inv", l, 2))
                pool.tensor_tensor(st[:, X_INV2], st[:, X_INV], st[:, X_INV], ALU.mult)\
                    .then_inc(sem["x_inv2"], 1)
                link(power("y", 2, Y_INV, Y_MS, "y_ms", 2))
                pool.tensor_tensor(st[:, Y_INV], st[:, Y_INV], st[:, X_INV2], ALU.mult)\
                    .then_inc(sem["y_inv"], 1)
                assert links[0] == POOL_LINKS

        @block.scalar
        def _(act):
            for l in range(DEPTH):
                for r0, n, a in ((G_MIX, KT, pre_mix_norm[l]), (G_MLP, KT, pre_mlp_norm[l]),
                                 (G_ATTN, AW // P, attn_out_norm[l]), (G_SSD, SW // P, ssd_out_norm[l]),
                                 (G_TAP, TAPS * NCT, conv_w[l].rearrange("k n -> (k n)")),
                                 (G_BIAS, NCT, conv_b[l])):
                    act.dma_start(probs[r0:r0 + n, l * P:(l + 1) * P], a.rearrange("(r n) -> r n", n=P))\
                        .then_inc(once["prm_landed"], 16)
            with nc.allow_non_contiguous_dma(reason="256 positions, a token a partition"):
                act.dma_start(pos[:], positions[0].rearrange("(t p) -> p t", p=P))\
                    .then_inc(once["pos_landed"], 16)
            act.wait_ge(once["row_landed"], 16 * 3 * DEPTH)
            act.activation(row_all[:, :, 1], row_all[:, :, 1], ACT.Exp).then_inc(once["row_exp"], 1)
            act.wait_ge(once["prm_mm"], DEPTH)
            for l in range(DEPTH):
                act.activation(prm_all[:, l], M[l][:, 0:NPRM], ACT.Copy).then_inc(once["prm_copied"], 1)
            act.wait_ge(once["table_angle"], 1)
            act.activation(four(wk[:, 3])[:, :, 0:ROPE], four(wk[:, 2])[:, :, 0:ROPE], ACT.Sin)\
                .then_inc(once["table_sin"], 1)
            act.wait_ge(once["table_mm"], 1)
            act.activation(cosT[:], M[2][0:ROPE, 0:SEQ], ACT.Copy).then_inc(once["table_ready"], 1)
            act.activation(sinT[:], M[2][0:ROPE, SEQ:2 * SEQ], ACT.Copy).then_inc(once["table_ready"], 1)

            def round_hi(b, c):
                act.wait_ge(raw_landed[c % RING], (b * (NC // RING) + c // RING + 1) * 16)
                act.wait_ge(sem["mm_done"], chunk(b, c) + 1)
                act.activation(w_hi[:, c % RING], raw[:, c % RING], ACT.Copy).then_inc(sem["hi_ready"], 1)

            for c in range(AHEAD):
                round_hi(0, c)
            with act.Fori(0, DEPTH) as l:
                squares = [0]

                def square(in_, total, extra=0):
                    if squares[0] or extra:
                        act.wait_ge(*upto("squared", l, squares[0] + extra))
                    act.activation(junk, in_, ACT.Square, accum_out=total).then_inc(sem["squared"], 1)
                    squares[0] += 1

                def load_gain(gains):
                    act.dma_start(zg[:], gains[bass.ds(l, 1)].rearrange("a n -> (a n)").partition_broadcast(P))\
                        .then_inc(sem["gain_landed"], 16)

                def norm_in(n, gain):
                    for c in range(4):
                        for j in (2 * c, 2 * c + 1):
                            act.wait_ge(*upto("xT_mm", l, 8 * n + j + 1))
                            for kk in range(2):
                                k = 2 * j + kk
                                ins = act.activation(a_hi[:, k], M[j % 4][:, kk * SEQ:(kk + 1) * SEQ], ACT.Copy,
                                                     scale=prm[:, gain + k:gain + k + 1])
                            ins.then_inc(sem["xT_hi"], 1)
                        for t in range(TT):
                            square(x_sb[:, t, c * CB:(c + 1) * CB], sq[:, t, c:c + 1])

                def to_hi(name, n, j, bank, gain):
                    act.wait_ge(*upto(name + "_mm", l, n))
                    for kk in range(2):
                        k = 2 * j + kk
                        ins = act.activation(u_hi[:, k], M[bank][:, kk * SEQ:(kk + 1) * SEQ], ACT.Copy,
                                             scale=prm[:, gain + k:gain + k + 1])
                    ins.then_inc(sem[name + "_hi"], 1)

                act.wait_ge(*upto("prm_ready", l, 1))
                norm_in(0, G_MIX)
                act.wait_ge(*upto("wdt_landed", l, 16))
                act.activation(wdt_hi[:, 0:KT * SH], wdt, ACT.Copy).then_inc(sem["wdt_hi_ready"], 1)
                for slot in range(AHEAD, MIX_SLOTS + AHEAD):
                    b, c = divmod(slot, NC)
                    round_hi(l * NB + b, c)
                    if slot == leaves(0):
                        act.wait_ge(*upto("diag_mm", l, 1))
                        act.activation(inv_row[:], M[0][:, 0:SEQ], ACT.Copy).then_inc(sem["inv_row_ready"], 1)
                    if slot == AD_DT:
                        act.wait_ge(*upto("dt_abs", l, 1))
                        act.activation(dts[:, DT_EXP], dts[:, DT_ABS], ACT.Exp, scale=-1.0)\
                            .then_inc(sem["dt_exp"], 1)
                    if slot == AD_DECAY:
                        act.wait_ge(*upto("decay_mm", l, 1))
                        act.activation(decay[:].rearrange("p a n -> p (a n)"), M[0][:, 0:2 * SH], ACT.Exp)\
                            .then_inc(sem["decay_ready"], 1)
                    for i in range(3):
                        if slot == leaves(i) + 3:
                            act.wait_ge(*upto("conv_step", l, 16 * (i + 1)))
                            act.activation(xbcT[:, 4 * i:4 * i + 4], xbcT[:, 4 * i:4 * i + 4], ACT.Silu)\
                                .then_inc(sem["silu_ready"], 1)
                    for i in range(TT * SG):
                        if slot == AD_XTOK + i:
                            t, g = divmod(i, SG)
                            act.wait_ge(*upto("xtok_mm", l, i + 1))
                            act.activation(x_tok[:, t, g * CB:(g + 1) * CB], M[i][:], ACT.Copy)\
                                .then_inc(sem["xtok_ready"], 1)
                    if slot == AD_CB:
                        act.wait_ge(*upto("btok_mm", l, 1))
                        act.activation(b_tok[:].rearrange("p g n -> p (g n)"), M[0][:, 0:SG * SN], ACT.Copy)\
                            .then_inc(sem["btok_ready"], 1)
                    if slot == AD_STATE:
                        act.wait_ge(*upto("state_mm", l, 1))
                        act.activation(wk[:, 2], M[0][:], ACT.Copy)
                        act.activation(wk[:, 3], M[3][:], ACT.Copy).then_inc(sem["state_ready"], 1)
                    for i in range(8):
                        if slot == AD_SEG[i]:
                            act.wait_ge(*upto("seg_mm", l, i + 1))
                            if i:
                                act.wait_ge(*upto("yd_mm", l, i))
                            act.activation(seg_e, M[1][:], ACT.Exp).then_inc(sem["sege_ready"], 1)
                    for p in range(4):
                        if slot == AD_SOFT[p]:
                            act.wait_ge(*upto("nmax_ready", l, p + 1))
                            for hh in range(2):
                                o = hh * 3 * P
                                act.activation(probs[:, o:o + 2 * P], M[0][:, hh * 2 * P:(hh + 1) * 2 * P],
                                               ACT.Exp, bias=mx[:, 2 * hh + 1:2 * hh + 2], scale=DH ** -0.5,
                                               accum_out=rs[:, 2 * hh + 1:2 * hh + 2])
                                ins = act.activation(probs[:, o + 2 * P:o + 3 * P], M[3][:, hh * P:(hh + 1) * P],
                                                     ACT.Exp, bias=mx[:, 2 * hh:2 * hh + 1], scale=DH ** -0.5,
                                                     accum_out=rs[:, 2 * hh:2 * hh + 1])
                            ins.then_inc(sem["probs_ready"], 1)
                        if slot == AD_PT[p]:
                            act.wait_ge(*upto("pt_mm", l, p + 1))
                            act.activation(probsT[:, 0:3 * P], M[1][:, 0:3 * P], ACT.Copy).then_inc(sem["pt_a"], 1)
                    for i in range(2):
                        if slot == leaves(B_V + i):
                            act.wait_ge(*through(l, B_V + i))
                            for t in range(TT):
                                act.activation(v_tok[:, t, i * CB:(i + 1) * CB], acc[(B_V + i) % 2][t][:], ACT.Copy,
                                               scale=st[:, X_INV, t:t + 1]).then_inc(acc_free[(B_V + i) % 2], 1)
                    for g in range(SG):
                        if slot == leaves(B_Z + g):
                            act.wait_ge(*through(l, B_Z + g))
                            for t in range(TT):
                                act.activation(zs[:, t, g * CB:(g + 1) * CB], acc[(B_Z + g) % 2][t][:], ACT.Silu,
                                               scale=st[:, X_INV, t:t + 1]).then_inc(acc_free[(B_Z + g) % 2], 1)
                        if slot == leaves(B_Z + g) + 1:
                            act.wait_ge(*upto("gated", l, g + 1))
                            for t in range(TT):
                                square(ys[:, t, g * CB:(g + 1) * CB], ssq[:, 1 + g, t:t + 1])
                            if g == 1:
                                load_gain(post_mix_norm)
                    if slot == AD_ATTN_NORM:
                        act.wait_ge(*upto("attn_out", l, 4))
                        for t in range(TT):
                            act.wait_ge(*upto("squared", l, squares[0]))
                            act.activation(x_tok[:, t].rearrange("p (h d) -> p h d", d=DH), attn[:, :, t, :],
                                           ACT.Square, accum_out=ssq[:, 0, t:t + 1]).then_inc(sem["squared"], 1)
                            squares[0] += 1
                    for j in range(4):
                        if slot == AD_SSDT[j]:
                            to_hi("ssdT", j + 1, 4 + j, SSDT_BANK[j], G_ATTN)
                        if slot == AD_ATTNT[j]:
                            to_hi("attnT", j + 1, j, ATTNT_BANK[j], G_ATTN)
                    for i in range(4):
                        if slot == leaves(B_OUT + i):
                            act.wait_ge(*through(l, B_OUT + i))
                            for t in range(TT):
                                a = acc[(B_OUT + i) % 2][t]
                                square(a[:], ysq[:, t, i:i + 1])
                                act.activation(y[:, t, i * CB:(i + 1) * CB], a[:], ACT.Copy)\
                                    .then_inc(acc_free[(B_OUT + i) % 2], 1)
                norm_in(1, G_MLP)
                assert squares[0] == SQ_X1
                act.wait_ge(*upto("x_ready", l, 16))
                load_gain(post_mlp_norm)
                with act.Fori(0, QUARTERS) as q:
                    with act.Fori(0, QB // 2) as i:
                        for j in range(2):
                            b = l * NB + q * (2 * QB) + i * 2 + (B_MLP + j)
                            for c in range(AHEAD, NC):
                                round_hi(b, c)
                            for c in range(AHEAD):
                                round_hi(b + 1, c)
                            act.wait_ge(sem["mm_done"], RING + chunk(b + 1, 0))
                            for k in range(2):
                                n = q * (2 * QB) + i * 4 + (2 * j + k)
                                act.wait_ge(*upto("u_sq", l, n + 1))
                                act.activation(wk[:, k], acc[1 - j][k][:], ACT.Relu).then_inc(acc_free[1 - j], 1)
                                act.wait_ge(*left(l, B_MLP + j, k + 1, q * QB + i))
                                act.activation(u_hi[:, bass.ds(i * 8 + (4 * j + 2 * k), 2)].rearrange("p k s -> p (k s)"),
                                               wk[:, k], ACT.Square).then_inc(sem["u_hi_ready"], 1)
                    with act.Fori(0, QB // 2) as i:
                        for j in range(2):
                            b = l * NB + q * (2 * QB) + i * 2 + (B_MLP + QB + j)
                            for c in range(AHEAD, NC):
                                round_hi(b, c)
                            for c in range(AHEAD):
                                round_hi(b + 1, c)
                            for t in range(TT):
                                act.wait_ge(*left(l, B_MLP + QB + j, t + 1, q * QB + i))
                                n = q * (2 * QB) + i * 4 + (SQ_X1 + 2 * j + t)
                                act.wait_ge(*upto("squared", l, n))
                                act.activation(junk, y[:, t, bass.ds(i * (2 * CB) + j * CB, CB)], ACT.Square,
                                               accum_out=ysq[:, t, bass.ds(i * 2 + j, 1)]).then_inc(sem["squared"], 1)

        @block.tensor
        def _(pe):
            pe.wait_ge(once["const_ready"], 4)
            pe.wait_ge(once["typed_ready"], 5)
            pe.wait_ge(once["prm_landed"], 16 * 6 * DEPTH)
            for l in range(DEPTH):
                pe.transpose(M[l][:, 0:NPRM], probs[0:NPRM, l * P:(l + 1) * P], ident[0:NPRM, 0:NPRM])\
                    .then_inc(once["prm_mm"], 1)
            pe.wait_ge(once["table_sin"], 1)
            for i in range(4):
                ins = pe.transpose(M[2][:, i * P:(i + 1) * P], wk[:, 3, i * P:(i + 1) * P], ident[:])
            ins.then_inc(once["table_mm"], 1)
            pe.wait_ge(once["prm_copied"], DEPTH)
            pe.wait_ge(once["table_ready"], 2)

            def take(b, c):
                pe.wait_ge(sem["split_done"], RING + 1 + chunk(b, c))

            def token_chunk(c, par, s_hi, s_lo):
                for kk in range(CK):
                    k = c * CK + kk
                    wh, wl = (w[:, c % RING, kk * CB:(kk + 1) * CB] for w in (w_hi, w_lo))
                    for t in range(TT):
                        o = acc[par][t][:]
                        sh, sl = (s[:, k, t * P:(t + 1) * P] for s in (s_hi, s_lo))
                        pe.matmul(o, sh, wh, start=(k == 0), stop=False)
                        pe.matmul(o, sh, wl, start=False, stop=False)
                        ins = pe.matmul(o, sl, wh, start=False, stop=(k == KT - 1))
                ins.then_inc(sem["mm_done"], 1)

            def feature_chunk(c, par):
                for kk in range(CK):
                    k = c * CK + kk
                    for m in range(CB // P):
                        o = acc[par][m // 2][:, m % 2 * SEQ:(m % 2 + 1) * SEQ]
                        wh, wl = (w[:, c % RING, kk * CB + m * P:kk * CB + (m + 1) * P] for w in (w_hi, w_lo))
                        pe.matmul(o, wh, a_hi[:, k], start=(k == 0 and m % 2 == 0), stop=False,
                                  skip_group_check=True)
                        pe.matmul(o, wh, a_lo[:, k], start=False, stop=False, skip_group_check=True)
                        ins = pe.matmul(o, wl, a_hi[:, k], start=False, stop=(k == KT - 1),
                                        skip_group_check=True)
                ins.then_inc(sem["mm_done"], 1)

            with pe.Fori(0, DEPTH) as l:
                def norm_in(n):
                    for j in range(8):
                        if j % 2 == 0:
                            pe.wait_ge(*upto("x_ready", l, 8 * n + j + 2))
                        if j >= 4:
                            pe.wait_ge(*upto("xT_ready", l, 8 * n + j - 3))
                        for kk in range(2):
                            for t in range(TT):
                                k = 2 * j + kk
                                ins = pe.transpose(M[j % 4][:, kk * SEQ + t * P:kk * SEQ + (t + 1) * P],
                                                   x_sb[:, t, k * P:(k + 1) * P], ident[:])
                        ins.then_inc(sem["xT_mm"], 1)

                def inv_row_and_dt():
                    pe.wait_ge(*upto("diag_ready", l, 1))
                    for t in range(TT):
                        ins = pe.matmul(M[0][:, t * P:(t + 1) * P], ones[:], diag[:, t], start=True, stop=True)
                    ins.then_inc(sem["diag_mm"], 1)
                    pe.wait_ge(*upto("wdt_ready", l, 1))
                    o = M[1][:, 0:SEQ]
                    for k in range(KT):
                        wh, wl = (w[:, k * SH:k * SH + P] for w in (wdt_hi, wdt_lo))
                        pe.matmul(o, wh, a_hi[:, k], start=(k == 0), stop=False)
                        pe.matmul(o, wh, a_lo[:, k], start=False, stop=False)
                        ins = pe.matmul(o, wl, a_hi[:, k], start=False, stop=(k == KT - 1))
                    ins.then_inc(sem["dt_mm"], 1)

                def dt_turn():
                    pe.wait_ge(*upto("dtT_ready", l, 1))
                    for t in range(TT):
                        ins = pe.transpose(M[1][:, t * P:(t + 1) * P], dtT[:, t * P:(t + 1) * P], ident[:])
                    ins.then_inc(sem["dt_turned"], 1)

                def decays():
                    pe.wait_ge(*upto("adt_ready", l, 1))
                    pe.wait_ge(*upto("inv_row_ready", l, 1))
                    pe.matmul(M[0][:, 0:SH], low[:].bitcast(F32), dts[:, A_DT, 0], start=True, stop=True)
                    pe.matmul(M[0][:, SH:2 * SH], tri[:], dts[:, A_DT, 1], start=True, stop=True)\
                        .then_inc(sem["decay_mm"], 1)

                def x_tokens(i):
                    t, g = divmod(i, SG)
                    pe.wait_ge(*upto("silu_ready", l, g + 1))
                    pe.wait_ge(*upto("decay_ready", l, 1))
                    for k in range(4):
                        ins = pe.transpose(M[i][:, k * P:(k + 1) * P], xbcT[:, 4 * g + k, t * P:(t + 1) * P],
                                           ident[:])
                    ins.then_inc(sem["xtok_mm"], 1)

                def b_tokens_and_cb():
                    pe.wait_ge(*upto("silu_ready", l, 3))
                    pe.wait_ge(*upto("xtok_ready", l, 4))
                    nx = SW // P
                    for g in range(SG):
                        ins = pe.transpose(M[0][:, g * P:(g + 1) * P], xbcT[:, nx + g, 0:P], ident[:])
                    ins.then_inc(sem["btok_mm"], 1)
                    for t in range(TT):
                        for g in range(SG):
                            i = t * SG + g
                            ins = pe.matmul(M[1][:, i * P:(i + 1) * P], xbcT[:, nx + g, t * P:(t + 1) * P],
                                            xbcT[:, nx + SG + g, t * P:(t + 1) * P], start=True, stop=True)
                    ins.then_inc(sem["cb_mm"], 1)

                def states():
                    pe.wait_ge(*upto("btok_ready", l, 1))
                    pe.wait_ge(*upto("xdd_ready", l, 2))
                    for g in range(SG):
                        ins = pe.matmul(M[3 * g][:], b_tok[:, g], wk[:, 2 + g], start=True, stop=True)
                    ins.then_inc(sem["state_mm"], 1)

                def segment_sums(i):
                    pe.wait_ge(*upto("sega_ready", l, i + 1))
                    if i:
                        pe.wait_ge(*upto("sege_ready", l, i))
                    else:
                        pe.wait_ge(*upto("cbm_ready", l, 1))
                    pe.matmul(M[1][:], low[:], seg_hi[i % 2], start=True, stop=False)
                    pe.matmul(M[1][:], low[:], seg_lo[i % 2], start=False, stop=True).then_inc(sem["seg_mm"], 1)

                def y_diagonal(i):
                    t, g, hh = i // 4, i // 2 % 2, i % 2
                    pe.wait_ge(*upto("segm_ready", l, i + 1))
                    if i == 0:
                        pe.wait_ge(*upto("state_ready", l, 1))
                        pe.wait_ge(*upto("xdt_ready", l, 4))
                    if i in (4, 6):
                        pe.wait_ge(*upto("y_added", l, i // 2 - 1))
                    for h in range(4):
                        o = (hh * 4 + h) * SP_
                        ins = pe.matmul(M[3 * g][:, o:o + SP_], seg_e[:, h * P:(h + 1) * P],
                                        x_tok[:, t, g * CB + o:g * CB + o + SP_], start=True, stop=True)
                    ins.then_inc(sem["yd_mm"], 1)

                def y_offset(g):
                    if g == 1:
                        pe.wait_ge(*upto("sege_ready", l, 8))
                    pe.matmul(M[2 - g][:], xbcT[:, SW // P + SG + g, P:2 * P], wk[:, 2 + g], start=True,
                              stop=True).then_inc(sem["yoff_mm"], 1)

                def scores(p):
                    pe.wait_ge(*upto("rope_ready", l, 4 + p + 1))
                    if p == 0:
                        pe.wait_ge(*upto("y_added", l, 4))
                    else:
                        pe.wait_ge(*upto("pt_v", l, p))
                    for hh in range(2):
                        h = 2 * p + hh
                        o = M[0][:, hh * SEQ:(hh + 1) * SEQ]
                        pe.matmul(o, qk[:, h, P:SEQ], qk[:, HEADS + h], start=(hh == 0), stop=False,
                                  skip_group_check=True)
                        pe.matmul(o[:, P:SEQ], ident_b[:], cmask[:], start=False, stop=True,
                                  skip_group_check=True)
                    for hh in range(2):
                        h = 2 * p + hh
                        o = M[3][:, hh * P:(hh + 1) * P]
                        pe.matmul(o, qk[:, h, 0:P], qk[:, HEADS + h, 0:P], start=(hh == 0), stop=False,
                                  skip_group_check=True)
                        ins = pe.matmul(o, ident_b[:], cmask[:], start=False, stop=True, skip_group_check=True)
                    ins.then_inc(sem["score_mm"], 1)

                def probs_turn(p):
                    pe.wait_ge(*upto("probs_ready", l, p + 1))
                    if p == 0:
                        pe.wait_ge(*upto("yoff_mul", l, 2))
                    else:
                        pe.wait_ge(*upto("attn_out", l, p))
                    for hh in range(2):
                        for i in range(3):
                            ins = pe.transpose(M[1 + 2 * hh][:, i * P:(i + 1) * P],
                                               probs[:, (3 * hh + i) * P:(3 * hh + i + 1) * P], ident[:])
                    ins.then_inc(sem["pt_mm"], 1)

                def values(p):
                    pe.wait_ge(*upto("pt_a", l, p + 1))
                    pe.wait_ge(*upto("pt_v", l, p + 1))
                    pe.wait_ge(*left(l, B_V + p // 2, 2))
                    for hh in range(2):
                        h = 2 * p + hh
                        v0, v1 = (v_tok[:, t, h * DH:(h + 1) * DH] for t in range(TT))
                        a10, a11, a00 = (probsT[:, (3 * hh + i) * P:(3 * hh + i + 1) * P] for i in range(3))
                        o = M[1][:, 2 * hh * P:(2 * hh + 1) * P]
                        pe.matmul(o, a00, v0, start=True, stop=True)
                        o = M[1][:, (2 * hh + 1) * P:(2 * hh + 2) * P]
                        pe.matmul(o, a10, v0, start=True, stop=False)
                        ins = pe.matmul(o, a11, v1, start=False, stop=True)
                    ins.then_inc(sem["pv_mm"], 1)

                def attn_turn(j):
                    if j == 0:
                        pe.wait_ge(*upto("attn_ready", l, 1))
                    if j == 3:
                        pe.wait_ge(*upto("attnT_ready", l, 1))
                    for kk in range(2):
                        for t in range(TT):
                            ins = pe.transpose(M[ATTNT_BANK[j]][:, kk * SEQ + t * P:kk * SEQ + (t + 1) * P],
                                               attn[:, 2 * j + kk, t, :], ident[:])
                    ins.then_inc(sem["attnT_mm"], 1)

                def ssd_turn(j):
                    pe.wait_ge(*upto("ssd_ready", l, j // 2 + 1))
                    if j in (1, 2):
                        pe.wait_ge(*upto("ssdT_ready", l, j))
                    if j == 3:
                        pe.wait_ge(*upto("attnT_ready", l, 3))
                    for kk in range(2):
                        for t in range(TT):
                            k = 2 * j + kk
                            ins = pe.transpose(M[SSDT_BANK[j]][:, kk * SEQ + t * P:kk * SEQ + (t + 1) * P],
                                               ys[:, t, k * P:(k + 1) * P], ident[:])
                    ins.then_inc(sem["ssdT_mm"], 1)

                norm_in(0)
                for slot in range(MIX_SLOTS):
                    b, c = divmod(slot, NC)
                    if c == 0:
                        pe.wait_ge(*left(l, b, 0))
                    take(l * NB + b, c)
                    if b == 0:
                        pe.wait_ge(*upto("xT_ready", l, c + 1))
                    if b == B_OUT:
                        pe.wait_ge(*(upto("attnT_ready", l, c + 1) if c < 4 else upto("ssdT_ready", l, c - 3)))
                    if b < B_V:
                        feature_chunk(c, b % 2)
                    elif b < B_OUT:
                        token_chunk(c, b % 2, a_hi, a_lo)
                    else:
                        token_chunk(c, b % 2, u_hi, u_lo)
                    if slot == PE_DT:
                        inv_row_and_dt()
                    if slot == PE_DT_TURN:
                        dt_turn()
                    if slot == PE_DECAY:
                        decays()
                    if PE_XTOK <= slot < PE_XTOK + TT * SG:
                        x_tokens(slot - PE_XTOK)
                    if slot == PE_CB:
                        b_tokens_and_cb()
                    if slot == PE_STATE:
                        states()
                    if slot in PE_YD:
                        y_diagonal(PE_YD.index(slot))
                    if slot in PE_YOFF:
                        y_offset(PE_YOFF.index(slot))
                    if slot in PE_SEG:
                        segment_sums(PE_SEG.index(slot))
                    if slot in PE_SCORE:
                        scores(PE_SCORE.index(slot))
                    if slot in PE_PT:
                        probs_turn(PE_PT.index(slot))
                    if slot in PE_PV:
                        values(PE_PV.index(slot))
                    if slot in PE_SSDT:
                        ssd_turn(PE_SSDT.index(slot))
                    if slot in PE_ATTNT:
                        attn_turn(PE_ATTNT.index(slot))
                norm_in(1)
                with pe.Fori(0, QUARTERS) as q:
                    with pe.Fori(0, QB // 2) as i:
                        for j in range(2):
                            pe.wait_ge(*left(l, B_MLP + j, 0, q * QB + i))
                            for c in range(NC):
                                take(l * NB + q * (2 * QB) + i * 2 + (B_MLP + j), c)
                                pe.wait_ge(*upto("xT_ready", l, 8 + c + 1))
                                feature_chunk(c, 1 - j)
                    with pe.Fori(0, QB // 2) as i:
                        for j in range(2):
                            pe.wait_ge(*left(l, B_MLP + QB + j, 0, q * QB + i))
                            for c in range(NC):
                                take(l * NB + q * (2 * QB) + i * 2 + (B_MLP + QB + j), c)
                                pe.wait_ge(*upto("u_ready", l, q * (2 * QB) + (c + 1)))
                                token_chunk(c, 1 - j, u_hi, u_lo)

        @block.vector
        def _(dve):
            dve.memset(mx[:], 0.0).then_inc(sem["split_done"], RING)
            dve.memset(rs[:], 0.0).then_inc(sem["u_sq"], 2)
            tstep = [0]

            def tlink(ins):
                tstep[0] += 1
                ins.then_inc(once["table_step"], 1)
                dve.wait_ge(once["table_step"], tstep[0])

            def split_lo(b, c):
                dve.wait_ge(sem["hi_ready"], chunk(b, c) + 1)
                dve.tensor_tensor(w_lo[:, c % RING], raw[:, c % RING], w_hi[:, c % RING].bitcast(F32),
                                  ALU.subtract).then_inc(sem["split_done"], 1)

            dve.wait_ge(once["const_ready"], 4)
            dve.tensor_copy(ident_b[:], ident[:]).then_inc(once["typed_ready"], 1)
            dve.wait_ge(once["const_step"], 7)
            dve.tensor_copy(low[:], low_w[:]).then_inc(once["typed_ready"], 1)
            dve.tensor_copy(cmask[:], cmask_w[:]).then_inc(once["typed_ready"], 1)
            dve.tensor_copy(wdt_hi[:, KT * SH:], wdt_w[:]).then_inc(once["typed_ready"], 1)
            dve.tensor_copy(wdt_lo[:, KT * SH:], wdt_w[:]).then_inc(once["typed_ready"], 1)

            inv_freq = (np.float32(THETA) ** (-np.arange(HALF, dtype=np.float32) / np.float32(HALF)))
            for i in range(HALF):
                ins = dve.memset(cbm[:, 0, i:i + 1], float(inv_freq[i]))
            tlink(ins)
            dve.wait_ge(once["pos_landed"], 16)
            tlink(dve.tensor_copy(cbm[:, 1, 0:TT], pos[:]))
            angle, turn, left_over = cbm[:, 2, 0:TT * HALF], cbm[:, 2, 32:32 + TT * HALF], cbm[:, 2, 64:64 + TT * HALF]
            for t in range(TT):
                tlink(dve.tensor_scalar(angle[:, t * HALF:(t + 1) * HALF], cbm[:, 0, 0:HALF],
                                        cbm[:, 1, t:t + 1], None, ALU.mult))
            tlink(dve.memset(wk[:, 2:4], 0.0))
            c1 = float(np.float32(6.28125))
            c2 = float(np.float32(np.round((2 * np.pi - c1) * 2 ** 18) / 2 ** 18))
            c3 = float(np.float32(2 * np.pi - c1 - c2))
            for which, quarter in ((0, 0.25), (1, 0.0)):
                tlink(dve.tensor_scalar(turn, angle, float(1 / (2 * np.pi)), quarter, ALU.mult, ALU.add))
                tlink(dve.tensor_scalar(turn, turn, 1.5 * 2 ** 23, None, ALU.add))
                tlink(dve.tensor_scalar(turn, turn, 1.5 * 2 ** 23, None, ALU.subtract))
                tlink(dve.scalar_tensor_tensor(left_over, turn, -c1, angle, ALU.mult, ALU.add))
                tlink(dve.scalar_tensor_tensor(left_over, turn, -c2, left_over, ALU.mult, ALU.add))
                tlink(dve.scalar_tensor_tensor(left_over, turn, -c3, left_over, ALU.mult, ALU.add))
                tlink(dve.tensor_scalar(left_over, left_over, float(2 * np.pi * quarter), 3.1415925,
                                        ALU.add, ALU.min))
                tlink(dve.tensor_scalar(left_over, left_over, -3.1415925, None, ALU.max))
                for t in range(TT):
                    for half in range(2):
                        o = (which * TT + t) * P + half * HALF
                        sign = -1.0 if which == 1 and half == 0 else 1.0
                        tlink(dve.tensor_scalar(wk[:, 2, o:o + HALF], left_over[:, t * HALF:(t + 1) * HALF],
                                                sign, None, ALU.mult))
            dve.memset(dts[:, 0], 0.0).then_inc(once["table_angle"], 1)
            dve.wait_ge(once["row_exp"], 1)
            dve.tensor_scalar(row_all[:, :, 1], row_all[:, :, 1], -1.0, None, ALU.mult)\
                .then_inc(once["row_ready"], 1)
            for c in range(AHEAD):
                split_lo(0, c)
            dve.wait_ge(once["x_landed"], 16 * TT)
            dve.memset(rinv[:], 0.0).then_inc(sem["x_ready"], 8)

            with dve.Fori(0, DEPTH) as l:
                links = [0]

                def link(ins):
                    links[0] += 1
                    ins.then_inc(sem["dve_chain"], 1)
                    dve.wait_ge(*upto("dve_chain", l, links[0]))

                def norm_in(n, gain):
                    for j in range(8):
                        dve.wait_ge(*upto("xT_hi", l, 8 * n + j + 1))
                        for kk in range(2):
                            k = 2 * j + kk
                            ins = dve.scalar_tensor_tensor(a_lo[:, k], M[j % 4][:, kk * SEQ:(kk + 1) * SEQ],
                                                           prm[:, gain + k:gain + k + 1], a_hi[:, k].bitcast(F32),
                                                           ALU.mult, ALU.subtract)
                        ins.then_inc(sem["xT_ready"], 1)

                def x_mean(squares):
                    dve.wait_ge(*upto("squared", l, squares))
                    link(dve.tensor_reduce(st[:, X_SUM], sq[:], AX.X, ALU.add))
                    dve.tensor_scalar(st[:, X_MS], st[:, X_SUM], 1.0 / D, EPS, ALU.mult, ALU.add)\
                        .then_inc(sem["x_ms"], 1)

                def to_lo(name, n, j, bank, gain):
                    dve.wait_ge(*upto(name + "_hi", l, n))
                    for kk in range(2):
                        k = 2 * j + kk
                        ins = dve.scalar_tensor_tensor(u_lo[:, k], M[bank][:, kk * SEQ:(kk + 1) * SEQ],
                                                       prm[:, gain + k:gain + k + 1], u_hi[:, k].bitcast(F32),
                                                       ALU.mult, ALU.subtract)
                    ins.then_inc(sem[name + "_ready"], 1)

                def update_x(n):
                    dve.wait_ge(*upto("y_inv", l, n + 1))
                    dve.wait_ge(*upto("gain_landed", l, 16 * (n + 1)))
                    for c in range(4):
                        cols = slice(c * CB, (c + 1) * CB)
                        for t in range(TT):
                            dve.scalar_tensor_tensor(y[:, t, cols], y[:, t, cols], st[:, Y_INV, t:t + 1],
                                                     zg[:, cols], ALU.mult, ALU.mult).then_inc(sem["y_scaled"], 1)
                        for t in range(TT):
                            dve.wait_ge(*upto("y_scaled", l, 8 * n + 2 * c + t + 1))
                            dve.tensor_tensor(x_sb[:, t, cols], x_sb[:, t, cols], y[:, t, cols], ALU.add)\
                                .then_inc(sem["x_ready"], 1)

                def dt_steps():
                    dve.wait_ge(*upto("dt_turned", l, 1))
                    dve.wait_ge(*upto("x_inv", l, 1))
                    for t in range(TT):
                        link(dve.scalar_tensor_tensor(dts[:, DT_IN, t], M[1][:, t * P:t * P + SH],
                                                      st[:, X_INV, t:t + 1], row[:, 0], ALU.mult, ALU.add))
                    dve.scalar_tensor_tensor(dts[:, DT_ABS], dts[:, DT_IN], -1.0, dts[:, DT_IN], ALU.mult, ALU.max)\
                        .then_inc(sem["dt_abs"], 1)
                    dve.wait_ge(*upto("dt_exp", l, 1))
                    link(dve.tensor_scalar(dts[:, DT_TMP], dts[:, DT_EXP], 2.0, None, ALU.add))
                    link(dve.reciprocal(dts[:, DT_TMP], dts[:, DT_TMP]))
                    link(dve.tensor_tensor(dts[:, DT_S], dts[:, DT_EXP], dts[:, DT_TMP], ALU.mult))
                    link(dve.tensor_tensor(dts[:, DT_S2], dts[:, DT_S], dts[:, DT_S], ALU.mult))
                    link(dve.tensor_scalar(dts[:, DT], dts[:, DT_S2], 1.0 / 17, None, ALU.mult))
                    for k in (15, 13, 11, 9, 7, 5, 3):
                        link(dve.scalar_tensor_tensor(dts[:, DT], dts[:, DT], 1.0 / k, dts[:, DT_S2],
                                                      ALU.add, ALU.mult))
                    link(dve.scalar_tensor_tensor(dts[:, DT], dts[:, DT], 1.0, dts[:, DT_S], ALU.add, ALU.mult))
                    link(dve.tensor_scalar(dts[:, DT_TMP], dts[:, DT_IN], 0.0, None, ALU.max))
                    link(dve.scalar_tensor_tensor(dts[:, DT], dts[:, DT], 2.0, dts[:, DT_TMP], ALU.mult, ALU.add))
                    link(dve.tensor_tensor(dts[:, A_DT], dts[:, DT],
                                           row[:, 1].unsqueeze(1).broadcast_to([P, TT, SH]), ALU.mult))
                    dve.tensor_copy(adt_hi[:], dts[:, A_DT]).then_inc(sem["adt_hi_ready"], 1)
                    dve.wait_ge(*upto("adt_hi_ready", l, 1))
                    dve.tensor_tensor(adt_lo[:], dts[:, A_DT], adt_hi[:].bitcast(F32), ALU.subtract)\
                        .then_inc(sem["adt_ready"], 1)

                def conv(b, k):
                    n0 = 16 * b + 8 * k
                    dve.wait_ge(*left(l, b, k + 1))
                    for tap in range(TAPS - 1, -1, -1):
                        for m in range(2):
                            ct = 4 * b + 2 * k + m
                            n = n0 + 2 * (TAPS - 1 - tap) + m
                            src = convr[:, k, m, tap:tap + SEQ]
                            wt = prm[:, G_TAP + tap * NCT + ct:G_TAP + tap * NCT + ct + 1]
                            if tap == TAPS - 1:
                                ins = dve.tensor_scalar(xbcT[:, ct], src, wt, prm[:, G_BIAS + ct:G_BIAS + ct + 1],
                                                        ALU.mult, ALU.add)
                            else:
                                dve.wait_ge(*upto("conv_step", l, n - 1))
                                ins = dve.scalar_tensor_tensor(xbcT[:, ct], src, wt, xbcT[:, ct],
                                                               ALU.mult, ALU.add)
                            ins.then_inc(sem["conv_step"], 1)

                def two(a):
                    return a.rearrange("p (m s) -> p m s", m=2)

                inv_two = inv_row[:].unsqueeze(1).broadcast_to([P, 2, SEQ])

                dve.wait_ge(*upto("prm_ready", l, 1))
                norm_in(0, G_MIX)
                for slot in range(AHEAD, MIX_SLOTS + AHEAD):
                    b, c = divmod(slot, NC)
                    if slot in AD_ROPE:
                        r = AD_ROPE.index(slot)
                        dve.wait_ge(*left(l, B_Q + r // 2, r % 2 + 1))
                        if r:
                            dve.wait_ge(*upto("rope_ready", l, r))
                    split_lo(l * NB + b, c)
                    if slot == AHEAD:
                        x_mean(SQ_X0)
                    if slot == AD_DIAG:
                        dve.wait_ge(*upto("x_inv", l, 1))
                        for t in range(TT):
                            ins = dve.tensor_scalar(diag[:, t], ident[:], st[:, X_INV, t:t + 1], None, ALU.mult)
                        ins.then_inc(sem["diag_ready"], 1)
                        dve.wait_ge(*upto("wdt_hi_ready", l, 1))
                        dve.tensor_tensor(wdt_lo[:, 0:KT * SH], wdt, wdt_hi[:, 0:KT * SH].bitcast(F32), ALU.subtract)\
                            .then_inc(sem["wdt_ready"], 1)
                    for i in range(B_V):
                        if slot == leaves(i):
                            dve.wait_ge(*through(l, i))
                            dve.wait_ge(*upto("inv_row_ready", l, 1))
                            for k in range(2):
                                r = (i - B_Q) * 2 + k
                                dst = convr[:, k, :, TAPS - 1:] if i < B_Q else qk[:, 2 * r:2 * r + 2]
                                dve.tensor_tensor(dst, two(acc[i % 2][k][:]), inv_two, ALU.mult)\
                                    .then_inc(acc_free[i % 2], 1)
                        if i < B_Q and slot in (leaves(i) + 1, leaves(i) + 2):
                            conv(i, slot - leaves(i) - 1)
                    if slot == AD_DTT:
                        dve.wait_ge(*upto("dt_mm", l, 1))
                        dve.tensor_copy(dtT, M[1][:, 0:SEQ]).then_inc(sem["dtT_ready"], 1)
                    if slot == AD_DT:
                        dt_steps()
                    if slot == AD_XDT:
                        for i in range(TT * SG):
                            t, g = divmod(i, SG)
                            dve.wait_ge(*upto("skip_done", l, i + 1))
                            dve.tensor_tensor(heads8(x_tok, t, g), heads8(x_tok, t, g), per_head(dts[:, DT, t], g),
                                              ALU.mult).then_inc(sem["xdt_ready"], 1)
                    if slot == AD_XDT + 1:
                        dve.wait_ge(*upto("xdt_ready", l, 4))
                        dve.wait_ge(*upto("decay_ready", l, 1))
                        for g in range(SG):
                            dve.tensor_tensor(wk[:, 2 + g].rearrange("p (h n) -> p h n", n=SP_),
                                              heads8(x_tok, 0, g), per_head(decay[:, 0], g), ALU.mult)\
                                .then_inc(sem["xdd_ready"], 1)
                    if slot == AD_CB:
                        dve.wait_ge(*upto("cb_mm", l, 1))
                        dve.tensor_tensor(cbm[:], four(M[1][:]), tri[:].unsqueeze(1).broadcast_to([P, 4, P]),
                                          ALU.mult).then_inc(sem["cbm_ready"], 1)
                    for i in range(8):
                        if slot == AD_SEG[i]:
                            dve.wait_ge(*upto("sege_ready", l, i + 1))
                            dve.tensor_tensor(four(seg_e), four(seg_e),
                                              cbm[:, i // 2].unsqueeze(1).broadcast_to([P, 4, P]), ALU.mult)\
                                .then_inc(sem["segm_ready"], 1)
                    for j in range(4):
                        if slot == AD_Y[j]:
                            t, g = divmod(j, SG)
                            dve.wait_ge(*upto("yd_mm", l, 2 * j + 2))
                            ysg = ys[:, t, g * CB:(g + 1) * CB]
                            dve.tensor_tensor(ysg, ysg, M[3 * g][:], ALU.add).then_inc(sem["y_added"], 1)
                            if t:
                                dve.wait_ge(*upto("yoff_mm", l, g + 1))
                                dve.tensor_tensor(wk[:, 2 + g].rearrange("p (h n) -> p h n", n=SP_),
                                                  M[2 - g][:].rearrange("p (h n) -> p h n", n=SP_),
                                                  per_head(decay[:, 1], g), ALU.mult).then_inc(sem["yoff_mul"], 1)
                                dve.wait_ge(*upto("yoff_mul", l, g + 1))
                                dve.wait_ge(*upto("y_added", l, j + 1))
                                dve.tensor_tensor(ysg, ysg, wk[:, 2 + g], ALU.add).then_inc(sem["yoff_added"], 1)
                    for r in range(8):
                        if slot == AD_ROPE[r]:
                            dve.stream_shuffle(rope_t, qk[0:ROPE, 2 * r:2 * r + 2],
                                               [(i + HALF) % ROPE for i in range(ROPE)])\
                                .then_inc(sem["rope_swapped"], 1)
                            dve.wait_ge(*upto("rope_swapped", l, r + 1))
                            dve.tensor_tensor(rope_t, rope_t,
                                              sinT[:].unsqueeze(1).broadcast_to([ROPE, 2, SEQ]), ALU.mult)\
                                .then_inc(sem["rope_mul"], 1)
                        if slot == AD_ROPE[r] + 1:
                            dve.wait_ge(*upto("rope_mul", l, r + 1))
                            dve.wait_ge(*upto("rope_cos", l, r + 1))
                            rot = qk[0:ROPE, 2 * r:2 * r + 2]
                            dve.tensor_tensor(rot, rot, rope_t, ALU.add).then_inc(sem["rope_ready"], 1)
                    for p in range(4):
                        if slot == AD_SOFT[p]:
                            dve.wait_ge(*upto("score_mm", l, p + 1))
                            mxv = mx[:].rearrange("p (h t) -> p h t", t=TT)
                            link(dve.tensor_reduce(mxv[:, :, 1], two(M[0][:]), AX.X, ALU.max))
                            link(dve.tensor_reduce(mxv[:, :, 0], two(M[3][:, 0:2 * P]), AX.X, ALU.max))
                            dve.tensor_scalar(mx[:], mx[:], -(DH ** -0.5), None, ALU.mult)\
                                .then_inc(sem["nmax_ready"], 1)
                        if slot == AD_PT[p]:
                            dve.wait_ge(*upto("pt_mm", l, p + 1))
                            dve.tensor_copy(probsT[:, 3 * P:6 * P], M[3][:, 0:3 * P]).then_inc(sem["pt_v"], 1)
                            link(dve.reciprocal(rinv[:], rs[:]))
                        if slot == AD_O[p]:
                            dve.wait_ge(*upto("pv_mm", l, p + 1))
                            dve.tensor_tensor(four(ybuf[:, p * CB:(p + 1) * CB]), four(M[1][:]),
                                              rinv[:].unsqueeze(2).broadcast_to([P, 4, P]), ALU.mult)\
                                .then_inc(sem["attn_out"], 1)
                    if slot == AD_ATTN_NORM:
                        dve.wait_ge(*upto("squared", l, SQ_A))
                        dve.tensor_scalar(st[:, A_MS], ssq[:, 0], 1.0 / AW, EPS, ALU.mult, ALU.add)\
                            .then_inc(sem["attn_ms"], 1)
                    if slot == AD_ATTN_NORM + 1:
                        dve.wait_ge(*upto("attn_inv", l, 1))
                        for t in range(TT):
                            ins = dve.tensor_scalar(attn[:, :, t], attn[:, :, t], st[:, A_INV, t:t + 1], None,
                                                    ALU.mult)
                        ins.then_inc(sem["attn_ready"], 1)
                    for g in range(SG):
                        ms, inv = (S0_MS, S0_INV) if g == 0 else (S1_MS, S1_INV)
                        if slot == leaves(B_Z + g):
                            dve.wait_ge(*left(l, B_Z + g, 2))
                            dve.wait_ge(*upto("yoff_added", l, 2))
                            for t in range(TT):
                                ysg = ys[:, t, g * CB:(g + 1) * CB]
                                ins = dve.tensor_tensor(ysg, ysg, zs[:, t, g * CB:(g + 1) * CB], ALU.mult)
                            ins.then_inc(sem["gated"], 1)
                        if slot == leaves(B_Z + g) + 1:
                            dve.wait_ge(*upto("squared", l, SQ_S1 if g else SQ_S0))
                            dve.tensor_scalar(st[:, ms], ssq[:, 1 + g], 1.0 / CB, EPS, ALU.mult, ALU.add)\
                                .then_inc(sem["ssd_ms"], 1)
                        if slot == leaves(B_Z + g) + 2:
                            dve.wait_ge(*upto("ssd_inv", l, g + 1))
                            for t in range(TT):
                                ysg = ys[:, t, g * CB:(g + 1) * CB]
                                ins = dve.tensor_scalar(ysg, ysg, st[:, inv, t:t + 1], None, ALU.mult)
                            ins.then_inc(sem["ssd_ready"], 1)
                    for j in range(4):
                        if slot == AD_SSDT[j]:
                            to_lo("ssdT", j + 1, 4 + j, SSDT_BANK[j], G_ATTN)
                        if slot == AD_ATTNT[j]:
                            to_lo("attnT", j + 1, j, ATTNT_BANK[j], G_ATTN)
                dve.wait_ge(*upto("squared", l, SQ_Y0))
                dve.wait_ge(*left(l, B_MLP - 1, 2))
                link(dve.tensor_reduce(st[:, Y_SUM], ysq[:], AX.X, ALU.add))
                dve.tensor_scalar(st[:, Y_MS], st[:, Y_SUM], 1.0 / D, EPS, ALU.mult, ALU.add)\
                    .then_inc(sem["y_ms"], 1)
                update_x(0)
                norm_in(1, G_MLP)
                x_mean(SQ_X1)
                dve.wait_ge(*upto("x_ready", l, 16))
                dve.memset(ybuf[:], 0.0).then_inc(sem["y_zero"], 1)
                with dve.Fori(0, QUARTERS) as q:
                    with dve.Fori(0, QB // 2) as i:
                        for j in range(2):
                            b = l * NB + q * (2 * QB) + i * 2 + (B_MLP + j)
                            for c in range(AHEAD, NC):
                                split_lo(b, c)
                            for c in range(AHEAD):
                                split_lo(b + 1, c)
                            for k in range(2):
                                n = q * (2 * QB) + i * 4 + (2 * j + k)
                                dve.wait_ge(*left(l, B_MLP + j, k + 1, q * QB + i))
                                dve.tensor_tensor(wk[:, 2 + k], wk[:, k], wk[:, k], ALU.mult)\
                                    .then_inc(sem["u_sq"], 1)
                                dve.wait_ge(*upto("u_sq", l, n + 3))
                                dve.wait_ge(*upto("u_hi_ready", l, n + 1))
                                u = bass.ds(i * 8 + (4 * j + 2 * k), 2)
                                dve.tensor_tensor(u_lo[:, u].rearrange("p k s -> p (k s)"), wk[:, 2 + k],
                                                  u_hi[:, u].rearrange("p k s -> p (k s)").bitcast(F32),
                                                  ALU.subtract).then_inc(sem["u_ready"], 1)
                    with dve.Fori(0, QB // 2) as i:
                        for j in range(2):
                            b = l * NB + q * (2 * QB) + i * 2 + (B_MLP + QB + j)
                            for c in range(AHEAD, NC):
                                split_lo(b, c)
                            for c in range(AHEAD):
                                split_lo(b + 1, c)
                            dve.wait_ge(sem["mm_done"], RING + chunk(b + 1, 0))
                            dve.wait_ge(*upto("y_zero", l, 1))
                            for t in range(TT):
                                yp = y[:, t, bass.ds(i * (2 * CB) + j * CB, CB)]
                                dve.tensor_tensor(yp, yp, acc[1 - j][t][:], ALU.add).then_inc(acc_free[1 - j], 1)
                dve.wait_ge(*upto("squared", l, SQ_Y1))
                dve.wait_ge(*upto("x_inv2", l, 1))
                link(dve.tensor_reduce(st[:, Y_SUM], ysq[:], AX.X, ALU.add))
                link(dve.tensor_tensor(st[:, Y_SUM], st[:, Y_SUM], st[:, X_INV2], ALU.mult))
                link(dve.tensor_tensor(st[:, Y_SUM], st[:, Y_SUM], st[:, X_INV2], ALU.mult))
                dve.tensor_scalar(st[:, Y_MS], st[:, Y_SUM], 1.0 / D, EPS, ALU.mult, ALU.add)\
                    .then_inc(sem["y_ms"], 1)
                update_x(1)
                assert links[0] == DVE_LINKS, links[0]


_INS = ["x", "positions", "pre_mix_norm", "post_mix_norm", "pre_mlp_norm", "post_mlp_norm", "w_in", "conv_w",
        "conv_b", "dt_bias", "a_log", "d_skip", "attn_out_norm", "ssd_out_norm", "w_out", "w_up", "w_down"]


def kernel(**inputs):
    import concourse.bacc as bacc
    from concourse.bass_utils import run_bass_kernel_spmd

    nc = bacc.Bacc("TRN2", target_bir_lowering=False, num_devices=1)
    arrays, args = {}, []
    for name in _INS:
        a = np.ascontiguousarray(inputs[name])
        arrays[f"in_{name}"] = a
        args.append(nc.dram_tensor(f"in_{name}", a.shape, mybir.dt.from_np(a.dtype), kind="ExternalInput").ap())
    args.append(nc.dram_tensor("out_0", (1, SEQ, D), F32, kind="ExternalOutput").ap())
    trunk(nc, *args)
    r = run_bass_kernel_spmd(nc, [arrays], core_ids=[0])
    return r.results[0]["out_0"]
```

```python
from contextlib import ExitStack

import numpy as np

import concourse.bass as bass
from concourse import mybir

ALU = mybir.AluOpType
ACT = mybir.ActivationFunctionType
AX = mybir.AxisListType
F32 = mybir.dt.float32
F32R = mybir.dt.float32r
I32 = mybir.dt.int32
BF16 = mybir.dt.bfloat16

P = 128
DEPTH, D, SEQ, DFF = 2, 2048, 256, 8192
TT = SEQ // P
KT = D // P
HEADS, DH, ROPE, THETA = 8, 128, 32, 500000.0
HALF = ROPE // 2
AW = HEADS * DH
SH, SP_, SG, SN, TAPS = 16, 64, 2, 128, 4
SW = SH * SP_
CONV = SW + 2 * SG * SN
EPS = 1e-6
NEG = -3e38

RING = 4
CK = 2
CB = 512
NC = KT // CK
W = CK * CB
AHEAD = 3

B_XBC, B_Q, B_K, B_V, B_Z, B_OUT, B_MLP = 0, 3, 5, 7, 9, 11, 15
QUARTERS = 4
QB = DFF // QUARTERS // CB
NB = B_MLP + QUARTERS * 2 * QB
MIX_SLOTS = B_MLP * NC

COL_Q, COL_K, COL_V, COL_Z, COL_XBC = 0, AW, 2 * AW, 3 * AW, 3 * AW + SW
COL_DT = COL_XBC + CONV

NCT = CONV // P
G_MIX, G_MLP, G_ATTN, G_SSD = 0, KT, 2 * KT, 2 * KT + AW // P
G_TAP = G_SSD + SW // P
G_BIAS = G_TAP + TAPS * NCT
NPRM = G_BIAS + NCT

PE_DT, PE_DT_TURN, PE_DECAY, PE_XTOK, PE_CB, PE_STATE = 7, 10, 17, 20, 28, 31
PE_SEG = [34 + 2 * i for i in range(8)]
PE_YD = [36 + 2 * i for i in range(8)]
PE_YOFF = [46, 50]
PE_SCORE = [59 + 5 * p for p in range(4)]
PE_PT = [s + 3 for s in PE_SCORE]
PE_PV = [s + 6 for s in PE_SCORE]
PE_ATTNT = [84, 85, 86, 87]
PE_SSDT = [83, 85, 90, 91]
AD_DIAG, AD_DTT, AD_DT, AD_DECAY, AD_XTOK, AD_XDT, AD_CB, AD_STATE = 8, 11, 14, 21, 24, 30, 32, 35
AD_SEG = [38 + 2 * i for i in range(8)]
AD_Y = [42 + 4 * j for j in range(4)]
AD_ROPE = [37, 39, 45, 47, 53, 55, 60, 62]
AD_SOFT = [s + 4 for s in PE_SCORE]
AD_PT = [s + 7 for s in PE_SCORE]
AD_O = [s + 10 for s in PE_SCORE]
AD_ATTN_NORM = 85
AD_ATTNT = [88, 89, 90, 91]
AD_SSDT = [87, 89, 94, 95]
ATTNT_BANK, SSDT_BANK = [0, 1, 3, 0], [2, 2, 2, 3]

X_SUM, X_MS, X_INV, X_EPS, Y_SUM, Y_MS, Y_INV, A_MS, A_INV, S0_MS, S0_INV, S1_MS, S1_INV = range(13)
NST = 13
DT_IN, DT_ABS, DT_EXP, DT_TMP, DT_S, DT_S2, DT, A_DT = range(8)

SQ_X0, SQ_S0, SQ_A, SQ_S1, SQ_Y0, SQ_X1 = 8, 10, 12, 14, 22, 30
SQ_Y1 = SQ_X1 + TT * QB
DVE_LINKS = 36


NORM_PE = {0: (2, 3), 1: (4,), 2: (5,), 3: (6,), 4: (7,)}
NORM_AD = {AHEAD: (), AHEAD + 1: (2, 3), AHEAD + 2: (4, 5), AHEAD + 3: (6, 7)}


def is_first(q, i):
    return type(q) is int and type(i) is int and q == 0 and i == 0


def leaves(b):
    return NC * (b + 1) + AHEAD - 1


def trunk(nc, x, positions, pre_mix_norm, post_mix_norm, pre_mlp_norm, post_mlp_norm, w_in, conv_w,
          conv_b, dt_bias, a_log, d_skip, attn_out_norm, ssd_out_norm, w_out, w_up, w_down, out):
    ctx = ExitStack()
    with ctx:
        def sb(name, shape, dt=F32):
            return ctx.enter_context(nc.sbuf_tensor(name, shape, dt))

        raw = sb("raw", [P, RING, W])
        w_hi = sb("w_hi", [P, RING, W], F32R)
        w_lo = sb("w_lo", [P, RING, W], F32R)
        x_sb = sb("x_sb", [P, TT, D])
        a_hi = sb("a_hi", [P, KT, SEQ], F32R)
        a_lo = sb("a_lo", [P, KT, SEQ], F32R)
        u_hi = sb("u_hi", [P, KT, SEQ], F32R)
        u_lo = sb("u_lo", [P, KT, SEQ], F32R)
        ybuf = sb("ybuf", [P, TT * D])
        xbcT = sb("xbcT", [P, NCT, SEQ])
        x_tok = sb("x_tok", [P, TT, SW])
        v_tok = sb("v_tok", [P, TT, AW])
        zg = sb("zg", [P, D])
        b_tok = sb("b_tok", [P, SG, SN])
        convr = sb("convr", [P, 2, 2, TAPS - 1 + SEQ])
        wk = sb("wk", [P, 4, CB])
        cbm = sb("cbm", [P, TT * SG, P])
        wdt_hi = sb("wdt_hi", [P, KT * SH + P - SH], F32R)
        wdt_lo = sb("wdt_lo", [P, KT * SH + P - SH], F32R)
        ident = sb("ident", [P, P])
        tri = sb("tri", [P, P])
        low = sb("low", [P, P], F32R)
        cmask = sb("cmask", [P, P], BF16)
        ident_b = sb("ident_b", [P, P], BF16)
        ones = sb("ones", [P, P])
        cosT = sb("cosT", [ROPE, SEQ])
        sinT = sb("sinT", [ROPE, SEQ])
        inv_row = sb("inv_row", [P, SEQ])
        prm = sb("prm", [P, NPRM])
        prm_next = sb("prm_next", [P, DEPTH, NPRM])
        row = sb("row", [P, 3, SH])
        row_all = sb("row_all", [P, DEPTH + 1, 3, SH])
        minus_half = sb("minus_half", [P, 2])
        freq = sb("freq", [ROPE, 2])
        sq = sb("sq", [P, TT, 4])
        ysq = sb("ysq", [P, TT, 4])
        st = sb("st", [P, NST, TT])
        dts = sb("dts", [P, 8, TT, SH])
        adt_hi = sb("adt_hi", [P, TT, SH], F32R)
        adt_lo = sb("adt_lo", [P, TT, SH], F32R)
        decay = sb("decay", [P, 2, SH])
        mx = sb("mx", [P, 4])
        rs = sb("rs", [P, 4])
        rinv = sb("rinv", [P, 4])
        ssq = sb("ssq", [P, 3, TT])

        acc = [[ctx.enter_context(nc.psum_tensor(f"acc{i}{j}", [P, CB], F32)) for j in range(2)]
               for i in range(2)]
        M = [ctx.enter_context(nc.psum_tensor(f"M{i}", [P, CB], F32)) for i in range(4)]

        qk = ybuf[:, :].rearrange("p (h s) -> p h s", s=SEQ)
        attn = ybuf[:, 0:TT * AW].rearrange("p (h t d) -> p h t d", t=TT, d=DH)
        y = ybuf[:, :].rearrange("p (t n) -> p t n", t=TT)
        ys = xbcT[:, 0:SW // P, :].rearrange("p a s -> p (a s)").rearrange("p (t n) -> p t n", t=TT)
        zs = zg[:, :].rearrange("p (t n) -> p t n", t=TT)
        rope_t = convr[0:ROPE, 0, :, TAPS - 1:]
        wdt = wk[:, 3, 0:KT * SH]
        dtT = wk[:, 0, 0:SEQ]
        tab = x_tok[0:ROPE, :, :].rearrange("p t n -> p (t n)")
        tab_f, tab_m = tab[:, 0:HALF], tab[:, HALF:ROPE]
        tab_pos, tab_angle, tab_turn, tab_sin = (tab[:, i * SEQ:(i + 1) * SEQ] for i in range(1, 5))
        seg_hi = [u_hi[:, 2 * i:2 * i + 2].rearrange("p k s -> p (k s)") for i in range(2)]
        seg_lo = [u_lo[:, 2 * i:2 * i + 2].rearrange("p k s -> p (k s)") for i in range(2)]
        seg_e = wk[:, 1]
        low_w, cmask_w, wdt_w = v_tok[:, 0, 0:P], v_tok[:, 0, P:2 * P], v_tok[:, 0, 2 * P:3 * P - SH]
        probs = wk[:, 0:2].rearrange("p a n -> p (a n)")
        probsT = wk[:, 2:4].rearrange("p a n -> p (a n)")
        diag = wk[:, 1, 0:SEQ].rearrange("p (t n) -> p t n", t=TT)
        junk = cbm[:, :, :].rearrange("p a n -> p (a n)")

        up_banks = 2 * QB * QUARTERS
        per = dict(
            hi_ready=NB * NC,
            split_done=NB * NC,
            mm_done=NB * NC,
            x_ready=16,
            xT_mm=16, xT_hi=16, xT_ready=16,
            x_ms=1, x_inv=1,
            diag_ready=1, diag_mm=1, inv_row_ready=1,
            prm_ready=1, wdt_landed=16, wdt_hi_ready=1, wdt_ready=1,
            dt_mm=1, dtT_ready=1, dt_turned=1, dt_abs=1, dt_exp=1, row_exp=1, adt_hi_ready=1, adt_ready=1, decay_mm=1, decay_ready=1,
            conv_step=48, silu_ready=3,
            xtok_mm=4, xtok_ready=4, skip_done=4, xdt_ready=4, xdd_ready=2,
            btok_mm=1, btok_ready=1, cb_mm=1, cbm_ready=1, state_mm=1, state_ready=1,
            sega_hi=8, sega_ready=8, seg_mm=8, sege_ready=8, segm_ready=8, yd_mm=8, yoff_mm=2,
            y_added=4, yoff_mul=2, yoff_added=2,
            rope_swapped=8, rope_mul=8, rope_cos=8, rope_ready=8,
            score_mm=4, nmax_ready=4, probs_ready=4, pt_mm=4, pt_a=4, pt_v=4, pv_mm=4, attn_out=4,
            attn_ms=1, attn_inv=1, attn_ready=1, attnT_mm=4, attnT_hi=4, attnT_ready=4,
            gated=2, ssd_ms=2, ssd_inv=2, ssd_ready=2, ssdT_mm=4, ssdT_hi=4, ssdT_ready=4,
            squared=SQ_Y1,
            gain_landed=32, y_ms=2, y_inv=2, y_gained=8, y_zero=1,
            u_hi_ready=up_banks,
            u_sq=up_banks,
            u_ready=up_banks,
            dve_chain=DVE_LINKS,
        )
        sem = {n: ctx.enter_context(nc.semaphore(n)) for n in per}
        raw_landed = [ctx.enter_context(nc.semaphore(f"raw_landed{s}")) for s in range(RING)]
        acc_free = [ctx.enter_context(nc.semaphore(f"acc_free{i}")) for i in range(2)]
        names = ["const_step", "const_ready", "typed_ready", "prm_landed", "row_landed", "row_zero", "pos_landed",
                 "pos_ready", "table_step", "table_angle", "table_sin", "table_ready", "prm_mm", "prm_copied",
                 "out_landed"]
        x_landed = [ctx.enter_context(nc.semaphore(f"x_landed{c}")) for c in range(4)]
        once = {n: ctx.enter_context(nc.semaphore(n)) for n in names}

        def upto(name, l, n):
            return sem[name], l * per[name] + n

        def chunk(b, c):
            return b * NC + c

        def through(l, b):
            return sem["mm_done"], RING + chunk(l * NB + b + 1, 0)

        def left(l, b, n, pairs=0):
            return acc_free[b % 2], 2 * (l * ((NB + 1 - b % 2) // 2) + b // 2 + pairs) + 2 + n

        def heads8(a, t, g):
            return a[:, t, g * CB:(g + 1) * CB].rearrange("p (h n) -> p h n", h=SH // SG)

        def per_head(a, g):
            n = SH // SG
            return a[:, g * n:(g + 1) * n].unsqueeze(2).broadcast_to([P, n, SP_])

        def four(a):
            return a.rearrange("p (h n) -> p h n", h=4)

        block = ctx.enter_context(nc.Block())

        @block.sync
        def _(sp):
            def load(b, c, src):
                sp.wait_ge(sem["split_done"], chunk(b, c) + 1)
                sp.dma_start(raw[:, c % RING].rearrange("p (k n) -> p k n", k=CK),
                             src.rearrange("(k p) n -> p k n", p=P)).then_inc(raw_landed[c % RING], 16)

            def load_block(b, w, l, r0, c0):
                for c in range(NC):
                    load(b, c, w[l, bass.ds(r0 + c * CK * P, CK * P), bass.ds(c0, CB)])

            for c in range(4):
                sp.dma_start(x_sb[:, :, c * CB:(c + 1) * CB],
                             x[0, :, c * CB:(c + 1) * CB].rearrange("(t p) n -> p t n", p=P))\
                    .then_inc(x_landed[c], 16)
            for i, a in enumerate((dt_bias, a_log, d_skip)):
                sp.dma_start(row_all[:, 0:DEPTH, i], a.partition_broadcast(P)).then_inc(once["row_landed"], 16)
            with sp.Fori(0, DEPTH) as l:
                for b0, n, c0 in ((B_XBC, B_Q - B_XBC, COL_XBC), (B_Q, B_OUT - B_Q, COL_Q)):
                    with sp.Fori(0, n) as i:
                        load_block(l * NB + b0 + i, w_in, l, 0, i * CB + c0)
                with sp.Fori(0, B_MLP - B_OUT) as i:
                    load_block(l * NB + B_OUT + i, w_out, l, 0, i * CB)
                with sp.Fori(0, QUARTERS) as q:
                    with sp.Fori(0, QB) as i:
                        load_block(l * NB + q * (2 * QB) + i + B_MLP, w_up, l, 0, q * (QB * CB) + i * CB)
                    with sp.Fori(0, QB) as i:
                        load_block(l * NB + q * (2 * QB) + i + (B_MLP + QB), w_down, l, q * (QB * CB), i * CB)
            for c in range(AHEAD):
                load(DEPTH * NB, c, w_in[0, c * CK * P:(c + 1) * CK * P, COL_XBC:COL_XBC + CB])
            for c in range(4):
                sp.wait_ge(*upto("x_ready", DEPTH, 2 * (c + 1)))
                for t in range(TT):
                    sp.dma_start(out[0, t * P:(t + 1) * P, c * CB:(c + 1) * CB],
                                 x_sb[:, t, c * CB:(c + 1) * CB]).then_inc(once["out_landed"], 16)
            for s in range(RING):
                sp.wait_ge(raw_landed[s], 16 * (2 * DEPTH * NB + (1 if s < AHEAD else 0)))
            sp.wait_ge(once["out_landed"], 16 * 4 * TT)

        @block.gpsimd
        def _(pool):
            step, ready = once["const_step"], once["const_ready"]
            pool.memset(sq[:], 0.0).then_inc(sem["mm_done"], RING)
            pool.memset(ysq[:], 0.0).then_inc(acc_free[0], 2)
            pool.memset(minus_half[:], -0.5).then_inc(acc_free[1], 2)
            pool.memset(ident[:], 0.0).then_inc(step, 1)
            pool.memset(tri[:], 1.0).then_inc(step, 1)
            pool.memset(low_w[:], 1.0).then_inc(step, 1)
            pool.memset(cmask_w[:], 0.0).then_inc(step, 1)
            pool.memset(ones[:], 1.0).then_inc(ready, 1)
            pool.memset(convr[:, :, :, 0:TAPS - 1], 0.0).then_inc(ready, 1)
            pool.wait_ge(step, 4)
            pool.affine_select(out=ident[:], in_=ident[:], compare_op=ALU.not_equal, fill=1.0, base=0,
                               pattern=[[-1, P]], channel_multiplier=1).then_inc(ready, 1)
            pool.affine_select(out=tri[:], in_=tri[:], compare_op=ALU.is_ge, fill=0.0, base=0,
                               pattern=[[1, P]], channel_multiplier=-1).then_inc(ready, 1)
            pool.affine_select(out=low_w[:], in_=low_w[:], compare_op=ALU.is_gt, fill=0.0, base=0,
                               pattern=[[-1, P]], channel_multiplier=1).then_inc(step, 1)
            pool.affine_select(out=cmask_w[:], in_=cmask_w[:], compare_op=ALU.is_ge, fill=NEG, base=0,
                               pattern=[[-1, P]], channel_multiplier=1).then_inc(step, 1)
            pool.memset(wdt_w[:], 0.0).then_inc(step, 1)
            pool.memset(row_all[:, DEPTH], 0.0).then_inc(once["row_zero"], 1)
            for c in range(4):
                pool.wait_ge(x_landed[c], 16)
                pool.memset(rinv[:, c:c + 1], 0.0).then_inc(sem["x_ready"], 2)
            pool.wait_ge(once["row_landed"], 16 * 3)
            pool.tensor_copy(row[:], row_all[:, 0]).then_inc(once["row_zero"], 1)
            pool.wait_ge(once["row_zero"], 2)
            pool.wait_ge(once["prm_copied"], DEPTH)

            with pool.Fori(0, DEPTH) as l:
                def power(name, n, k_out, k_in, waited, w_n):
                    pool.wait_ge(*upto(waited, l, w_n))
                    return pool.tensor_tensor(st[:, k_out], st[:, k_in], minus_half[:], ALU.pow)

                pool.wait_ge(sem["mm_done"], RING + chunk(l * NB, 0))
                pool.dma_start(wdt.rearrange("p (k n) -> p k n", n=SH), w_in[bass.ds(l, 1), :, COL_DT:COL_DT + SH]
                               .rearrange("a (k p) n -> p (a k) n", p=P)).then_inc(sem["wdt_landed"], 16)
                power("x_inv", 1, X_INV, X_MS, "x_ms", 1).then_inc(sem["x_inv"], 1)
                pool.wait_ge(*upto("xtok_ready", l, 4))
                for i in range(TT * SG):
                    t, g = divmod(i, SG)
                    pool.tensor_tensor(heads8(ys, t, g), heads8(x_tok, t, g), per_head(row[:, 2], g),
                                       ALU.mult).then_inc(sem["skip_done"], 1)

                def seg_weights(i):
                    t, g, hh = i // 4, i // 2 % 2, i % 2
                    h0 = g * 8 + hh * 4
                    if i >= 2:
                        pool.wait_ge(*upto("seg_mm", l, i - 1))
                    for dst, a, done in ((seg_hi, adt_hi, "sega_hi"), (seg_lo, adt_lo, "sega_ready")):
                        pool.tensor_tensor(four(dst[i % 2]), tri[:].unsqueeze(1).broadcast_to([P, 4, P]),
                                           a[:, t, h0:h0 + 4].bitcast(F32).unsqueeze(2)
                                           .broadcast_to([P, 4, P]), ALU.mult).then_inc(sem[done], 1)

                def rope_cos(r):
                    pool.wait_ge(*upto("rope_swapped", l, r + 1))
                    pool.wait_ge(once["table_ready"], 1)
                    pool.tensor_tensor(qk[0:ROPE, 2 * r:2 * r + 2], qk[0:ROPE, 2 * r:2 * r + 2],
                                       cosT[:].unsqueeze(1).broadcast_to([ROPE, 2, SEQ]),
                                       ALU.mult).then_inc(sem["rope_cos"], 1)

                for slot in range(PE_SEG[0] - 3, AD_ROPE[-1] + 1):
                    if slot + 3 in PE_SEG:
                        seg_weights(PE_SEG.index(slot + 3))
                    if slot + 2 in AD_ROPE:
                        rope_cos(AD_ROPE.index(slot + 2))
                power("ssd", 1, S0_INV, S0_MS, "ssd_ms", 1).then_inc(sem["ssd_inv"], 1)
                power("attn", 1, A_INV, A_MS, "attn_ms", 1).then_inc(sem["attn_inv"], 1)
                power("ssd", 2, S1_INV, S1_MS, "ssd_ms", 2).then_inc(sem["ssd_inv"], 1)
                power("y", 1, Y_INV, Y_MS, "y_ms", 1).then_inc(sem["y_inv"], 1)
                pool.wait_ge(*upto("xT_ready", l, 16))
                pool.tensor_copy(row[:].rearrange("p i n -> p (i n)"),
                                 row_all[:].rearrange("p l i n -> p (l i n)")[:, bass.ds(l * (3 * SH) + 3 * SH, 3 * SH)])
                pool.tensor_copy(prm[:], prm_next[:].rearrange("p l n -> p (l n)")[:, bass.ds(l * NPRM, NPRM)])\
                    .then_inc(sem["prm_ready"], 1)
                power("y", 2, Y_INV, Y_MS, "y_ms", 2).then_inc(sem["y_inv"], 1)

        @block.scalar
        def _(act):
            act.dma_start(tab_pos.bitcast(I32), positions[0].partition_broadcast(ROPE))\
                .then_inc(once["pos_landed"], 16)
            for r0, n, a in ((G_MIX, KT, pre_mix_norm), (G_MLP, KT, pre_mlp_norm),
                             (G_ATTN, AW // P, attn_out_norm), (G_SSD, SW // P, ssd_out_norm),
                             (G_TAP, TAPS * NCT, conv_w.rearrange("l k n -> l (k n)")), (G_BIAS, NCT, conv_b)):
                act.dma_start(probs[r0:r0 + n, 0:DEPTH * P].rearrange("r (l n) -> r l n", n=P),
                              a.rearrange("l (r n) -> r l n", n=P)).then_inc(once["prm_landed"], 16)
            act.wait_ge(once["prm_mm"], DEPTH)
            act.activation(prm[:], M[0][:, 0:NPRM], ACT.Copy).then_inc(sem["prm_ready"], 1)
            act.wait_ge(once["table_angle"], 1)
            act.activation(sinT[:], tab_angle, ACT.Sin, scale=freq[:, 1:2])
            act.activation(tab_sin, tab_angle, ACT.Sin, scale=0.5).then_inc(once["table_sin"], 1)

            def round_hi(b, c):
                act.wait_ge(raw_landed[c % RING], (b * (NC // RING) + c // RING + 1) * 16)
                act.wait_ge(sem["mm_done"], chunk(b, c) + 1)
                act.activation(w_hi[:, c % RING], raw[:, c % RING], ACT.Copy).then_inc(sem["hi_ready"], 1)

            for c in range(AHEAD):
                round_hi(0, c)
            with act.Fori(0, DEPTH) as l:
                squares = [0]

                def square(in_, total, extra=0):
                    if squares[0] or extra:
                        act.wait_ge(*upto("squared", l, squares[0] + extra))
                    act.activation(junk, in_, ACT.Square, accum_out=total).then_inc(sem["squared"], 1)
                    squares[0] += 1

                def load_gain(gains):
                    act.dma_start(zg[:], gains[bass.ds(l, 1)].rearrange("a n -> (a n)").partition_broadcast(P))\
                        .then_inc(sem["gain_landed"], 16)

                def x_hi(n, j, gain):
                    act.wait_ge(*upto("xT_mm", l, 8 * n + j + 1))
                    for kk in range(2):
                        k = 2 * j + kk
                        ins = act.activation(a_hi[:, k], M[j % 4][:, kk * SEQ:(kk + 1) * SEQ], ACT.Copy,
                                             scale=prm[:, gain + k:gain + k + 1])
                    ins.then_inc(sem["xT_hi"], 1)

                def x_squares(n, c):
                    act.wait_ge(*upto("x_ready", l, 8 * n + 2 * c + 2))
                    for t in range(TT):
                        square(x_sb[:, t, c * CB:(c + 1) * CB], sq[:, t, c:c + 1])

                def norm_turn(n, slot, gain, split):
                    if slot == AHEAD:
                        x_hi(n, 0, gain)
                        x_hi(n, 1, gain)
                    split()
                    if slot in NORM_AD:
                        for j in NORM_AD[slot]:
                            x_hi(n, j, gain)
                        x_squares(n, slot - AHEAD)

                def to_hi(name, n, j, bank, gain):
                    act.wait_ge(*upto(name + "_mm", l, n))
                    for kk in range(2):
                        k = 2 * j + kk
                        ins = act.activation(u_hi[:, k], M[bank][:, kk * SEQ:(kk + 1) * SEQ], ACT.Copy,
                                             scale=prm[:, gain + k:gain + k + 1])
                    ins.then_inc(sem[name + "_hi"], 1)

                act.wait_ge(*upto("prm_ready", l, 1))
                for slot in range(AHEAD, MIX_SLOTS + AHEAD):
                    b, c = divmod(slot, NC)
                    norm_turn(0, slot, G_MIX, lambda: round_hi(l * NB + b, c))
                    if slot == AD_DIAG:
                        act.wait_ge(*upto("wdt_landed", l, 16))
                        act.activation(wdt_hi[:, 0:KT * SH], wdt, ACT.Copy).then_inc(sem["wdt_hi_ready"], 1)
                    if slot == leaves(0):
                        act.wait_ge(*upto("diag_mm", l, 1))
                        act.activation(inv_row[:], M[0][:, 0:SEQ], ACT.Copy).then_inc(sem["inv_row_ready"], 1)
                    if slot == AD_DT:
                        act.wait_ge(*upto("dt_abs", l, 1))
                        act.activation(dts[:, DT_EXP], dts[:, DT_ABS], ACT.Exp, scale=-1.0)\
                            .then_inc(sem["dt_exp"], 1)
                        act.activation(row[:, 1], row[:, 1], ACT.Exp).then_inc(sem["row_exp"], 1)
                    if slot == AD_DECAY:
                        act.wait_ge(*upto("decay_mm", l, 1))
                        act.activation(decay[:].rearrange("p a n -> p (a n)"), M[0][:, 0:2 * SH], ACT.Exp)\
                            .then_inc(sem["decay_ready"], 1)
                    for i in range(3):
                        if slot == leaves(i) + 3:
                            act.wait_ge(*upto("conv_step", l, 16 * (i + 1)))
                            act.activation(xbcT[:, 4 * i:4 * i + 4], xbcT[:, 4 * i:4 * i + 4], ACT.Silu)\
                                .then_inc(sem["silu_ready"], 1)
                    for i in range(TT * SG):
                        if slot == AD_XTOK + i:
                            t, g = divmod(i, SG)
                            act.wait_ge(*upto("xtok_mm", l, i + 1))
                            act.activation(x_tok[:, t, g * CB:(g + 1) * CB], M[i][:], ACT.Copy)\
                                .then_inc(sem["xtok_ready"], 1)
                    if slot == AD_CB:
                        act.wait_ge(*upto("btok_mm", l, 1))
                        act.activation(b_tok[:].rearrange("p g n -> p (g n)"), M[0][:, 0:SG * SN], ACT.Copy)\
                            .then_inc(sem["btok_ready"], 1)
                    if slot == AD_STATE:
                        act.wait_ge(*upto("state_mm", l, 1))
                        act.activation(wk[:, 2], M[0][:], ACT.Copy)
                        act.activation(wk[:, 3], M[3][:], ACT.Copy).then_inc(sem["state_ready"], 1)
                    for i in range(8):
                        if slot == AD_SEG[i]:
                            act.wait_ge(*upto("seg_mm", l, i + 1))
                            if i:
                                act.wait_ge(*upto("yd_mm", l, i))
                            act.activation(seg_e, M[1][:], ACT.Exp).then_inc(sem["sege_ready"], 1)
                    for p in range(4):
                        if slot == AD_SOFT[p]:
                            act.wait_ge(*upto("nmax_ready", l, p + 1))
                            for hh in range(2):
                                o = hh * 3 * P
                                act.activation(probs[:, o:o + 2 * P], M[0][:, hh * 2 * P:(hh + 1) * 2 * P],
                                               ACT.Exp, bias=mx[:, 2 * hh + 1:2 * hh + 2], scale=DH ** -0.5,
                                               accum_out=rs[:, 2 * hh + 1:2 * hh + 2])
                                ins = act.activation(probs[:, o + 2 * P:o + 3 * P], M[3][:, hh * P:(hh + 1) * P],
                                                     ACT.Exp, bias=mx[:, 2 * hh:2 * hh + 1], scale=DH ** -0.5,
                                                     accum_out=rs[:, 2 * hh:2 * hh + 1])
                            ins.then_inc(sem["probs_ready"], 1)
                        if slot == AD_PT[p]:
                            act.wait_ge(*upto("pt_mm", l, p + 1))
                            act.activation(probsT[:, 0:3 * P], M[1][:, 0:3 * P], ACT.Copy).then_inc(sem["pt_a"], 1)
                    for i in range(2):
                        if slot == leaves(B_V + i):
                            act.wait_ge(*through(l, B_V + i))
                            for t in range(TT):
                                act.activation(v_tok[:, t, i * CB:(i + 1) * CB], acc[(B_V + i) % 2][t][:], ACT.Copy,
                                               scale=st[:, X_INV, t:t + 1]).then_inc(acc_free[(B_V + i) % 2], 1)
                    for g in range(SG):
                        if slot == leaves(B_Z + g):
                            act.wait_ge(*through(l, B_Z + g))
                            for t in range(TT):
                                act.activation(zs[:, t, g * CB:(g + 1) * CB], acc[(B_Z + g) % 2][t][:], ACT.Silu,
                                               scale=st[:, X_INV, t:t + 1]).then_inc(acc_free[(B_Z + g) % 2], 1)
                        if slot == leaves(B_Z + g) + 1:
                            act.wait_ge(*upto("gated", l, g + 1))
                            for t in range(TT):
                                square(ys[:, t, g * CB:(g + 1) * CB], ssq[:, 1 + g, t:t + 1])
                            if g == 1:
                                load_gain(post_mix_norm)
                    if slot == AD_ATTN_NORM:
                        act.wait_ge(*upto("attn_out", l, 4))
                        for t in range(TT):
                            act.wait_ge(*upto("squared", l, squares[0]))
                            act.activation(x_tok[:, t].rearrange("p (h d) -> p h d", d=DH), attn[:, :, t, :],
                                           ACT.Square, accum_out=ssq[:, 0, t:t + 1]).then_inc(sem["squared"], 1)
                            squares[0] += 1
                    for j in range(4):
                        if slot == AD_SSDT[j]:
                            to_hi("ssdT", j + 1, 4 + j, SSDT_BANK[j], G_ATTN)
                        if slot == AD_ATTNT[j]:
                            to_hi("attnT", j + 1, j, ATTNT_BANK[j], G_ATTN)
                    for i in range(4):
                        if slot == leaves(B_OUT + i):
                            act.wait_ge(*through(l, B_OUT + i))
                            for t in range(TT):
                                a = acc[(B_OUT + i) % 2][t]
                                square(a[:], ysq[:, t, i:i + 1])
                def up_pair(q, i):
                    for j in range(2):
                        b = l * NB + q * (2 * QB) + i * 2 + (B_MLP + j)
                        first = j == 0 and is_first(q, i)
                        for c in range(AHEAD, NC + AHEAD):
                            split = (lambda: round_hi(b, c)) if c < NC else (lambda: round_hi(b + 1, c - NC))
                            if first:
                                norm_turn(1, c, G_MLP, split)
                            else:
                                split()
                        if first:
                            assert squares[0] == SQ_X1
                            act.wait_ge(*left(l, B_MLP - 1, 2))
                            load_gain(post_mlp_norm)
                        act.wait_ge(sem["mm_done"], RING + chunk(b + 1, 0))
                        for k in range(2):
                            n = q * (2 * QB) + i * 4 + (2 * j + k)
                            act.wait_ge(*upto("u_sq", l, n + 1))
                            act.activation(wk[:, k], acc[1 - j][k][:], ACT.Relu).then_inc(acc_free[1 - j], 1)
                            act.wait_ge(*left(l, B_MLP + j, k + 1, q * QB + i))
                            u = u_hi[:, 8 * i + 4 * j + 2 * k:8 * i + 4 * j + 2 * k + 2] if type(i) is int else \
                                u_hi[:, bass.ds(i * 8 + (4 * j + 2 * k), 2)]
                            act.activation(u.rearrange("p k s -> p (k s)"), wk[:, k], ACT.Square)\
                                .then_inc(sem["u_hi_ready"], 1)

                def down_pair(q, i):
                    for j in range(2):
                        b = l * NB + q * (2 * QB) + i * 2 + (B_MLP + QB + j)
                        for c in range(AHEAD, NC):
                            round_hi(b, c)
                        for c in range(AHEAD):
                            round_hi(b + 1, c)
                        if type(q) is not int:
                            continue
                        for t in range(TT):
                            act.wait_ge(*left(l, B_MLP + QB + j, t + 1, q * QB + i))
                            n = 2 * i + j
                            square(y[:, t, n * CB:(n + 1) * CB], ysq[:, t, n:n + 1])

                up_pair(0, 0)
                up_pair(0, 1)
                with act.Fori(0, QUARTERS - 1) as q:
                    with act.Fori(0, QB // 2) as i:
                        down_pair(q, i)
                    with act.Fori(0, QB // 2) as i:
                        up_pair(q + 1, i)
                down_pair(QUARTERS - 1, 0)
                down_pair(QUARTERS - 1, 1)
                assert squares[0] == SQ_Y1

        @block.tensor
        def _(pe):
            pe.wait_ge(once["const_ready"], 4)
            pe.wait_ge(once["prm_landed"], 16 * 6)
            for l in range(DEPTH):
                pe.transpose(M[l][:, 0:NPRM], probs[0:NPRM, l * P:(l + 1) * P], ident[0:NPRM, 0:NPRM])\
                    .then_inc(once["prm_mm"], 1)
            pe.wait_ge(once["prm_copied"], DEPTH)
            pe.wait_ge(sem["prm_ready"], 1)

            def take(b, c):
                pe.wait_ge(sem["split_done"], RING + 1 + chunk(b, c))

            def token_chunk(c, par, s_hi, s_lo):
                for kk in range(CK):
                    k = c * CK + kk
                    wh, wl = (w[:, c % RING, kk * CB:(kk + 1) * CB] for w in (w_hi, w_lo))
                    for t in range(TT):
                        o = acc[par][t][:]
                        sh, sl = (s[:, k, t * P:(t + 1) * P] for s in (s_hi, s_lo))
                        pe.matmul(o, sh, wh, start=(k == 0), stop=False)
                        pe.matmul(o, sh, wl, start=False, stop=False)
                        ins = pe.matmul(o, sl, wh, start=False, stop=(k == KT - 1))
                ins.then_inc(sem["mm_done"], 1)

            def feature_chunk(c, par):
                for kk in range(CK):
                    k = c * CK + kk
                    for m in range(CB // P):
                        o = acc[par][m // 2][:, m % 2 * SEQ:(m % 2 + 1) * SEQ]
                        wh, wl = (w[:, c % RING, kk * CB + m * P:kk * CB + (m + 1) * P] for w in (w_hi, w_lo))
                        pe.matmul(o, wh, a_hi[:, k], start=(k == 0 and m % 2 == 0), stop=False,
                                  skip_group_check=True)
                        pe.matmul(o, wh, a_lo[:, k], start=False, stop=False, skip_group_check=True)
                        ins = pe.matmul(o, wl, a_hi[:, k], start=False, stop=(k == KT - 1),
                                        skip_group_check=True)
                ins.then_inc(sem["mm_done"], 1)

            with pe.Fori(0, DEPTH) as l:
                def x_turn(n, j):
                    if j % 2 == 0:
                        pe.wait_ge(*upto("x_ready", l, 8 * n + j + 2))
                    if j >= 4:
                        pe.wait_ge(*upto("xT_ready", l, 8 * n + j - 3))
                    for kk in range(2):
                        for t in range(TT):
                            k = 2 * j + kk
                            ins = pe.transpose(M[j % 4][:, kk * SEQ + t * P:kk * SEQ + (t + 1) * P],
                                               x_sb[:, t, k * P:(k + 1) * P], ident[:])
                    ins.then_inc(sem["xT_mm"], 1)

                def inv_row_and_dt():
                    pe.wait_ge(once["typed_ready"], 5)
                    pe.wait_ge(*upto("diag_ready", l, 1))
                    for t in range(TT):
                        ins = pe.matmul(M[0][:, t * P:(t + 1) * P], ones[:], diag[:, t], start=True, stop=True)
                    ins.then_inc(sem["diag_mm"], 1)
                    pe.wait_ge(*upto("wdt_ready", l, 1))
                    o = M[1][:, 0:SEQ]
                    for k in range(KT):
                        wh, wl = (w[:, k * SH:k * SH + P] for w in (wdt_hi, wdt_lo))
                        pe.matmul(o, wh, a_hi[:, k], start=(k == 0), stop=False)
                        pe.matmul(o, wh, a_lo[:, k], start=False, stop=False)
                        ins = pe.matmul(o, wl, a_hi[:, k], start=False, stop=(k == KT - 1))
                    ins.then_inc(sem["dt_mm"], 1)

                def dt_turn():
                    pe.wait_ge(*upto("dtT_ready", l, 1))
                    for t in range(TT):
                        ins = pe.transpose(M[1][:, t * P:(t + 1) * P], dtT[:, t * P:(t + 1) * P], ident[:])
                    ins.then_inc(sem["dt_turned"], 1)

                def decays():
                    pe.wait_ge(*upto("adt_ready", l, 1))
                    pe.wait_ge(*upto("inv_row_ready", l, 1))
                    pe.matmul(M[0][:, 0:SH], low[:].bitcast(F32), dts[:, A_DT, 0], start=True, stop=True)
                    pe.matmul(M[0][:, SH:2 * SH], tri[:], dts[:, A_DT, 1], start=True, stop=True)\
                        .then_inc(sem["decay_mm"], 1)

                def x_tokens(i):
                    t, g = divmod(i, SG)
                    pe.wait_ge(*upto("silu_ready", l, g + 1))
                    pe.wait_ge(*upto("decay_ready", l, 1))
                    for k in range(4):
                        ins = pe.transpose(M[i][:, k * P:(k + 1) * P], xbcT[:, 4 * g + k, t * P:(t + 1) * P],
                                           ident[:])
                    ins.then_inc(sem["xtok_mm"], 1)

                def b_tokens_and_cb():
                    pe.wait_ge(*upto("silu_ready", l, 3))
                    pe.wait_ge(*upto("xtok_ready", l, 4))
                    nx = SW // P
                    for g in range(SG):
                        ins = pe.transpose(M[0][:, g * P:(g + 1) * P], xbcT[:, nx + g, 0:P], ident[:])
                    ins.then_inc(sem["btok_mm"], 1)
                    for t in range(TT):
                        for g in range(SG):
                            i = t * SG + g
                            ins = pe.matmul(M[1][:, i * P:(i + 1) * P], xbcT[:, nx + g, t * P:(t + 1) * P],
                                            xbcT[:, nx + SG + g, t * P:(t + 1) * P], start=True, stop=True)
                    ins.then_inc(sem["cb_mm"], 1)

                def states():
                    pe.wait_ge(*upto("btok_ready", l, 1))
                    pe.wait_ge(*upto("xdd_ready", l, 2))
                    for g in range(SG):
                        ins = pe.matmul(M[3 * g][:], b_tok[:, g], wk[:, 2 + g], start=True, stop=True)
                    ins.then_inc(sem["state_mm"], 1)

                def segment_sums(i):
                    pe.wait_ge(*upto("sega_ready", l, i + 1))
                    if i:
                        pe.wait_ge(*upto("sege_ready", l, i))
                    else:
                        pe.wait_ge(*upto("cbm_ready", l, 1))
                    pe.matmul(M[1][:], low[:], seg_hi[i % 2], start=True, stop=False)
                    pe.matmul(M[1][:], low[:], seg_lo[i % 2], start=False, stop=True).then_inc(sem["seg_mm"], 1)

                def y_diagonal(i):
                    t, g, hh = i // 4, i // 2 % 2, i % 2
                    pe.wait_ge(*upto("segm_ready", l, i + 1))
                    if i == 0:
                        pe.wait_ge(*upto("state_ready", l, 1))
                        pe.wait_ge(*upto("xdt_ready", l, 4))
                    if i in (4, 6):
                        pe.wait_ge(*upto("y_added", l, i // 2 - 1))
                    for h in range(4):
                        o = (hh * 4 + h) * SP_
                        ins = pe.matmul(M[3 * g][:, o:o + SP_], seg_e[:, h * P:(h + 1) * P],
                                        x_tok[:, t, g * CB + o:g * CB + o + SP_], start=True, stop=True)
                    ins.then_inc(sem["yd_mm"], 1)

                def y_offset(g):
                    if g == 1:
                        pe.wait_ge(*upto("sege_ready", l, 8))
                    pe.matmul(M[2 - g][:], xbcT[:, SW // P + SG + g, P:2 * P], wk[:, 2 + g], start=True,
                              stop=True).then_inc(sem["yoff_mm"], 1)

                def scores(p):
                    pe.wait_ge(*upto("rope_ready", l, 4 + p + 1))
                    if p == 0:
                        pe.wait_ge(*upto("y_added", l, 4))
                    else:
                        pe.wait_ge(*upto("pt_v", l, p))
                    for hh in range(2):
                        h = 2 * p + hh
                        o = M[0][:, hh * SEQ:(hh + 1) * SEQ]
                        pe.matmul(o, qk[:, h, P:SEQ], qk[:, HEADS + h], start=(hh == 0), stop=False,
                                  skip_group_check=True)
                        pe.matmul(o[:, P:SEQ], ident_b[:], cmask[:], start=False, stop=True,
                                  skip_group_check=True)
                    for hh in range(2):
                        h = 2 * p + hh
                        o = M[3][:, hh * P:(hh + 1) * P]
                        pe.matmul(o, qk[:, h, 0:P], qk[:, HEADS + h, 0:P], start=(hh == 0), stop=False,
                                  skip_group_check=True)
                        ins = pe.matmul(o, ident_b[:], cmask[:], start=False, stop=True, skip_group_check=True)
                    ins.then_inc(sem["score_mm"], 1)

                def probs_turn(p):
                    pe.wait_ge(*upto("probs_ready", l, p + 1))
                    if p == 0:
                        pe.wait_ge(*upto("yoff_mul", l, 2))
                    else:
                        pe.wait_ge(*upto("attn_out", l, p))
                    for hh in range(2):
                        for i in range(3):
                            ins = pe.transpose(M[1 + 2 * hh][:, i * P:(i + 1) * P],
                                               probs[:, (3 * hh + i) * P:(3 * hh + i + 1) * P], ident[:])
                    ins.then_inc(sem["pt_mm"], 1)

                def values(p):
                    pe.wait_ge(*upto("pt_a", l, p + 1))
                    pe.wait_ge(*upto("pt_v", l, p + 1))
                    pe.wait_ge(*left(l, B_V + p // 2, 2))
                    for hh in range(2):
                        h = 2 * p + hh
                        v0, v1 = (v_tok[:, t, h * DH:(h + 1) * DH] for t in range(TT))
                        a10, a11, a00 = (probsT[:, (3 * hh + i) * P:(3 * hh + i + 1) * P] for i in range(3))
                        o = M[1][:, 2 * hh * P:(2 * hh + 1) * P]
                        pe.matmul(o, a00, v0, start=True, stop=True)
                        o = M[1][:, (2 * hh + 1) * P:(2 * hh + 2) * P]
                        pe.matmul(o, a10, v0, start=True, stop=False)
                        ins = pe.matmul(o, a11, v1, start=False, stop=True)
                    ins.then_inc(sem["pv_mm"], 1)

                def attn_turn(j):
                    if j == 0:
                        pe.wait_ge(*upto("attn_ready", l, 1))
                    if j == 3:
                        pe.wait_ge(*upto("attnT_ready", l, 1))
                    for kk in range(2):
                        for t in range(TT):
                            ins = pe.transpose(M[ATTNT_BANK[j]][:, kk * SEQ + t * P:kk * SEQ + (t + 1) * P],
                                               attn[:, 2 * j + kk, t, :], ident[:])
                    ins.then_inc(sem["attnT_mm"], 1)

                def ssd_turn(j):
                    pe.wait_ge(*upto("ssd_ready", l, j // 2 + 1))
                    if j in (1, 2):
                        pe.wait_ge(*upto("ssdT_ready", l, j))
                    if j == 3:
                        pe.wait_ge(*upto("attnT_ready", l, 3))
                    for kk in range(2):
                        for t in range(TT):
                            k = 2 * j + kk
                            ins = pe.transpose(M[SSDT_BANK[j]][:, kk * SEQ + t * P:kk * SEQ + (t + 1) * P],
                                               ys[:, t, k * P:(k + 1) * P], ident[:])
                    ins.then_inc(sem["ssdT_mm"], 1)

                x_turn(0, 0)
                x_turn(0, 1)
                for slot in range(MIX_SLOTS):
                    b, c = divmod(slot, NC)
                    if c == 0:
                        pe.wait_ge(*left(l, b, 0))
                    take(l * NB + b, c)
                    if b == 0:
                        pe.wait_ge(*upto("xT_ready", l, c + 1))
                    if b == B_OUT:
                        pe.wait_ge(*(upto("attnT_ready", l, c + 1) if c < 4 else upto("ssdT_ready", l, c - 3)))
                    if b < B_V:
                        feature_chunk(c, b % 2)
                    elif b < B_OUT:
                        token_chunk(c, b % 2, a_hi, a_lo)
                    else:
                        token_chunk(c, b % 2, u_hi, u_lo)
                    for j in NORM_PE.get(slot, ()):
                        x_turn(0, j)
                    if slot == PE_DT:
                        inv_row_and_dt()
                    if slot == PE_DT_TURN:
                        dt_turn()
                    if slot == PE_DECAY:
                        decays()
                    if PE_XTOK <= slot < PE_XTOK + TT * SG:
                        x_tokens(slot - PE_XTOK)
                    if slot == PE_CB:
                        b_tokens_and_cb()
                    if slot == PE_STATE:
                        states()
                    if slot in PE_YD:
                        y_diagonal(PE_YD.index(slot))
                    if slot in PE_YOFF:
                        y_offset(PE_YOFF.index(slot))
                    if slot in PE_SEG:
                        segment_sums(PE_SEG.index(slot))
                    if slot in PE_SCORE:
                        scores(PE_SCORE.index(slot))
                    if slot in PE_PT:
                        probs_turn(PE_PT.index(slot))
                    if slot in PE_PV:
                        values(PE_PV.index(slot))
                    if slot in PE_SSDT:
                        ssd_turn(PE_SSDT.index(slot))
                    if slot in PE_ATTNT:
                        attn_turn(PE_ATTNT.index(slot))

                def up_pair(q, i):
                    for j in range(2):
                        first = j == 0 and is_first(q, i)
                        if first:
                            x_turn(1, 0)
                            x_turn(1, 1)
                        pe.wait_ge(*left(l, B_MLP + j, 0, q * QB + i))
                        for c in range(NC):
                            take(l * NB + q * (2 * QB) + i * 2 + (B_MLP + j), c)
                            pe.wait_ge(*upto("xT_ready", l, 8 + c + 1))
                            feature_chunk(c, 1 - j)
                            if first:
                                for jj in NORM_PE.get(c, ()):
                                    x_turn(1, jj)

                def down_pair(q, i):
                    for j in range(2):
                        pe.wait_ge(*left(l, B_MLP + QB + j, 0, q * QB + i))
                        for c in range(NC):
                            take(l * NB + q * (2 * QB) + i * 2 + (B_MLP + QB + j), c)
                            pe.wait_ge(*upto("u_ready", l, q * (2 * QB) + (c + 1)))
                            token_chunk(c, 1 - j, u_hi, u_lo)

                up_pair(0, 0)
                up_pair(0, 1)
                with pe.Fori(0, QUARTERS - 1) as q:
                    with pe.Fori(0, QB // 2) as i:
                        down_pair(q, i)
                    with pe.Fori(0, QB // 2) as i:
                        up_pair(q + 1, i)
                down_pair(QUARTERS - 1, 0)
                down_pair(QUARTERS - 1, 1)

        @block.vector
        def _(dve):
            dve.memset(mx[:], 0.0).then_inc(sem["split_done"], RING)
            dve.memset(rs[:], 0.0).then_inc(sem["u_sq"], 2)
            tstep = [0]

            def tlink(ins):
                tstep[0] += 1
                ins.then_inc(once["table_step"], 1)
                dve.wait_ge(once["table_step"], tstep[0])

            def split_lo(b, c):
                dve.wait_ge(sem["hi_ready"], chunk(b, c) + 1)
                dve.tensor_tensor(w_lo[:, c % RING], raw[:, c % RING], w_hi[:, c % RING].bitcast(F32),
                                  ALU.subtract).then_inc(sem["split_done"], 1)

            inv_freq = (np.float32(THETA) ** (-np.arange(HALF, dtype=np.float32) / np.float32(HALF)))
            for i in range(HALF):
                ins = dve.memset(tab_f[:, i:i + 1], float(inv_freq[i]))
            tlink(dve.memset(freq[:, 1:2], 1.0))
            tlink(dve.memset(freq[0:HALF, 1:2], -1.0))
            dve.wait_ge(once["const_ready"], 4)
            tlink(dve.tensor_tensor(tab_m, ident[0:ROPE, 0:HALF], ident[0:ROPE, HALF:ROPE], ALU.add))
            tlink(dve.tensor_tensor(tab_m, tab_m, tab_f, ALU.mult))
            tlink(dve.tensor_reduce(freq[:, 0:1], tab_m, AX.X, ALU.add))
            dve.wait_ge(once["pos_landed"], 16)
            tlink(dve.tensor_copy(tab_turn, tab_pos.bitcast(I32)))
            tlink(dve.tensor_scalar(tab_angle, tab_turn, freq[:, 0:1], None, ALU.mult))
            c1 = float(np.float32(6.28125))
            c2 = float(np.float32(np.round((2 * np.pi - c1) * 2 ** 18) / 2 ** 18))
            c3 = float(np.float32(2 * np.pi - c1 - c2))
            tlink(dve.tensor_scalar(tab_turn, tab_angle, float(1 / (2 * np.pi)), 1.5 * 2 ** 23, ALU.mult, ALU.add))
            tlink(dve.tensor_scalar(tab_turn, tab_turn, 1.5 * 2 ** 23, None, ALU.subtract))
            for part in (c1, c2, c3):
                tlink(dve.scalar_tensor_tensor(tab_angle, tab_turn, -part, tab_angle, ALU.mult, ALU.add))
            dve.tensor_scalar(tab_angle, tab_angle, 3.1415925, -3.1415925, ALU.min, ALU.max)\
                .then_inc(once["table_angle"], 1)
            dve.wait_ge(sem["prm_ready"], 1)
            for l in range(DEPTH):
                dve.tensor_copy(prm_next[:, l], M[(l + 1) % DEPTH][:, 0:NPRM]).then_inc(once["prm_copied"], 1)
            for c in range(AHEAD):
                split_lo(0, c)
            dve.tensor_copy(ident_b[:], ident[:]).then_inc(once["typed_ready"], 1)
            dve.wait_ge(once["const_step"], 7)
            dve.tensor_copy(low[:], low_w[:]).then_inc(once["typed_ready"], 1)
            dve.tensor_copy(cmask[:], cmask_w[:]).then_inc(once["typed_ready"], 1)
            dve.tensor_copy(wdt_hi[:, KT * SH:], wdt_w[:]).then_inc(once["typed_ready"], 1)
            dve.tensor_copy(wdt_lo[:, KT * SH:], wdt_w[:]).then_inc(once["typed_ready"], 1)
            dve.wait_ge(once["table_sin"], 1)
            tlink(dve.tensor_tensor(tab_turn, tab_sin, tab_sin, ALU.mult))
            dve.tensor_scalar(cosT[:], tab_turn, -2.0, 1.0, ALU.mult, ALU.add).then_inc(once["table_ready"], 1)

            with dve.Fori(0, DEPTH) as l:
                links = [0]

                def link(ins):
                    links[0] += 1
                    ins.then_inc(sem["dve_chain"], 1)
                    dve.wait_ge(*upto("dve_chain", l, links[0]))

                def x_lo(n, j, gain):
                    dve.wait_ge(*upto("xT_hi", l, 8 * n + j + 1))
                    for kk in range(2):
                        k = 2 * j + kk
                        ins = dve.scalar_tensor_tensor(a_lo[:, k], M[j % 4][:, kk * SEQ:(kk + 1) * SEQ],
                                                       prm[:, gain + k:gain + k + 1], a_hi[:, k].bitcast(F32),
                                                       ALU.mult, ALU.subtract)
                    ins.then_inc(sem["xT_ready"], 1)

                def x_mean(squares):
                    dve.wait_ge(*upto("squared", l, squares))
                    link(dve.tensor_reduce(st[:, X_SUM], sq[:], AX.X, ALU.add))
                    dve.tensor_scalar(st[:, X_MS], st[:, X_SUM], 1.0 / D, EPS, ALU.mult, ALU.add)\
                        .then_inc(sem["x_ms"], 1)

                def to_lo(name, n, j, bank, gain):
                    dve.wait_ge(*upto(name + "_hi", l, n))
                    for kk in range(2):
                        k = 2 * j + kk
                        ins = dve.scalar_tensor_tensor(u_lo[:, k], M[bank][:, kk * SEQ:(kk + 1) * SEQ],
                                                       prm[:, gain + k:gain + k + 1], u_hi[:, k].bitcast(F32),
                                                       ALU.mult, ALU.subtract)
                    ins.then_inc(sem[name + "_ready"], 1)

                def y_mean(squares):
                    dve.wait_ge(*upto("squared", l, squares))
                    link(dve.tensor_reduce(st[:, Y_SUM], ysq[:], AX.X, ALU.add))
                    if squares == SQ_Y0:
                        ins = dve.tensor_scalar(st[:, Y_MS], st[:, Y_SUM], 1.0 / D, EPS, ALU.mult, ALU.add)
                    else:
                        ins = dve.scalar_tensor_tensor(st[:, Y_MS], st[:, Y_SUM], 1.0 / D, st[:, X_EPS],
                                                       ALU.mult, ALU.add)
                    ins.then_inc(sem["y_ms"], 1)

                def update_x(n, c):
                    cols = slice(c * CB, (c + 1) * CB)
                    if c == 0:
                        dve.wait_ge(*upto("y_inv", l, n + 1))
                    for t in range(TT):
                        dve.wait_ge(*(upto("y_gained", l, 2 * c + t + 1) if n else left(l, B_OUT + c, t + 1)))
                        dve.scalar_tensor_tensor(x_sb[:, t, cols], y[:, t, cols], st[:, Y_INV, t:t + 1],
                                                 x_sb[:, t, cols], ALU.mult, ALU.add).then_inc(sem["x_ready"], 1)

                def norm_turn(n, slot, gain, split):
                    if slot == AHEAD:
                        if n:
                            update_x(0, 0)
                        x_lo(n, 0, gain)
                        if n:
                            update_x(0, 1)
                        x_lo(n, 1, gain)
                    split()
                    if slot in NORM_AD:
                        if n and slot - AHEAD in (0, 1):
                            update_x(0, slot - AHEAD + 2)
                        for j in NORM_AD[slot]:
                            x_lo(n, j, gain)

                def dt_steps():
                    dve.wait_ge(*upto("dt_turned", l, 1))
                    dve.wait_ge(*upto("x_inv", l, 1))
                    for t in range(TT):
                        link(dve.scalar_tensor_tensor(dts[:, DT_IN, t], M[1][:, t * P:t * P + SH],
                                                      st[:, X_INV, t:t + 1], row[:, 0], ALU.mult, ALU.add))
                    dve.scalar_tensor_tensor(dts[:, DT_ABS], dts[:, DT_IN], -1.0, dts[:, DT_IN], ALU.mult, ALU.max)\
                        .then_inc(sem["dt_abs"], 1)
                    dve.wait_ge(*upto("dt_exp", l, 1))
                    link(dve.tensor_scalar(dts[:, DT_TMP], dts[:, DT_EXP], 2.0, None, ALU.add))
                    link(dve.reciprocal(dts[:, DT_TMP], dts[:, DT_TMP]))
                    link(dve.tensor_tensor(dts[:, DT_S], dts[:, DT_EXP], dts[:, DT_TMP], ALU.mult))
                    link(dve.tensor_tensor(dts[:, DT_S2], dts[:, DT_S], dts[:, DT_S], ALU.mult))
                    link(dve.tensor_scalar(dts[:, DT], dts[:, DT_S2], 1.0 / 17, None, ALU.mult))
                    for k in (15, 13, 11, 9, 7, 5, 3):
                        link(dve.scalar_tensor_tensor(dts[:, DT], dts[:, DT], 1.0 / k, dts[:, DT_S2],
                                                      ALU.add, ALU.mult))
                    link(dve.scalar_tensor_tensor(dts[:, DT], dts[:, DT], 1.0, dts[:, DT_S], ALU.add, ALU.mult))
                    link(dve.tensor_scalar(dts[:, DT_TMP], dts[:, DT_IN], 0.0, None, ALU.max))
                    link(dve.scalar_tensor_tensor(dts[:, DT], dts[:, DT], 2.0, dts[:, DT_TMP], ALU.mult, ALU.add))
                    dve.wait_ge(*upto("row_exp", l, 1))
                    link(dve.scalar_tensor_tensor(dts[:, A_DT], dts[:, DT], -1.0,
                                                  row[:, 1].unsqueeze(1).broadcast_to([P, TT, SH]),
                                                  ALU.mult, ALU.mult))
                    dve.tensor_copy(adt_hi[:], dts[:, A_DT]).then_inc(sem["adt_hi_ready"], 1)
                    dve.wait_ge(*upto("adt_hi_ready", l, 1))
                    dve.tensor_tensor(adt_lo[:], dts[:, A_DT], adt_hi[:].bitcast(F32), ALU.subtract)\
                        .then_inc(sem["adt_ready"], 1)

                def conv(b, k):
                    n0 = 16 * b + 8 * k
                    dve.wait_ge(*left(l, b, k + 1))
                    for tap in range(TAPS - 1, -1, -1):
                        for m in range(2):
                            ct = 4 * b + 2 * k + m
                            n = n0 + 2 * (TAPS - 1 - tap) + m
                            src = convr[:, k, m, tap:tap + SEQ]
                            wt = prm[:, G_TAP + tap * NCT + ct:G_TAP + tap * NCT + ct + 1]
                            if tap == TAPS - 1:
                                ins = dve.tensor_scalar(xbcT[:, ct], src, wt, prm[:, G_BIAS + ct:G_BIAS + ct + 1],
                                                        ALU.mult, ALU.add)
                            else:
                                dve.wait_ge(*upto("conv_step", l, n - 1))
                                ins = dve.scalar_tensor_tensor(xbcT[:, ct], src, wt, xbcT[:, ct],
                                                               ALU.mult, ALU.add)
                            ins.then_inc(sem["conv_step"], 1)

                def two(a):
                    return a.rearrange("p (m s) -> p m s", m=2)

                inv_two = inv_row[:].unsqueeze(1).broadcast_to([P, 2, SEQ])

                dve.wait_ge(*upto("prm_ready", l, 1))
                for slot in range(AHEAD, MIX_SLOTS + AHEAD):
                    b, c = divmod(slot, NC)
                    if slot in AD_ROPE:
                        r = AD_ROPE.index(slot)
                        dve.wait_ge(*left(l, B_Q + r // 2, r % 2 + 1))
                        if r:
                            dve.wait_ge(*upto("rope_ready", l, r))
                    norm_turn(0, slot, G_MIX, lambda: split_lo(l * NB + b, c))
                    if slot == AHEAD + 4:
                        x_mean(SQ_X0)
                    if slot == AD_DIAG:
                        dve.wait_ge(*upto("x_inv", l, 1))
                        for t in range(TT):
                            ins = dve.tensor_scalar(diag[:, t], ident[:], st[:, X_INV, t:t + 1], None, ALU.mult)
                        ins.then_inc(sem["diag_ready"], 1)
                        dve.wait_ge(*upto("wdt_hi_ready", l, 1))
                        dve.tensor_tensor(wdt_lo[:, 0:KT * SH], wdt, wdt_hi[:, 0:KT * SH].bitcast(F32), ALU.subtract)\
                            .then_inc(sem["wdt_ready"], 1)
                    for i in range(B_V):
                        if slot == leaves(i):
                            dve.wait_ge(*through(l, i))
                            dve.wait_ge(*upto("inv_row_ready", l, 1))
                            for k in range(2):
                                r = (i - B_Q) * 2 + k
                                dst = convr[:, k, :, TAPS - 1:] if i < B_Q else qk[:, 2 * r:2 * r + 2]
                                dve.tensor_tensor(dst, two(acc[i % 2][k][:]), inv_two, ALU.mult)\
                                    .then_inc(acc_free[i % 2], 1)
                        if i < B_Q and slot in (leaves(i) + 1, leaves(i) + 2):
                            conv(i, slot - leaves(i) - 1)
                    if slot == AD_DTT:
                        dve.wait_ge(*upto("dt_mm", l, 1))
                        dve.tensor_copy(dtT, M[1][:, 0:SEQ]).then_inc(sem["dtT_ready"], 1)
                    if slot == AD_DT:
                        dt_steps()
                    if slot == AD_XDT:
                        for i in range(TT * SG):
                            t, g = divmod(i, SG)
                            dve.wait_ge(*upto("skip_done", l, i + 1))
                            dve.tensor_tensor(heads8(x_tok, t, g), heads8(x_tok, t, g), per_head(dts[:, DT, t], g),
                                              ALU.mult).then_inc(sem["xdt_ready"], 1)
                    if slot == AD_XDT + 1:
                        dve.wait_ge(*upto("xdt_ready", l, 4))
                        dve.wait_ge(*upto("decay_ready", l, 1))
                        for g in range(SG):
                            dve.tensor_tensor(wk[:, 2 + g].rearrange("p (h n) -> p h n", n=SP_),
                                              heads8(x_tok, 0, g), per_head(decay[:, 0], g), ALU.mult)\
                                .then_inc(sem["xdd_ready"], 1)
                    if slot == AD_CB:
                        dve.wait_ge(*upto("cb_mm", l, 1))
                        dve.tensor_tensor(cbm[:], four(M[1][:]), tri[:].unsqueeze(1).broadcast_to([P, 4, P]),
                                          ALU.mult).then_inc(sem["cbm_ready"], 1)
                    for i in range(8):
                        if slot == AD_SEG[i]:
                            dve.wait_ge(*upto("sege_ready", l, i + 1))
                            dve.tensor_tensor(four(seg_e), four(seg_e),
                                              cbm[:, i // 2].unsqueeze(1).broadcast_to([P, 4, P]), ALU.mult)\
                                .then_inc(sem["segm_ready"], 1)
                    for j in range(4):
                        if slot == AD_Y[j]:
                            t, g = divmod(j, SG)
                            dve.wait_ge(*upto("yd_mm", l, 2 * j + 2))
                            ysg = ys[:, t, g * CB:(g + 1) * CB]
                            dve.tensor_tensor(ysg, ysg, M[3 * g][:], ALU.add).then_inc(sem["y_added"], 1)
                            if t:
                                dve.wait_ge(*upto("yoff_mm", l, g + 1))
                                dve.tensor_tensor(wk[:, 2 + g].rearrange("p (h n) -> p h n", n=SP_),
                                                  M[2 - g][:].rearrange("p (h n) -> p h n", n=SP_),
                                                  per_head(decay[:, 1], g), ALU.mult).then_inc(sem["yoff_mul"], 1)
                                dve.wait_ge(*upto("yoff_mul", l, g + 1))
                                dve.wait_ge(*upto("y_added", l, j + 1))
                                dve.tensor_tensor(ysg, ysg, wk[:, 2 + g], ALU.add).then_inc(sem["yoff_added"], 1)
                    for r in range(8):
                        if slot == AD_ROPE[r]:
                            dve.stream_shuffle(rope_t, qk[0:ROPE, 2 * r:2 * r + 2],
                                               [(i + HALF) % ROPE for i in range(ROPE)])\
                                .then_inc(sem["rope_swapped"], 1)
                            dve.wait_ge(*upto("rope_swapped", l, r + 1))
                            dve.tensor_tensor(rope_t, rope_t,
                                              sinT[:].unsqueeze(1).broadcast_to([ROPE, 2, SEQ]), ALU.mult)\
                                .then_inc(sem["rope_mul"], 1)
                        if slot == AD_ROPE[r] + 1:
                            dve.wait_ge(*upto("rope_mul", l, r + 1))
                            dve.wait_ge(*upto("rope_cos", l, r + 1))
                            rot = qk[0:ROPE, 2 * r:2 * r + 2]
                            dve.tensor_tensor(rot, rot, rope_t, ALU.add).then_inc(sem["rope_ready"], 1)
                    for p in range(4):
                        if slot == AD_SOFT[p]:
                            dve.wait_ge(*upto("score_mm", l, p + 1))
                            mxv = mx[:].rearrange("p (h t) -> p h t", t=TT)
                            link(dve.tensor_reduce(mxv[:, :, 1], two(M[0][:]), AX.X, ALU.max))
                            link(dve.tensor_reduce(mxv[:, :, 0], two(M[3][:, 0:2 * P]), AX.X, ALU.max))
                            dve.tensor_scalar(mx[:], mx[:], -(DH ** -0.5), None, ALU.mult)\
                                .then_inc(sem["nmax_ready"], 1)
                        if slot == AD_PT[p]:
                            dve.wait_ge(*upto("pt_mm", l, p + 1))
                            dve.tensor_copy(probsT[:, 3 * P:6 * P], M[3][:, 0:3 * P]).then_inc(sem["pt_v"], 1)
                            link(dve.reciprocal(rinv[:], rs[:]))
                        if slot == AD_O[p]:
                            dve.wait_ge(*upto("pv_mm", l, p + 1))
                            dve.tensor_tensor(four(ybuf[:, p * CB:(p + 1) * CB]), four(M[1][:]),
                                              rinv[:].unsqueeze(2).broadcast_to([P, 4, P]), ALU.mult)\
                                .then_inc(sem["attn_out"], 1)
                    if slot == AD_ATTN_NORM:
                        dve.wait_ge(*upto("squared", l, SQ_A))
                        dve.tensor_scalar(st[:, A_MS], ssq[:, 0], 1.0 / AW, EPS, ALU.mult, ALU.add)\
                            .then_inc(sem["attn_ms"], 1)
                    if slot == AD_ATTN_NORM + 1:
                        dve.wait_ge(*upto("attn_inv", l, 1))
                        for t in range(TT):
                            ins = dve.tensor_scalar(attn[:, :, t], attn[:, :, t], st[:, A_INV, t:t + 1], None,
                                                    ALU.mult)
                        ins.then_inc(sem["attn_ready"], 1)
                    for g in range(SG):
                        ms, inv = (S0_MS, S0_INV) if g == 0 else (S1_MS, S1_INV)
                        if slot == leaves(B_Z + g):
                            dve.wait_ge(*left(l, B_Z + g, 2))
                            dve.wait_ge(*upto("yoff_added", l, 2))
                            for t in range(TT):
                                ysg = ys[:, t, g * CB:(g + 1) * CB]
                                ins = dve.tensor_tensor(ysg, ysg, zs[:, t, g * CB:(g + 1) * CB], ALU.mult)
                            ins.then_inc(sem["gated"], 1)
                        if slot == leaves(B_Z + g) + 1:
                            dve.wait_ge(*upto("squared", l, SQ_S1 if g else SQ_S0))
                            dve.tensor_scalar(st[:, ms], ssq[:, 1 + g], 1.0 / CB, EPS, ALU.mult, ALU.add)\
                                .then_inc(sem["ssd_ms"], 1)
                        if slot == leaves(B_Z + g) + 2:
                            dve.wait_ge(*upto("ssd_inv", l, g + 1))
                            for t in range(TT):
                                ysg = ys[:, t, g * CB:(g + 1) * CB]
                                ins = dve.tensor_scalar(ysg, ysg, st[:, inv, t:t + 1], None, ALU.mult)
                            ins.then_inc(sem["ssd_ready"], 1)
                    for i in range(4):
                        if slot == leaves(B_OUT + i):
                            if i == 0:
                                dve.wait_ge(*upto("gain_landed", l, 16))
                            if i == 3:
                                y_mean(SQ_Y0)
                            for t in range(TT):
                                cols = slice(i * CB, (i + 1) * CB)
                                dve.wait_ge(*upto("squared", l, SQ_S1 + 2 * i + t + 1))
                                dve.tensor_tensor(y[:, t, cols], acc[(B_OUT + i) % 2][t][:], zg[:, cols], ALU.mult)\
                                    .then_inc(acc_free[(B_OUT + i) % 2], 1)
                    for j in range(4):
                        if slot == AD_SSDT[j]:
                            to_lo("ssdT", j + 1, 4 + j, SSDT_BANK[j], G_ATTN)
                        if slot == AD_ATTNT[j]:
                            to_lo("attnT", j + 1, j, ATTNT_BANK[j], G_ATTN)

                def up_pair(q, i):
                    for j in range(2):
                        b = l * NB + q * (2 * QB) + i * 2 + (B_MLP + j)
                        first = j == 0 and is_first(q, i)
                        for c in range(AHEAD, NC + AHEAD):
                            split = (lambda: split_lo(b, c)) if c < NC else (lambda: split_lo(b + 1, c - NC))
                            if first:
                                norm_turn(1, c, G_MLP, split)
                            else:
                                split()
                        if first:
                            dve.wait_ge(*upto("squared", l, SQ_X1))
                            link(dve.tensor_reduce(st[:, X_SUM], sq[:], AX.X, ALU.add))
                            link(dve.tensor_scalar(st[:, X_MS], st[:, X_SUM], 1.0 / D, EPS, ALU.mult, ALU.add))
                            link(dve.scalar_tensor_tensor(st[:, X_EPS], st[:, X_MS], EPS, st[:, X_MS],
                                                          ALU.mult, ALU.mult))
                            dve.wait_ge(*upto("x_ready", l, 16))
                            dve.memset(ybuf[:], 0.0).then_inc(sem["y_zero"], 1)
                        for k in range(2):
                            n = q * (2 * QB) + i * 4 + (2 * j + k)
                            dve.wait_ge(*left(l, B_MLP + j, k + 1, q * QB + i))
                            dve.tensor_tensor(wk[:, 2 + k], wk[:, k], wk[:, k], ALU.mult)\
                                .then_inc(sem["u_sq"], 1)
                            dve.wait_ge(*upto("u_sq", l, n + 3))
                            dve.wait_ge(*upto("u_hi_ready", l, n + 1))
                            k0 = i * 8 + (4 * j + 2 * k)
                            uh, ul = (a[:, k0:k0 + 2] if type(i) is int else a[:, bass.ds(k0, 2)]
                                      for a in (u_hi, u_lo))
                            dve.tensor_tensor(ul.rearrange("p k s -> p (k s)"), wk[:, 2 + k],
                                              uh.rearrange("p k s -> p (k s)").bitcast(F32),
                                              ALU.subtract).then_inc(sem["u_ready"], 1)

                def down_pair(q, i):
                    for j in range(2):
                        b = l * NB + q * (2 * QB) + i * 2 + (B_MLP + QB + j)
                        for c in range(AHEAD, NC):
                            split_lo(b, c)
                        for c in range(AHEAD):
                            split_lo(b + 1, c)
                        dve.wait_ge(sem["mm_done"], RING + chunk(b + 1, 0))
                        last = type(q) is int
                        n = 2 * i + j
                        if not last:
                            dve.wait_ge(*upto("y_zero", l, 1))
                        for t in range(TT):
                            yp = y[:, t, n * CB:(n + 1) * CB] if last else \
                                y[:, t, bass.ds(i * (2 * CB) + j * CB, CB)]
                            dve.tensor_tensor(yp, yp, acc[1 - j][t][:], ALU.add).then_inc(acc_free[1 - j], 1)
                        if last:
                            if n == 0:
                                dve.wait_ge(*upto("gain_landed", l, 32))
                            if n == QB - 1:
                                y_mean(SQ_Y1)
                            for t in range(TT):
                                dve.wait_ge(*upto("squared", l, SQ_X1 + 2 * n + t + 1))
                                yp = y[:, t, n * CB:(n + 1) * CB]
                                dve.tensor_tensor(yp, yp, zg[:, n * CB:(n + 1) * CB], ALU.mult)\
                                    .then_inc(sem["y_gained"], 1)

                up_pair(0, 0)
                up_pair(0, 1)
                with dve.Fori(0, QUARTERS - 1) as q:
                    with dve.Fori(0, QB // 2) as i:
                        down_pair(q, i)
                    with dve.Fori(0, QB // 2) as i:
                        up_pair(q + 1, i)
                down_pair(QUARTERS - 1, 0)
                down_pair(QUARTERS - 1, 1)
                for c in range(4):
                    update_x(1, c)
                assert links[0] == DVE_LINKS, links[0]


_INS = ["x", "positions", "pre_mix_norm", "post_mix_norm", "pre_mlp_norm", "post_mlp_norm", "w_in", "conv_w",
        "conv_b", "dt_bias", "a_log", "d_skip", "attn_out_norm", "ssd_out_norm", "w_out", "w_up", "w_down"]


def kernel(**inputs):
    import concourse.bacc as bacc
    from concourse.bass_utils import run_bass_kernel_spmd

    nc = bacc.Bacc("TRN2", target_bir_lowering=False, num_devices=1)
    arrays, args = {}, []
    for name in _INS:
        a = np.ascontiguousarray(inputs[name])
        arrays[f"in_{name}"] = a
        args.append(nc.dram_tensor(f"in_{name}", a.shape, mybir.dt.from_np(a.dtype), kind="ExternalInput").ap())
    args.append(nc.dram_tensor("out_0", (1, SEQ, D), F32, kind="ExternalOutput").ap())
    trunk(nc, *args)
    r = run_bass_kernel_spmd(nc, [arrays], core_ids=[0])
    return r.results[0]["out_0"]
```

```python
from contextlib import ExitStack

import numpy as np

import concourse.bass as bass
from concourse import mybir

ALU = mybir.AluOpType
ACT = mybir.ActivationFunctionType
AX = mybir.AxisListType
F32 = mybir.dt.float32
F32R = mybir.dt.float32r
I32 = mybir.dt.int32
BF16 = mybir.dt.bfloat16

P = 128
DEPTH, D, SEQ, DFF = 2, 2048, 256, 8192
TT = SEQ // P
KT = D // P
HEADS, DH, ROPE, THETA = 8, 128, 32, 500000.0
HALF = ROPE // 2
AW = HEADS * DH
SH, SP_, SG, SN, TAPS = 16, 64, 2, 128, 4
SW = SH * SP_
CONV = SW + 2 * SG * SN
EPS = 1e-6
NEG = -3e38

RING = 4
CK = 2
CB = 512
NC = KT // CK
W = CK * CB
WARM = 12
AHEAD = 3

B_XBC, B_Q, B_K, B_V, B_Z, B_OUT, B_MLP = 0, 3, 5, 7, 9, 11, 15
QUARTERS = 4
QB = DFF // QUARTERS // CB
NB = B_MLP + QUARTERS * 2 * QB
MIX_SLOTS = B_MLP * NC

COL_Q, COL_K, COL_V, COL_Z, COL_XBC = 0, AW, 2 * AW, 3 * AW, 3 * AW + SW
COL_DT = COL_XBC + CONV

NCT = CONV // P
G_MIX, G_MLP, G_ATTN, G_SSD = 0, KT, 2 * KT, 2 * KT + AW // P
G_TAP = G_SSD + SW // P
G_BIAS = G_TAP + TAPS * NCT
NPRM = G_BIAS + NCT

PE_DT, PE_DT_TURN, PE_DECAY, PE_XTOK, PE_CB, PE_STATE = 7, 10, 17, 20, 28, 31
PE_SEG = [34 + 2 * i for i in range(8)]
PE_YD = [36 + 2 * i for i in range(8)]
PE_YOFF = [46, 50]
PE_SCORE = [59 + 5 * p for p in range(4)]
PE_PT = [s + 3 for s in PE_SCORE]
PE_PV = [s + 6 for s in PE_SCORE]
PE_ATTNT = [84, 85, 86, 87]
PE_SSDT = [83, 85, 90, 91]
AD_DIAG, AD_DTT, AD_DT, AD_DECAY, AD_XTOK, AD_XDT, AD_CB, AD_STATE = 8, 11, 14, 21, 24, 30, 32, 35
AD_SEG = [38 + 2 * i for i in range(8)]
AD_Y = [42 + 4 * j for j in range(4)]
AD_ROPE = [37, 39, 45, 47, 53, 55, 60, 62]
AD_SOFT = [s + 4 for s in PE_SCORE]
AD_PT = [s + 7 for s in PE_SCORE]
AD_O = [s + 10 for s in PE_SCORE]
AD_ATTN_NORM = 85
AD_ATTNT = [88, 89, 90, 91]
AD_SSDT = [87, 89, 94, 95]
ATTNT_BANK, SSDT_BANK = [0, 1, 3, 0], [2, 2, 2, 3]

X_SUM, X_MS, X_INV, X_EPS, Y_SUM, Y_MS, Y_INV, A_MS, A_INV, S0_MS, S0_INV, S1_MS, S1_INV = range(13)
NST = 13
DT_IN, DT_ABS, DT_EXP, DT_TMP, DT_S, DT_S2, DT, A_DT = range(8)

SQ_X0, SQ_S0, SQ_A, SQ_S1, SQ_Y0, SQ_X1 = 8, 10, 12, 14, 22, 30
SQ_Y1 = SQ_X1 + TT * QB
DVE_LINKS = 38


NORM_PE = {0: (2, 3), 1: (4,), 2: (5,), 3: (6,), 4: (7,)}
NORM_BEFORE = {AHEAD: (0, 1), AHEAD + 1: (2, 3)}
NORM_BEHIND = {AHEAD + 2: (4,), AHEAD + 3: (5,), AHEAD + 4: (6,), AHEAD + 5: (7,)}


def is_first(q, i):
    return type(q) is int and type(i) is int and q == 0 and i == 0


def leaves(b):
    return NC * (b + 1) + AHEAD - 1


def trunk(nc, x, positions, pre_mix_norm, post_mix_norm, pre_mlp_norm, post_mlp_norm, w_in, conv_w,
          conv_b, dt_bias, a_log, d_skip, attn_out_norm, ssd_out_norm, w_out, w_up, w_down, out):
    ctx = ExitStack()
    with ctx:
        def sb(name, shape, dt=F32):
            return ctx.enter_context(nc.sbuf_tensor(name, shape, dt))

        raw = sb("raw", [P, RING, W])
        w_hi = sb("w_hi", [P, RING, W], F32R)
        w_lo = sb("w_lo", [P, RING, W], F32R)
        x_sb = sb("x_sb", [P, TT, D])
        a_hi = sb("a_hi", [P, KT, SEQ], F32R)
        a_lo = sb("a_lo", [P, KT, SEQ], F32R)
        u_hi = sb("u_hi", [P, KT, SEQ], F32R)
        u_lo = sb("u_lo", [P, KT, SEQ], F32R)
        ybuf = sb("ybuf", [P, TT * D])
        xbcT = sb("xbcT", [P, NCT, SEQ])
        x_tok = sb("x_tok", [P, TT, SW])
        v_tok = sb("v_tok", [P, TT, AW])
        zg = sb("zg", [P, D])
        b_tok = sb("b_tok", [P, SG, SN])
        convr = sb("convr", [P, 2, 2, TAPS - 1 + SEQ])
        wk = sb("wk", [P, 4, CB])
        cbm = sb("cbm", [P, TT * SG, P])
        wdt_both = sb("wdt_both", [P, 2 * KT * SH + P - 2 * SH], F32R)
        ident = sb("ident", [P, P])
        tri = sb("tri", [P, P])
        low = sb("low", [P, P], F32R)
        cmask = sb("cmask", [P, P], BF16)
        ident_b = sb("ident_b", [P, P], BF16)
        ones = sb("ones", [P, P])
        cosT = sb("cosT", [ROPE, SEQ])
        sinT = sb("sinT", [ROPE, SEQ])
        inv_row = sb("inv_row", [P, SEQ])
        prm = sb("prm", [P, NPRM])
        prm_next = sb("prm_next", [P, DEPTH, NPRM])
        row = sb("row", [P, 3, SH])
        row_all = sb("row_all", [P, DEPTH + 1, 3, SH])
        minus_half = sb("minus_half", [P, 2])
        freq = sb("freq", [ROPE, 2])
        sq = sb("sq", [P, TT, 4])
        ysq = sb("ysq", [P, TT, 4])
        st = sb("st", [P, NST, TT])
        dts = sb("dts", [P, 8, TT, SH])
        adt_hi = sb("adt_hi", [P, TT, SH], F32R)
        adt_lo = sb("adt_lo", [P, TT, SH], F32R)
        decay = sb("decay", [P, 2, SH])
        mx = sb("mx", [P, 4])
        rs = sb("rs", [P, 4])
        rinv = sb("rinv", [P, 4])
        ssq = sb("ssq", [P, 3, TT])

        acc = [[ctx.enter_context(nc.psum_tensor(f"acc{i}{j}", [P, CB], F32)) for j in range(2)]
               for i in range(2)]
        M = [ctx.enter_context(nc.psum_tensor(f"M{i}", [P, CB], F32)) for i in range(4)]

        qk = ybuf[:, :].rearrange("p (h s) -> p h s", s=SEQ)
        attn = ybuf[:, 0:TT * AW].rearrange("p (h t d) -> p h t d", t=TT, d=DH)
        y = ybuf[:, :].rearrange("p (t n) -> p t n", t=TT)
        ys = xbcT[:, 0:SW // P, :].rearrange("p a s -> p (a s)").rearrange("p (t n) -> p t n", t=TT)
        zs = zg[:, :].rearrange("p (t n) -> p t n", t=TT)
        rope_t = convr[0:ROPE, 0, :, TAPS - 1:]
        wdt = wk[:, 3, 0:KT * SH].rearrange("p (k n) -> p k n", n=SH)
        dtT = wk[:, 0, 0:SEQ]
        wdt_parts = wdt_both[:, 0:2 * KT * SH].rearrange("p (k a n) -> p k a n", a=2, n=SH)
        wdt_hi, wdt_lo = wdt_parts[:, :, 0], wdt_parts[:, :, 1]
        tab = x_tok[0:ROPE, :, :].rearrange("p t n -> p (t n)")
        tab_f, tab_m = tab[:, 0:HALF], tab[:, HALF:ROPE]
        tab_pos, tab_angle, tab_turn, tab_sin = (tab[:, i * SEQ:(i + 1) * SEQ] for i in range(1, 5))
        seg_hi = [u_hi[:, 2 * i:2 * i + 2].rearrange("p k s -> p (k s)") for i in range(2)]
        seg_lo = [u_lo[:, 2 * i:2 * i + 2].rearrange("p k s -> p (k s)") for i in range(2)]
        seg_e = wk[:, 1]
        tab_first, tab_last = x_tok[0:ROPE, 1, 2 * CB - 4:2 * CB], x_tok[0:ROPE, 1, 2 * CB - 8:2 * CB - 4]
        low_w, cmask_w, wdt_w = v_tok[:, 0, 0:P], v_tok[:, 0, P:2 * P], v_tok[:, 0, 2 * P:3 * P - 2 * SH]
        probs = wk[:, 0:2].rearrange("p a n -> p (a n)")
        probsT = wk[:, 2:4].rearrange("p a n -> p (a n)")
        diag = wk[:, 1, 0:SEQ].rearrange("p (t n) -> p t n", t=TT)
        junk = cbm[:, :, :].rearrange("p a n -> p (a n)")

        up_banks = 2 * QB * QUARTERS
        per = dict(
            hi_ready=NB * NC,
            split_done=NB * NC,
            mm_done=NB * NC,
            x_ready=16,
            xT_mm=16, xT_hi=16, xT_ready=16,
            x_ms=1, x_inv=1,
            diag_ready=1, diag_mm=1, inv_row_ready=1,
            prm_ready=1, wdt_landed=16, wdt_hi_ready=1, wdt_ready=1,
            dt_mm=1, dtT_ready=1, dt_turned=1, dt_abs=1, dt_exp=1, row_exp=1, adt_hi_ready=1, adt_ready=1,
            decay_mm=1, decay_ready=1,
            conv_step=48, silu_ready=3,
            xtok_mm=4, xtok_ready=4, skip_done=4, xdt_ready=4, xdd_ready=2,
            btok_mm=1, btok_ready=1, cb_mm=1, cbm_ready=1, state_mm=1, state_ready=1,
            sega_hi=8, sega_ready=8, seg_mm=8, sege_ready=8, segm_ready=8, yd_mm=8, yoff_mm=2,
            y_added=4, yoff_mul=2, yoff_added=2,
            rope_swapped=8, rope_mul=8, rope_cos=8, rope_ready=8,
            score_mm=4, nmax_ready=4, probs_ready=4, pt_mm=4, pt_a=4, pt_v=4, pv_mm=4, attn_out=4,
            attn_ms=1, attn_inv=1, attn_ready=1, attnT_mm=4, attnT_hi=4, attnT_ready=4,
            gated=2, ssd_ms=2, ssd_inv=2, ssd_ready=2, ssdT_mm=4, ssdT_hi=4, ssdT_ready=4,
            squared=SQ_Y1,
            gain_landed=32, y_ms=2, y_inv=2, y_gained=8, y_zero=4,
            tile_done=2,
            u_hi_ready=up_banks,
            u_sq=up_banks,
            u_ready=up_banks,
            dve_chain=DVE_LINKS,
        )
        sem = {n: ctx.enter_context(nc.semaphore(n)) for n in per}
        raw_landed = [ctx.enter_context(nc.semaphore(f"raw_landed{s}")) for s in range(RING)]
        acc_free = [ctx.enter_context(nc.semaphore(f"acc_free{i}")) for i in range(2)]
        names = ["const_step", "const_ready", "ident_ready", "prm_landed", "out_norms_landed", "row_landed",
                 "row_ready", "pos_landed", "table_step", "table_angle", "table_sin", "table_ready", "prm_mm",
                 "prm_copied", "out_landed"]
        x_landed = [ctx.enter_context(nc.semaphore(f"x_landed{c}")) for c in range(4)]
        once = {n: ctx.enter_context(nc.semaphore(n)) for n in names}

        def upto(name, l, n):
            return sem[name], l * per[name] + n

        def chunk(b, c):
            return b * NC + c

        def through(l, b):
            return sem["mm_done"], RING + chunk(l * NB + b + 1, 0)

        def left(l, b, n, pairs=0):
            return acc_free[b % 2], 2 * (l * ((NB + 1 - b % 2) // 2) + b // 2 + pairs) + 2 + n

        def heads8(a, t, g):
            return a[:, t, g * CB:(g + 1) * CB].rearrange("p (h n) -> p h n", h=SH // SG)

        def per_head(a, g):
            n = SH // SG
            return a[:, g * n:(g + 1) * n].unsqueeze(2).broadcast_to([P, n, SP_])

        def four(a):
            return a.rearrange("p (h n) -> p h n", h=4)

        block = ctx.enter_context(nc.Block())

        def load_x(engine, c):
            engine.dma_start(x_sb[:, :, c * CB:(c + 1) * CB],
                             x[0, :, c * CB:(c + 1) * CB].rearrange("(t p) n -> p t n", p=P))\
                .then_inc(x_landed[c], 16)

        def load_parameters(engine, landed, r0, n, a):
            engine.dma_start(probs[r0:r0 + n, 0:DEPTH * P].rearrange("r (l n) -> r l n", n=P),
                             a.rearrange("l (r n) -> r l n", n=P)).then_inc(once[landed], 16)

        @block.sync
        def _(sp):
            def load(b, c, src):
                sp.wait_ge(sem["split_done"], chunk(b, c) + 1)
                sp.dma_start(raw[:, c % RING].rearrange("p (k n) -> p k n", k=CK),
                             src.rearrange("(k p) n -> p k n", p=P)).then_inc(raw_landed[c % RING], 16)

            def load_block(b, w, l, r0, c0):
                for c in range(NC):
                    load(b, c, w[l, bass.ds(r0 + c * CK * P, CK * P), bass.ds(c0, CB)])

            load_parameters(sp, "prm_landed", G_TAP, TAPS * NCT, conv_w.rearrange("l k n -> l (k n)"))
            load_parameters(sp, "prm_landed", G_BIAS, NCT, conv_b)
            with sp.Fori(0, DEPTH) as l:
                for b0, n, c0 in ((B_XBC, B_Q - B_XBC, COL_XBC), (B_Q, B_OUT - B_Q, COL_Q)):
                    with sp.Fori(0, n) as i:
                        load_block(l * NB + b0 + i, w_in, l, 0, i * CB + c0)
                with sp.Fori(0, B_MLP - B_OUT) as i:
                    load_block(l * NB + B_OUT + i, w_out, l, 0, i * CB)
                with sp.Fori(0, QUARTERS) as q:
                    with sp.Fori(0, QB) as i:
                        load_block(l * NB + q * (2 * QB) + i + B_MLP, w_up, l, 0, q * (QB * CB) + i * CB)
                    with sp.Fori(0, QB) as i:
                        load_block(l * NB + q * (2 * QB) + i + (B_MLP + QB), w_down, l, q * (QB * CB), i * CB)
            for c in range(AHEAD):
                load(DEPTH * NB, c, w_in[0, c * CK * P:(c + 1) * CK * P, COL_XBC:COL_XBC + CB])
            for c in range(4):
                for t in range(TT):
                    sp.wait_ge(*upto("x_ready", DEPTH, 2 * c + t + 1))
                    sp.dma_start(out[0, t * P:(t + 1) * P, c * CB:(c + 1) * CB],
                                 x_sb[:, t, c * CB:(c + 1) * CB]).then_inc(once["out_landed"], 16)
            for s in range(RING):
                sp.wait_ge(raw_landed[s], 16 * (2 * DEPTH * NB + (1 if s < AHEAD else 0)))
            sp.wait_ge(once["out_landed"], 16 * 4 * TT)

        @block.gpsimd
        def _(pool):
            step, ready = once["const_step"], once["const_ready"]
            pool.memset(ident[:], 0.0).then_inc(step, 1)
            pool.memset(sq[:], 0.0).then_inc(sem["mm_done"], RING)
            pool.memset(ysq[:], 0.0).then_inc(acc_free[0], 2)
            pool.memset(minus_half[:], -0.5).then_inc(acc_free[1], 2)
            pool.wait_ge(step, 1)
            pool.affine_select(out=ident[:], in_=ident[:], compare_op=ALU.not_equal, fill=1.0, base=0,
                               pattern=[[-1, P]], channel_multiplier=1).then_inc(once["ident_ready"], 1)
            load_parameters(pool, "out_norms_landed", G_ATTN, AW // P, attn_out_norm)
            load_parameters(pool, "out_norms_landed", G_SSD, SW // P, ssd_out_norm)

            def relay_x(c):
                pool.wait_ge(x_landed[c], 16)
                pool.memset(rinv[:, c:c + 1], 0.0).then_inc(sem["x_ready"], 2)

            pool.memset(tri[:], 1.0).then_inc(step, 1)
            pool.memset(low_w, 1.0).then_inc(step, 1)
            pool.memset(cmask_w, 0.0).then_inc(step, 1)
            pool.memset(wdt_w, 0.0).then_inc(step, 1)
            pool.memset(ones[:], 1.0).then_inc(ready, 1)
            pool.memset(convr[:, :, :, 0:TAPS - 1], 0.0).then_inc(ready, 1)
            pool.wait_ge(step, 5)
            pool.affine_select(out=tri[:], in_=tri[:], compare_op=ALU.is_ge, fill=0.0, base=0,
                               pattern=[[1, P]], channel_multiplier=-1).then_inc(ready, 1)
            pool.affine_select(out=low_w, in_=low_w, compare_op=ALU.is_gt, fill=0.0, base=0,
                               pattern=[[-1, P]], channel_multiplier=1).then_inc(step, 1)
            pool.affine_select(out=cmask_w, in_=cmask_w, compare_op=ALU.is_ge, fill=NEG, base=0,
                               pattern=[[-1, P]], channel_multiplier=1).then_inc(step, 1)
            load_x(pool, 1)
            relay_x(0)
            for c in range(2, 4):
                load_x(pool, c)
            for c in range(1, 4):
                relay_x(c)
            for i, a in enumerate((dt_bias, a_log, d_skip)):
                pool.dma_start(row_all[:, 0:DEPTH, i], a.partition_broadcast(P)).then_inc(once["row_landed"], 16)
            pool.wait_ge(step, 7)
            pool.tensor_copy(ident_b[:], ident[:]).then_inc(ready, 1)
            pool.tensor_copy(low[:], low_w).then_inc(ready, 1)
            pool.tensor_copy(cmask[:], cmask_w).then_inc(ready, 1)
            pool.tensor_copy(wdt_both[:, 2 * KT * SH:], wdt_w).then_inc(ready, 1)
            pool.wait_ge(once["table_sin"], 2)
            pool.tensor_tensor(tab_turn, tab_sin, tab_sin, ALU.mult).then_inc(step, 1)
            pool.wait_ge(step, 8)
            pool.tensor_scalar(cosT[:], tab_turn, -2.0, 1.0, ALU.mult, ALU.add).then_inc(once["table_ready"], 1)
            pool.memset(row_all[:, DEPTH], 0.0).then_inc(once["row_ready"], 1)
            pool.wait_ge(once["row_landed"], 16 * 3)
            pool.tensor_copy(row[:], row_all[:, 0]).then_inc(once["row_ready"], 1)
            pool.wait_ge(once["row_ready"], 2)

            with pool.Fori(0, DEPTH) as l:
                def power(k_out, k_in, waited, w_n):
                    pool.wait_ge(*upto(waited, l, w_n))
                    return pool.tensor_tensor(st[:, k_out], st[:, k_in], minus_half[:], ALU.pow)

                pool.wait_ge(sem["mm_done"], RING + chunk(l * NB, 0))
                pool.dma_start(wdt, w_in[bass.ds(l, 1), :, COL_DT:COL_DT + SH]
                               .rearrange("a (k p) n -> p (a k) n", p=P)).then_inc(sem["wdt_landed"], 16)
                power(X_INV, X_MS, "x_ms", 1).then_inc(sem["x_inv"], 1)
                pool.wait_ge(*upto("xtok_ready", l, 4))
                for i in range(TT * SG):
                    t, g = divmod(i, SG)
                    pool.tensor_tensor(heads8(ys, t, g), heads8(x_tok, t, g), per_head(row[:, 2], g),
                                       ALU.mult).then_inc(sem["skip_done"], 1)

                def seg_weights(i):
                    t, g, hh = i // 4, i // 2 % 2, i % 2
                    h0 = g * 8 + hh * 4
                    if i >= 2:
                        pool.wait_ge(*upto("seg_mm", l, i - 1))
                    for dst, a, done in ((seg_hi, adt_hi, "sega_hi"), (seg_lo, adt_lo, "sega_ready")):
                        pool.tensor_tensor(four(dst[i % 2]), tri[:].unsqueeze(1).broadcast_to([P, 4, P]),
                                           a[:, t, h0:h0 + 4].bitcast(F32).unsqueeze(2)
                                           .broadcast_to([P, 4, P]), ALU.mult).then_inc(sem[done], 1)

                def rope_cos(r):
                    pool.wait_ge(*upto("rope_swapped", l, r + 1))
                    pool.wait_ge(once["table_ready"], 1)
                    pool.tensor_tensor(qk[0:ROPE, 2 * r:2 * r + 2], qk[0:ROPE, 2 * r:2 * r + 2],
                                       cosT[:].unsqueeze(1).broadcast_to([ROPE, 2, SEQ]),
                                       ALU.mult).then_inc(sem["rope_cos"], 1)

                for slot in range(PE_SEG[0] - 3, AD_ROPE[-1] + 1):
                    if slot + 3 in PE_SEG:
                        seg_weights(PE_SEG.index(slot + 3))
                    if slot + 2 in AD_ROPE:
                        rope_cos(AD_ROPE.index(slot + 2))
                power(S0_INV, S0_MS, "ssd_ms", 1).then_inc(sem["ssd_inv"], 1)
                power(A_INV, A_MS, "attn_ms", 1).then_inc(sem["attn_inv"], 1)
                power(S1_INV, S1_MS, "ssd_ms", 2).then_inc(sem["ssd_inv"], 1)
                power(Y_INV, Y_MS, "y_ms", 1).then_inc(sem["y_inv"], 1)
                pool.wait_ge(once["prm_copied"], DEPTH)
                pool.wait_ge(*upto("xT_ready", l, 16))
                rows = row_all[:].rearrange("p l i n -> p (l i n)")
                pool.tensor_copy(row[:].rearrange("p i n -> p (i n)"),
                                 rows[:, bass.ds(l * (3 * SH) + 3 * SH, 3 * SH)])
                pool.tensor_copy(prm[:], prm_next[:].rearrange("p l n -> p (l n)")[:, bass.ds(l * NPRM, NPRM)])\
                    .then_inc(sem["prm_ready"], 1)
                power(Y_INV, Y_MS, "y_ms", 2).then_inc(sem["y_inv"], 1)

        @block.scalar
        def _(act):
            act.dma_start(tab_pos.bitcast(I32), positions[0].partition_broadcast(ROPE))\
                .then_inc(once["pos_landed"], 16)
            load_parameters(act, "prm_landed", G_MIX, KT, pre_mix_norm)
            load_parameters(act, "prm_landed", G_MLP, KT, pre_mlp_norm)
            load_x(act, 0)
            act.wait_ge(sem["split_done"], RING)
            act.activation(tab_first, mx[0:ROPE, :], ACT.Sin).then_inc(once["table_sin"], 1)

            def round_hi(b, c):
                act.wait_ge(raw_landed[c % RING], (b * (NC // RING) + c // RING + 1) * 16)
                act.wait_ge(sem["mm_done"], chunk(b, c) + 1)
                act.activation(w_hi[:, c % RING], raw[:, c % RING], ACT.Copy).then_inc(sem["hi_ready"], 1)

            round_hi(0, 0)
            act.wait_ge(once["prm_mm"], DEPTH)
            act.activation(prm[:], M[2][:, 0:NPRM], ACT.Copy).then_inc(sem["prm_ready"], 1)
            round_hi(0, 1)
            act.wait_ge(once["table_angle"], 1)
            act.activation(sinT[:], tab_angle, ACT.Sin, scale=freq[:, 1:2])
            act.activation(tab_sin, tab_angle, ACT.Sin, scale=0.5).then_inc(once["table_sin"], 1)
            act.activation(tab_last, mx[0:ROPE, :], ACT.Silu)
            round_hi(0, 2)
            with act.Fori(0, DEPTH) as l:
                squares = [0]

                def square(in_, total, extra=0):
                    if squares[0] or extra:
                        act.wait_ge(*upto("squared", l, squares[0] + extra))
                    act.activation(junk, in_, ACT.Square, accum_out=total).then_inc(sem["squared"], 1)
                    squares[0] += 1

                def load_gain(gains):
                    act.dma_start(zg[:], gains[bass.ds(l, 1)].rearrange("a n -> (a n)").partition_broadcast(P))\
                        .then_inc(sem["gain_landed"], 16)

                def x_hi(n, j, gain):
                    act.wait_ge(*upto("xT_mm", l, 8 * n + j + 1))
                    for kk in range(2):
                        k = 2 * j + kk
                        ins = act.activation(a_hi[:, k], M[j % 4][:, kk * SEQ:(kk + 1) * SEQ], ACT.Copy,
                                             scale=prm[:, gain + k:gain + k + 1])
                    ins.then_inc(sem["xT_hi"], 1)

                def x_squares(n, c):
                    act.wait_ge(*upto("x_ready", l, 8 * n + 2 * c + 2))
                    for t in range(TT):
                        square(x_sb[:, t, c * CB:(c + 1) * CB], sq[:, t, c:c + 1])

                def norm_turn(n, slot, gain, split):
                    for j in NORM_BEFORE.get(slot, ()):
                        x_hi(n, j, gain)
                    split()
                    for j in NORM_BEHIND.get(slot, ()):
                        x_hi(n, j, gain)
                    if AHEAD <= slot < AHEAD + 4:
                        x_squares(n, slot - AHEAD)

                def to_hi(name, n, j, bank, gain):
                    act.wait_ge(*upto(name + "_mm", l, n))
                    for kk in range(2):
                        k = 2 * j + kk
                        ins = act.activation(u_hi[:, k], M[bank][:, kk * SEQ:(kk + 1) * SEQ], ACT.Copy,
                                             scale=prm[:, gain + k:gain + k + 1])
                    ins.then_inc(sem[name + "_hi"], 1)

                act.wait_ge(*upto("prm_ready", l, 1))
                for slot in range(AHEAD, MIX_SLOTS + AHEAD):
                    b, c = divmod(slot, NC)
                    norm_turn(0, slot, G_MIX, lambda: round_hi(l * NB + b, c))
                    if slot == AD_DIAG:
                        act.wait_ge(*upto("wdt_landed", l, 16))
                        act.activation(wdt_hi, wdt, ACT.Copy).then_inc(sem["wdt_hi_ready"], 1)
                    if slot == leaves(0):
                        act.wait_ge(*upto("diag_mm", l, 1))
                        act.activation(inv_row[:], M[0][:, 0:SEQ], ACT.Copy).then_inc(sem["inv_row_ready"], 1)
                    if slot == AD_DT:
                        act.wait_ge(*upto("dt_abs", l, 1))
                        act.activation(dts[:, DT_EXP], dts[:, DT_ABS], ACT.Exp, scale=-1.0)\
                            .then_inc(sem["dt_exp"], 1)
                        act.activation(row[:, 1], row[:, 1], ACT.Exp).then_inc(sem["row_exp"], 1)
                    if slot == AD_DECAY:
                        act.wait_ge(*upto("decay_mm", l, 1))
                        act.activation(decay[:].rearrange("p a n -> p (a n)"), M[0][:, 0:2 * SH], ACT.Exp)\
                            .then_inc(sem["decay_ready"], 1)
                    for i in range(3):
                        if slot == leaves(i) + 3:
                            act.wait_ge(*upto("conv_step", l, 16 * (i + 1)))
                            act.activation(xbcT[:, 4 * i:4 * i + 4], xbcT[:, 4 * i:4 * i + 4], ACT.Silu)\
                                .then_inc(sem["silu_ready"], 1)
                    for i in range(TT * SG):
                        if slot == AD_XTOK + i:
                            t, g = divmod(i, SG)
                            act.wait_ge(*upto("xtok_mm", l, i + 1))
                            act.activation(x_tok[:, t, g * CB:(g + 1) * CB], M[i][:], ACT.Copy)\
                                .then_inc(sem["xtok_ready"], 1)
                    if slot == AD_CB:
                        act.wait_ge(*upto("btok_mm", l, 1))
                        act.activation(b_tok[:].rearrange("p g n -> p (g n)"), M[0][:, 0:SG * SN], ACT.Copy)\
                            .then_inc(sem["btok_ready"], 1)
                    if slot == AD_STATE:
                        act.wait_ge(*upto("state_mm", l, 1))
                        act.activation(wk[:, 2], M[0][:], ACT.Copy)
                        act.activation(wk[:, 3], M[3][:], ACT.Copy).then_inc(sem["state_ready"], 1)
                    for i in range(8):
                        if slot == AD_SEG[i]:
                            act.wait_ge(*upto("seg_mm", l, i + 1))
                            if i:
                                act.wait_ge(*upto("yd_mm", l, i))
                            act.activation(seg_e, M[1][:], ACT.Exp).then_inc(sem["sege_ready"], 1)
                    for p in range(4):
                        if slot == AD_SOFT[p]:
                            act.wait_ge(*upto("nmax_ready", l, p + 1))
                            for hh in range(2):
                                o = hh * 3 * P
                                act.activation(probs[:, o:o + 2 * P], M[0][:, hh * 2 * P:(hh + 1) * 2 * P],
                                               ACT.Exp, bias=mx[:, 2 * hh + 1:2 * hh + 2], scale=DH ** -0.5,
                                               accum_out=rs[:, 2 * hh + 1:2 * hh + 2])
                                ins = act.activation(probs[:, o + 2 * P:o + 3 * P], M[3][:, hh * P:(hh + 1) * P],
                                                     ACT.Exp, bias=mx[:, 2 * hh:2 * hh + 1], scale=DH ** -0.5,
                                                     accum_out=rs[:, 2 * hh:2 * hh + 1])
                            ins.then_inc(sem["probs_ready"], 1)
                        if slot == AD_PT[p]:
                            act.wait_ge(*upto("pt_mm", l, p + 1))
                            act.activation(probsT[:, 0:3 * P], M[1][:, 0:3 * P], ACT.Copy).then_inc(sem["pt_a"], 1)
                    for i in range(2):
                        if slot == leaves(B_V + i):
                            act.wait_ge(*through(l, B_V + i))
                            for t in range(TT):
                                act.activation(v_tok[:, t, i * CB:(i + 1) * CB], acc[(B_V + i) % 2][t][:], ACT.Copy,
                                               scale=st[:, X_INV, t:t + 1]).then_inc(acc_free[(B_V + i) % 2], 1)
                    for g in range(SG):
                        if slot == leaves(B_Z + g):
                            act.wait_ge(*through(l, B_Z + g))
                            for t in range(TT):
                                act.activation(zs[:, t, g * CB:(g + 1) * CB], acc[(B_Z + g) % 2][t][:], ACT.Silu,
                                               scale=st[:, X_INV, t:t + 1]).then_inc(acc_free[(B_Z + g) % 2], 1)
                        if slot == leaves(B_Z + g) + 1:
                            act.wait_ge(*upto("gated", l, g + 1))
                            for t in range(TT):
                                square(ys[:, t, g * CB:(g + 1) * CB], ssq[:, 1 + g, t:t + 1])
                            if g == 1:
                                load_gain(post_mix_norm)
                    if slot == AD_ATTN_NORM:
                        act.wait_ge(*upto("attn_out", l, 4))
                        for t in range(TT):
                            act.wait_ge(*upto("squared", l, squares[0]))
                            act.activation(x_tok[:, t].rearrange("p (h d) -> p h d", d=DH), attn[:, :, t, :],
                                           ACT.Square, accum_out=ssq[:, 0, t:t + 1]).then_inc(sem["squared"], 1)
                            squares[0] += 1
                    for j in range(4):
                        if slot == AD_SSDT[j]:
                            to_hi("ssdT", j + 1, 4 + j, SSDT_BANK[j], G_ATTN)
                        if slot == AD_ATTNT[j]:
                            to_hi("attnT", j + 1, j, ATTNT_BANK[j], G_ATTN)
                    for i in range(4):
                        if slot == leaves(B_OUT + i):
                            for t in range(TT):
                                first = (i, t) == (3, 0)
                                act.wait_ge(*(upto("tile_done", l, 1) if first else through(l, B_OUT + i)))
                                a = acc[(B_OUT + i) % 2][t]
                                square(a[:], ysq[:, t, i:i + 1])
                def up_pair(q, i):
                    for j in range(2):
                        b = l * NB + q * (2 * QB) + i * 2 + (B_MLP + j)
                        first = j == 0 and is_first(q, i)
                        for c in range(AHEAD, NC + AHEAD):
                            split = (lambda: round_hi(b, c)) if c < NC else (lambda: round_hi(b + 1, c - NC))
                            if first:
                                norm_turn(1, c, G_MLP, split)
                            else:
                                split()
                        if first:
                            assert squares[0] == SQ_X1
                            act.wait_ge(*left(l, B_MLP - 1, 2))
                            load_gain(post_mlp_norm)
                        act.wait_ge(sem["mm_done"], RING + chunk(b + 1, 0))
                        for k in range(2):
                            n = q * (2 * QB) + i * 4 + (2 * j + k)
                            act.wait_ge(*upto("u_sq", l, n + 1))
                            act.activation(wk[:, k], acc[1 - j][k][:], ACT.Relu).then_inc(acc_free[1 - j], 1)
                            act.wait_ge(*left(l, B_MLP + j, k + 1, q * QB + i))
                            u = u_hi[:, 8 * i + 4 * j + 2 * k:8 * i + 4 * j + 2 * k + 2] if type(i) is int else \
                                u_hi[:, bass.ds(i * 8 + (4 * j + 2 * k), 2)]
                            act.activation(u.rearrange("p k s -> p (k s)"), wk[:, k], ACT.Square)\
                                .then_inc(sem["u_hi_ready"], 1)

                def down_pair(q, i):
                    for j in range(2):
                        b = l * NB + q * (2 * QB) + i * 2 + (B_MLP + QB + j)
                        for c in range(AHEAD, NC):
                            round_hi(b, c)
                        for c in range(AHEAD):
                            round_hi(b + 1, c)
                        if type(q) is not int:
                            continue
                        for t in range(TT):
                            act.wait_ge(*left(l, B_MLP + QB + j, t + 1, q * QB + i))
                            n = 2 * i + j
                            square(y[:, t, n * CB:(n + 1) * CB], ysq[:, t, n:n + 1])

                up_pair(0, 0)
                up_pair(0, 1)
                with act.Fori(0, QUARTERS - 1) as q:
                    with act.Fori(0, QB // 2) as i:
                        down_pair(q, i)
                    with act.Fori(0, QB // 2) as i:
                        up_pair(q + 1, i)
                down_pair(QUARTERS - 1, 0)
                down_pair(QUARTERS - 1, 1)
                assert squares[0] == SQ_Y1

        @block.tensor
        def _(pe):
            pe.wait_ge(once["ident_ready"], 1)
            pe.wait_ge(once["prm_landed"], 16 * 4)
            pe.wait_ge(once["out_norms_landed"], 16 * 2)
            for l in range(DEPTH):
                pe.transpose(M[2 + l][:, 0:NPRM], probs[0:NPRM, l * P:(l + 1) * P], ident[0:NPRM, 0:NPRM])\
                    .then_inc(once["prm_mm"], 1)

            def take(b, c):
                pe.wait_ge(sem["split_done"], RING + 1 + chunk(b, c))

            def token_chunk(c, par, s_hi, s_lo, tile_first=False):
                for i in range(CK * TT):
                    kk, t = (i % CK, i // CK) if tile_first else (i // TT, i % TT)
                    k = c * CK + kk
                    wh, wl = (w[:, c % RING, kk * CB:(kk + 1) * CB] for w in (w_hi, w_lo))
                    o = acc[par][t][:]
                    sh, sl = (s[:, k, t * P:(t + 1) * P] for s in (s_hi, s_lo))
                    pe.matmul(o, sh, wh, start=(k == 0), stop=False)
                    pe.matmul(o, sh, wl, start=False, stop=False)
                    ins = pe.matmul(o, sl, wh, start=False, stop=(k == KT - 1))
                    if tile_first and i == CK - 1:
                        ins.then_inc(sem["tile_done"], 1)
                ins.then_inc(sem["mm_done"], 1)

            def feature_chunk(c, par, lo_ready=None):
                def o(m):
                    return acc[par][m // 2][:, m % 2 * SEQ:(m % 2 + 1) * SEQ]

                def w(a, kk, m):
                    return a[:, c % RING, kk * CB + m * P:kk * CB + (m + 1) * P]

                if lo_ready:
                    for kk in range(CK):
                        k = c * CK + kk
                        for m in range(CB // P):
                            pe.matmul(o(m), w(w_hi, kk, m), a_hi[:, k], start=(k == 0 and m % 2 == 0), stop=False,
                                      skip_group_check=True)
                            pe.matmul(o(m), w(w_lo, kk, m), a_hi[:, k], start=False, stop=False,
                                      skip_group_check=True)
                    pe.wait_ge(*lo_ready)
                    for kk in range(CK):
                        for m in range(CB // P):
                            ins = pe.matmul(o(m), w(w_hi, kk, m), a_lo[:, c * CK + kk], start=False, stop=False,
                                            skip_group_check=True)
                    ins.then_inc(sem["mm_done"], 1)
                    return
                for kk in range(CK):
                    k = c * CK + kk
                    for m in range(CB // P):
                        pe.matmul(o(m), w(w_hi, kk, m), a_hi[:, k], start=(k == 0 and m % 2 == 0), stop=False,
                                  skip_group_check=True)
                        pe.matmul(o(m), w(w_hi, kk, m), a_lo[:, k], start=False, stop=False, skip_group_check=True)
                        ins = pe.matmul(o(m), w(w_lo, kk, m), a_hi[:, k], start=False, stop=(k == KT - 1),
                                        skip_group_check=True)
                ins.then_inc(sem["mm_done"], 1)

            with pe.Fori(0, DEPTH) as l:
                def x_turn(n, j):
                    if j % 2 == 0:
                        pe.wait_ge(*upto("x_ready", l, 8 * n + j + 2))
                    if j >= 4:
                        pe.wait_ge(*upto("xT_ready", l, 8 * n + j - 3))
                    for kk in range(2):
                        for t in range(TT):
                            k = 2 * j + kk
                            ins = pe.transpose(M[j % 4][:, kk * SEQ + t * P:kk * SEQ + (t + 1) * P],
                                               x_sb[:, t, k * P:(k + 1) * P], ident[:])
                    ins.then_inc(sem["xT_mm"], 1)

                def inv_row_and_dt():
                    pe.wait_ge(once["const_ready"], 7)
                    pe.wait_ge(*upto("diag_ready", l, 1))
                    for t in range(TT):
                        ins = pe.matmul(M[0][:, t * P:(t + 1) * P], ones[:], diag[:, t], start=True, stop=True)
                    ins.then_inc(sem["diag_mm"], 1)
                    pe.wait_ge(*upto("wdt_ready", l, 1))
                    o = M[1][:, 0:SEQ]
                    for k in range(KT):
                        w = wdt_both[:, k * 2 * SH:k * 2 * SH + P]
                        pe.matmul(o, w, a_hi[:, k], start=(k == 0), stop=False)
                        ins = pe.matmul(o, w, a_lo[:, k], start=False, stop=(k == KT - 1))
                    ins.then_inc(sem["dt_mm"], 1)

                def dt_turn():
                    pe.wait_ge(*upto("dtT_ready", l, 1))
                    for t in range(TT):
                        ins = pe.transpose(M[1][:, t * P:(t + 1) * P], dtT[:, t * P:(t + 1) * P], ident[:])
                    ins.then_inc(sem["dt_turned"], 1)

                def decays():
                    pe.wait_ge(*upto("adt_ready", l, 1))
                    pe.wait_ge(*upto("inv_row_ready", l, 1))
                    pe.matmul(M[0][:, 0:SH], low[:].bitcast(F32), dts[:, A_DT, 0], start=True, stop=True)
                    pe.matmul(M[0][:, SH:2 * SH], tri[:], dts[:, A_DT, 1], start=True, stop=True)\
                        .then_inc(sem["decay_mm"], 1)

                def x_tokens(i):
                    t, g = divmod(i, SG)
                    pe.wait_ge(*upto("silu_ready", l, g + 1))
                    pe.wait_ge(*upto("decay_ready", l, 1))
                    for k in range(4):
                        ins = pe.transpose(M[i][:, k * P:(k + 1) * P], xbcT[:, 4 * g + k, t * P:(t + 1) * P],
                                           ident[:])
                    ins.then_inc(sem["xtok_mm"], 1)

                def b_tokens_and_cb():
                    pe.wait_ge(*upto("silu_ready", l, 3))
                    pe.wait_ge(*upto("xtok_ready", l, 4))
                    nx = SW // P
                    for g in range(SG):
                        ins = pe.transpose(M[0][:, g * P:(g + 1) * P], xbcT[:, nx + g, 0:P], ident[:])
                    ins.then_inc(sem["btok_mm"], 1)
                    for t in range(TT):
                        for g in range(SG):
                            i = t * SG + g
                            ins = pe.matmul(M[1][:, i * P:(i + 1) * P], xbcT[:, nx + g, t * P:(t + 1) * P],
                                            xbcT[:, nx + SG + g, t * P:(t + 1) * P], start=True, stop=True)
                    ins.then_inc(sem["cb_mm"], 1)

                def states():
                    pe.wait_ge(*upto("btok_ready", l, 1))
                    pe.wait_ge(*upto("xdd_ready", l, 2))
                    for g in range(SG):
                        ins = pe.matmul(M[3 * g][:], b_tok[:, g], wk[:, 2 + g], start=True, stop=True)
                    ins.then_inc(sem["state_mm"], 1)

                def segment_sums(i):
                    pe.wait_ge(*upto("sega_ready", l, i + 1))
                    if i:
                        pe.wait_ge(*upto("sege_ready", l, i))
                    else:
                        pe.wait_ge(*upto("cbm_ready", l, 1))
                    pe.matmul(M[1][:], low[:], seg_hi[i % 2], start=True, stop=False)
                    pe.matmul(M[1][:], low[:], seg_lo[i % 2], start=False, stop=True).then_inc(sem["seg_mm"], 1)

                def y_diagonal(i):
                    t, g, hh = i // 4, i // 2 % 2, i % 2
                    pe.wait_ge(*upto("segm_ready", l, i + 1))
                    if i == 0:
                        pe.wait_ge(*upto("state_ready", l, 1))
                        pe.wait_ge(*upto("xdt_ready", l, 4))
                    if i in (4, 6):
                        pe.wait_ge(*upto("y_added", l, i // 2 - 1))
                    for h in range(4):
                        o = (hh * 4 + h) * SP_
                        ins = pe.matmul(M[3 * g][:, o:o + SP_], seg_e[:, h * P:(h + 1) * P],
                                        x_tok[:, t, g * CB + o:g * CB + o + SP_], start=True, stop=True)
                    ins.then_inc(sem["yd_mm"], 1)

                def y_offset(g):
                    if g == 1:
                        pe.wait_ge(*upto("sege_ready", l, 8))
                    pe.matmul(M[2 - g][:], xbcT[:, SW // P + SG + g, P:2 * P], wk[:, 2 + g], start=True,
                              stop=True).then_inc(sem["yoff_mm"], 1)

                def scores(p):
                    pe.wait_ge(*upto("rope_ready", l, 4 + p + 1))
                    if p == 0:
                        pe.wait_ge(*upto("y_added", l, 4))
                    else:
                        pe.wait_ge(*upto("pt_v", l, p))
                    for hh in range(2):
                        h = 2 * p + hh
                        o = M[0][:, hh * SEQ:(hh + 1) * SEQ]
                        pe.matmul(o, qk[:, h, P:SEQ], qk[:, HEADS + h], start=(hh == 0), stop=False,
                                  skip_group_check=True)
                        pe.matmul(o[:, P:SEQ], ident_b[:], cmask[:], start=False, stop=True,
                                  skip_group_check=True)
                    for hh in range(2):
                        h = 2 * p + hh
                        o = M[3][:, hh * P:(hh + 1) * P]
                        pe.matmul(o, qk[:, h, 0:P], qk[:, HEADS + h, 0:P], start=(hh == 0), stop=False,
                                  skip_group_check=True)
                        ins = pe.matmul(o, ident_b[:], cmask[:], start=False, stop=True, skip_group_check=True)
                    ins.then_inc(sem["score_mm"], 1)

                def probs_turn(p):
                    pe.wait_ge(*upto("probs_ready", l, p + 1))
                    if p == 0:
                        pe.wait_ge(*upto("yoff_mul", l, 2))
                    else:
                        pe.wait_ge(*upto("attn_out", l, p))
                    for hh in range(2):
                        for i in range(3):
                            ins = pe.transpose(M[1 + 2 * hh][:, i * P:(i + 1) * P],
                                               probs[:, (3 * hh + i) * P:(3 * hh + i + 1) * P], ident[:])
                    ins.then_inc(sem["pt_mm"], 1)

                def values(p):
                    pe.wait_ge(*upto("pt_a", l, p + 1))
                    pe.wait_ge(*upto("pt_v", l, p + 1))
                    pe.wait_ge(*left(l, B_V + p // 2, 2))
                    for hh in range(2):
                        h = 2 * p + hh
                        v0, v1 = (v_tok[:, t, h * DH:(h + 1) * DH] for t in range(TT))
                        a10, a11, a00 = (probsT[:, (3 * hh + i) * P:(3 * hh + i + 1) * P] for i in range(3))
                        o = M[1][:, 2 * hh * P:(2 * hh + 1) * P]
                        pe.matmul(o, a00, v0, start=True, stop=True)
                        o = M[1][:, (2 * hh + 1) * P:(2 * hh + 2) * P]
                        pe.matmul(o, a10, v0, start=True, stop=False)
                        ins = pe.matmul(o, a11, v1, start=False, stop=True)
                    ins.then_inc(sem["pv_mm"], 1)

                def attn_turn(j):
                    if j == 0:
                        pe.wait_ge(*upto("attn_ready", l, 1))
                    if j == 3:
                        pe.wait_ge(*upto("attnT_ready", l, 1))
                    for kk in range(2):
                        for t in range(TT):
                            ins = pe.transpose(M[ATTNT_BANK[j]][:, kk * SEQ + t * P:kk * SEQ + (t + 1) * P],
                                               attn[:, 2 * j + kk, t, :], ident[:])
                    ins.then_inc(sem["attnT_mm"], 1)

                def ssd_turn(j):
                    pe.wait_ge(*upto("ssd_ready", l, j // 2 + 1))
                    if j in (1, 2):
                        pe.wait_ge(*upto("ssdT_ready", l, j))
                    if j == 3:
                        pe.wait_ge(*upto("attnT_ready", l, 3))
                    for kk in range(2):
                        for t in range(TT):
                            k = 2 * j + kk
                            ins = pe.transpose(M[SSDT_BANK[j]][:, kk * SEQ + t * P:kk * SEQ + (t + 1) * P],
                                               ys[:, t, k * P:(k + 1) * P], ident[:])
                    ins.then_inc(sem["ssdT_mm"], 1)

                def stay_warm():
                    for _ in range(WARM):
                        pe.matmul(M[0][:, 0:P], ident[:], ident[:], start=True, stop=True)

                stay_warm()
                x_turn(0, 0)
                x_turn(0, 1)
                for slot in range(MIX_SLOTS):
                    b, c = divmod(slot, NC)
                    if c == 0:
                        pe.wait_ge(*left(l, b, 0))
                    take(l * NB + b, c)
                    if b == 0:
                        pe.wait_ge(*upto("xT_ready" if c else "xT_hi", l, c + 1))
                    if b == B_OUT:
                        pe.wait_ge(*(upto("attnT_ready", l, c + 1) if c < 4 else upto("ssdT_ready", l, c - 3)))
                    if b < B_V:
                        feature_chunk(c, b % 2, upto("xT_ready", l, 1) if slot == 0 else None)
                    elif b < B_OUT:
                        token_chunk(c, b % 2, a_hi, a_lo)
                    else:
                        token_chunk(c, b % 2, u_hi, u_lo, slot == MIX_SLOTS - 1)
                    for j in NORM_PE.get(slot, ()):
                        x_turn(0, j)
                    if slot == PE_DT:
                        inv_row_and_dt()
                    if slot == PE_DT_TURN:
                        dt_turn()
                    if slot == PE_DECAY:
                        decays()
                    if PE_XTOK <= slot < PE_XTOK + TT * SG:
                        x_tokens(slot - PE_XTOK)
                    if slot == PE_CB:
                        b_tokens_and_cb()
                    if slot == PE_STATE:
                        states()
                    if slot in PE_YD:
                        y_diagonal(PE_YD.index(slot))
                    if slot in PE_YOFF:
                        y_offset(PE_YOFF.index(slot))
                    if slot in PE_SEG:
                        segment_sums(PE_SEG.index(slot))
                    if slot in PE_SCORE:
                        scores(PE_SCORE.index(slot))
                    if slot in PE_PT:
                        probs_turn(PE_PT.index(slot))
                    if slot in PE_PV:
                        values(PE_PV.index(slot))
                    if slot in PE_SSDT:
                        ssd_turn(PE_SSDT.index(slot))
                    if slot in PE_ATTNT:
                        attn_turn(PE_ATTNT.index(slot))

                def up_pair(q, i):
                    for j in range(2):
                        first = j == 0 and is_first(q, i)
                        if first:
                            stay_warm()
                            x_turn(1, 0)
                            x_turn(1, 1)
                        pe.wait_ge(*left(l, B_MLP + j, 0, q * QB + i))
                        for c in range(NC):
                            take(l * NB + q * (2 * QB) + i * 2 + (B_MLP + j), c)
                            hi_first = first and c == 0
                            pe.wait_ge(*upto("xT_hi" if hi_first else "xT_ready", l, 8 + c + 1))
                            feature_chunk(c, 1 - j, upto("xT_ready", l, 8 + 1) if hi_first else None)
                            if first:
                                for jj in NORM_PE.get(c, ()):
                                    x_turn(1, jj)

                def down_pair(q, i):
                    for j in range(2):
                        pe.wait_ge(*left(l, B_MLP + QB + j, 0, q * QB + i))
                        for c in range(NC):
                            take(l * NB + q * (2 * QB) + i * 2 + (B_MLP + QB + j), c)
                            pe.wait_ge(*upto("u_ready", l, q * (2 * QB) + (c + 1)))
                            last = type(q) is int and (i, j, c) == (QB // 2 - 1, 1, NC - 1)
                            token_chunk(c, 1 - j, u_hi, u_lo, last)

                up_pair(0, 0)
                up_pair(0, 1)
                with pe.Fori(0, QUARTERS - 1) as q:
                    with pe.Fori(0, QB // 2) as i:
                        down_pair(q, i)
                    with pe.Fori(0, QB // 2) as i:
                        up_pair(q + 1, i)
                down_pair(QUARTERS - 1, 0)
                down_pair(QUARTERS - 1, 1)

        @block.vector
        def _(dve):
            dve.memset(mx[:], 0.0).then_inc(sem["split_done"], RING)
            dve.memset(rs[:], 0.0).then_inc(sem["u_sq"], 2)
            tstep = [0]

            def tlink(ins):
                tstep[0] += 1
                ins.then_inc(once["table_step"], 1)
                dve.wait_ge(once["table_step"], tstep[0])

            def split_lo(b, c):
                dve.wait_ge(sem["hi_ready"], chunk(b, c) + 1)
                dve.tensor_tensor(w_lo[:, c % RING], raw[:, c % RING], w_hi[:, c % RING].bitcast(F32),
                                  ALU.subtract).then_inc(sem["split_done"], 1)

            inv_freq = (np.float32(THETA) ** (-np.arange(HALF, dtype=np.float32) / np.float32(HALF)))
            for i in range(HALF):
                ins = dve.memset(tab_f[:, i:i + 1], float(inv_freq[i]))
            tlink(dve.memset(freq[:, 1:2], 1.0))
            tlink(dve.memset(freq[0:HALF, 1:2], -1.0))
            dve.wait_ge(once["ident_ready"], 1)
            tlink(dve.tensor_tensor(tab_m, ident[0:ROPE, 0:HALF], ident[0:ROPE, HALF:ROPE], ALU.add))
            tlink(dve.tensor_tensor(tab_m, tab_m, tab_f, ALU.mult))
            tlink(dve.tensor_reduce(freq[:, 0:1], tab_m, AX.X, ALU.add))
            dve.wait_ge(once["pos_landed"], 16)
            tlink(dve.tensor_copy(tab_turn, tab_pos.bitcast(I32)))
            tlink(dve.tensor_scalar(tab_angle, tab_turn, freq[:, 0:1], None, ALU.mult))
            c1 = float(np.float32(6.28125))
            c2 = float(np.float32(np.round((2 * np.pi - c1) * 2 ** 18) / 2 ** 18))
            c3 = float(np.float32(2 * np.pi - c1 - c2))
            tlink(dve.tensor_scalar(tab_turn, tab_angle, float(1 / (2 * np.pi)), 1.5 * 2 ** 23, ALU.mult, ALU.add))
            tlink(dve.tensor_scalar(tab_turn, tab_turn, 1.5 * 2 ** 23, None, ALU.subtract))
            for part in (c1, c2, c3):
                tlink(dve.scalar_tensor_tensor(tab_angle, tab_turn, -part, tab_angle, ALU.mult, ALU.add))
            dve.tensor_scalar(tab_angle, tab_angle, 3.1415925, -3.1415925, ALU.min, ALU.max)\
                .then_inc(once["table_angle"], 1)
            for c in range(AHEAD):
                split_lo(0, c)
            dve.wait_ge(sem["prm_ready"], 1)
            for l in range(DEPTH):
                dve.tensor_copy(prm_next[:, l], M[2 + (l + 1) % DEPTH][:, 0:NPRM]).then_inc(once["prm_copied"], 1)

            with dve.Fori(0, DEPTH) as l:
                links = [0]

                def link(ins):
                    links[0] += 1
                    ins.then_inc(sem["dve_chain"], 1)
                    dve.wait_ge(*upto("dve_chain", l, links[0]))

                def x_lo(n, j, gain):
                    dve.wait_ge(*upto("xT_hi", l, 8 * n + j + 1))
                    for kk in range(2):
                        k = 2 * j + kk
                        ins = dve.scalar_tensor_tensor(a_lo[:, k], M[j % 4][:, kk * SEQ:(kk + 1) * SEQ],
                                                       prm[:, gain + k:gain + k + 1], a_hi[:, k].bitcast(F32),
                                                       ALU.mult, ALU.subtract)
                    ins.then_inc(sem["xT_ready"], 1)

                def x_mean(squares):
                    dve.wait_ge(*upto("squared", l, squares))
                    link(dve.tensor_reduce(st[:, X_SUM], sq[:], AX.X, ALU.add))
                    dve.tensor_scalar(st[:, X_MS], st[:, X_SUM], 1.0 / D, EPS, ALU.mult, ALU.add)\
                        .then_inc(sem["x_ms"], 1)

                def to_lo(name, n, j, bank, gain):
                    dve.wait_ge(*upto(name + "_hi", l, n))
                    for kk in range(2):
                        k = 2 * j + kk
                        ins = dve.scalar_tensor_tensor(u_lo[:, k], M[bank][:, kk * SEQ:(kk + 1) * SEQ],
                                                       prm[:, gain + k:gain + k + 1], u_hi[:, k].bitcast(F32),
                                                       ALU.mult, ALU.subtract)
                    ins.then_inc(sem[name + "_ready"], 1)

                def y_mean(squares):
                    dve.wait_ge(*upto("squared", l, squares))
                    link(dve.tensor_reduce(st[:, Y_SUM], ysq[:], AX.X, ALU.add))
                    if squares == SQ_Y0:
                        ins = dve.tensor_scalar(st[:, Y_MS], st[:, Y_SUM], 1.0 / D, EPS, ALU.mult, ALU.add)
                    else:
                        ins = dve.scalar_tensor_tensor(st[:, Y_MS], st[:, Y_SUM], 1.0 / D, st[:, X_EPS],
                                                       ALU.mult, ALU.add)
                    ins.then_inc(sem["y_ms"], 1)

                def update_x(n, c):
                    cols = slice(c * CB, (c + 1) * CB)
                    if c == 0:
                        dve.wait_ge(*upto("y_inv", l, n + 1))
                    for t in range(TT):
                        dve.wait_ge(*(upto("y_gained", l, 2 * c + t + 1) if n else left(l, B_OUT + c, t + 1)))
                        dve.scalar_tensor_tensor(x_sb[:, t, cols], y[:, t, cols], st[:, Y_INV, t:t + 1],
                                                 x_sb[:, t, cols], ALU.mult, ALU.add).then_inc(sem["x_ready"], 1)

                def norm_turn(n, slot, gain, split):
                    for j in NORM_BEFORE.get(slot, ()):
                        if n and slot == AHEAD:
                            update_x(0, j)
                        x_lo(n, j, gain)
                    split()
                    if n and slot in (AHEAD, AHEAD + 1):
                        update_x(0, slot - AHEAD + 2)
                    for j in NORM_BEHIND.get(slot, ()):
                        x_lo(n, j, gain)

                def dt_steps():
                    dve.wait_ge(*upto("dt_turned", l, 1))
                    dve.wait_ge(*upto("x_inv", l, 1))
                    for t in range(TT):
                        for part in range(2):
                            src = M[1][:, t * P + part * SH:t * P + (part + 1) * SH]
                            link(dve.scalar_tensor_tensor(dts[:, DT_IN, t], src, st[:, X_INV, t:t + 1],
                                                          dts[:, DT_IN, t] if part else row[:, 0],
                                                          ALU.mult, ALU.add))
                    dve.scalar_tensor_tensor(dts[:, DT_ABS], dts[:, DT_IN], -1.0, dts[:, DT_IN], ALU.mult, ALU.max)\
                        .then_inc(sem["dt_abs"], 1)
                    dve.wait_ge(*upto("dt_exp", l, 1))
                    link(dve.tensor_scalar(dts[:, DT_TMP], dts[:, DT_EXP], 2.0, None, ALU.add))
                    link(dve.reciprocal(dts[:, DT_TMP], dts[:, DT_TMP]))
                    link(dve.tensor_tensor(dts[:, DT_S], dts[:, DT_EXP], dts[:, DT_TMP], ALU.mult))
                    link(dve.tensor_tensor(dts[:, DT_S2], dts[:, DT_S], dts[:, DT_S], ALU.mult))
                    link(dve.tensor_scalar(dts[:, DT], dts[:, DT_S2], 1.0 / 17, None, ALU.mult))
                    for k in (15, 13, 11, 9, 7, 5, 3):
                        link(dve.scalar_tensor_tensor(dts[:, DT], dts[:, DT], 1.0 / k, dts[:, DT_S2],
                                                      ALU.add, ALU.mult))
                    link(dve.scalar_tensor_tensor(dts[:, DT], dts[:, DT], 1.0, dts[:, DT_S], ALU.add, ALU.mult))
                    link(dve.tensor_scalar(dts[:, DT_TMP], dts[:, DT_IN], 0.0, None, ALU.max))
                    link(dve.scalar_tensor_tensor(dts[:, DT], dts[:, DT], 2.0, dts[:, DT_TMP], ALU.mult, ALU.add))
                    dve.wait_ge(*upto("row_exp", l, 1))
                    link(dve.scalar_tensor_tensor(dts[:, A_DT], dts[:, DT], -1.0,
                                                  row[:, 1].unsqueeze(1).broadcast_to([P, TT, SH]),
                                                  ALU.mult, ALU.mult))
                    dve.tensor_copy(adt_hi[:], dts[:, A_DT]).then_inc(sem["adt_hi_ready"], 1)
                    dve.wait_ge(*upto("adt_hi_ready", l, 1))
                    dve.tensor_tensor(adt_lo[:], dts[:, A_DT], adt_hi[:].bitcast(F32), ALU.subtract)\
                        .then_inc(sem["adt_ready"], 1)

                def conv(b, k):
                    n0 = 16 * b + 8 * k
                    dve.wait_ge(*left(l, b, k + 1))
                    for tap in range(TAPS - 1, -1, -1):
                        for m in range(2):
                            ct = 4 * b + 2 * k + m
                            n = n0 + 2 * (TAPS - 1 - tap) + m
                            src = convr[:, k, m, tap:tap + SEQ]
                            wt = prm[:, G_TAP + tap * NCT + ct:G_TAP + tap * NCT + ct + 1]
                            if tap == TAPS - 1:
                                ins = dve.tensor_scalar(xbcT[:, ct], src, wt, prm[:, G_BIAS + ct:G_BIAS + ct + 1],
                                                        ALU.mult, ALU.add)
                            else:
                                dve.wait_ge(*upto("conv_step", l, n - 1))
                                ins = dve.scalar_tensor_tensor(xbcT[:, ct], src, wt, xbcT[:, ct],
                                                               ALU.mult, ALU.add)
                            ins.then_inc(sem["conv_step"], 1)

                def two(a):
                    return a.rearrange("p (m s) -> p m s", m=2)

                inv_two = inv_row[:].unsqueeze(1).broadcast_to([P, 2, SEQ])

                dve.wait_ge(*upto("prm_ready", l, 1))
                for slot in range(AHEAD, MIX_SLOTS + AHEAD):
                    b, c = divmod(slot, NC)
                    if slot in AD_ROPE:
                        r = AD_ROPE.index(slot)
                        dve.wait_ge(*left(l, B_Q + r // 2, r % 2 + 1))
                        if r:
                            dve.wait_ge(*upto("rope_ready", l, r))
                    norm_turn(0, slot, G_MIX, lambda: split_lo(l * NB + b, c))
                    if slot == AHEAD + 4:
                        x_mean(SQ_X0)
                    if slot == AD_DIAG:
                        dve.wait_ge(*upto("x_inv", l, 1))
                        for t in range(TT):
                            ins = dve.tensor_scalar(diag[:, t], ident[:], st[:, X_INV, t:t + 1], None, ALU.mult)
                        ins.then_inc(sem["diag_ready"], 1)
                        dve.wait_ge(*upto("wdt_hi_ready", l, 1))
                        dve.tensor_tensor(wdt_lo, wdt, wdt_hi.bitcast(F32), ALU.subtract)\
                            .then_inc(sem["wdt_ready"], 1)
                    for i in range(B_V):
                        if slot == leaves(i):
                            dve.wait_ge(*through(l, i))
                            dve.wait_ge(*upto("inv_row_ready", l, 1))
                            for k in range(2):
                                r = (i - B_Q) * 2 + k
                                dst = convr[:, k, :, TAPS - 1:] if i < B_Q else qk[:, 2 * r:2 * r + 2]
                                dve.tensor_tensor(dst, two(acc[i % 2][k][:]), inv_two, ALU.mult)\
                                    .then_inc(acc_free[i % 2], 1)
                        if i < B_Q and slot in (leaves(i) + 1, leaves(i) + 2):
                            conv(i, slot - leaves(i) - 1)
                    if slot == AD_DTT:
                        dve.wait_ge(*upto("dt_mm", l, 1))
                        dve.tensor_copy(dtT, M[1][:, 0:SEQ]).then_inc(sem["dtT_ready"], 1)
                    if slot == AD_DT:
                        dt_steps()
                    if slot == AD_XDT:
                        for i in range(TT * SG):
                            t, g = divmod(i, SG)
                            dve.wait_ge(*upto("skip_done", l, i + 1))
                            dve.tensor_tensor(heads8(x_tok, t, g), heads8(x_tok, t, g), per_head(dts[:, DT, t], g),
                                              ALU.mult).then_inc(sem["xdt_ready"], 1)
                    if slot == AD_XDT + 1:
                        dve.wait_ge(*upto("xdt_ready", l, 4))
                        dve.wait_ge(*upto("decay_ready", l, 1))
                        for g in range(SG):
                            dve.tensor_tensor(wk[:, 2 + g].rearrange("p (h n) -> p h n", n=SP_),
                                              heads8(x_tok, 0, g), per_head(decay[:, 0], g), ALU.mult)\
                                .then_inc(sem["xdd_ready"], 1)
                    if slot == AD_CB:
                        dve.wait_ge(*upto("cb_mm", l, 1))
                        dve.tensor_tensor(cbm[:], four(M[1][:]), tri[:].unsqueeze(1).broadcast_to([P, 4, P]),
                                          ALU.mult).then_inc(sem["cbm_ready"], 1)
                    for i in range(8):
                        if slot == AD_SEG[i]:
                            dve.wait_ge(*upto("sege_ready", l, i + 1))
                            dve.tensor_tensor(four(seg_e), four(seg_e),
                                              cbm[:, i // 2].unsqueeze(1).broadcast_to([P, 4, P]), ALU.mult)\
                                .then_inc(sem["segm_ready"], 1)
                    for j in range(4):
                        if slot == AD_Y[j]:
                            t, g = divmod(j, SG)
                            dve.wait_ge(*upto("yd_mm", l, 2 * j + 2))
                            ysg = ys[:, t, g * CB:(g + 1) * CB]
                            dve.tensor_tensor(ysg, ysg, M[3 * g][:], ALU.add).then_inc(sem["y_added"], 1)
                            if t:
                                dve.wait_ge(*upto("yoff_mm", l, g + 1))
                                dve.tensor_tensor(wk[:, 2 + g].rearrange("p (h n) -> p h n", n=SP_),
                                                  M[2 - g][:].rearrange("p (h n) -> p h n", n=SP_),
                                                  per_head(decay[:, 1], g), ALU.mult).then_inc(sem["yoff_mul"], 1)
                                dve.wait_ge(*upto("yoff_mul", l, g + 1))
                                dve.wait_ge(*upto("y_added", l, j + 1))
                                dve.tensor_tensor(ysg, ysg, wk[:, 2 + g], ALU.add).then_inc(sem["yoff_added"], 1)
                    for r in range(8):
                        if slot == AD_ROPE[r]:
                            dve.stream_shuffle(rope_t, qk[0:ROPE, 2 * r:2 * r + 2],
                                               [(i + HALF) % ROPE for i in range(ROPE)])\
                                .then_inc(sem["rope_swapped"], 1)
                            dve.wait_ge(*upto("rope_swapped", l, r + 1))
                            dve.tensor_tensor(rope_t, rope_t,
                                              sinT[:].unsqueeze(1).broadcast_to([ROPE, 2, SEQ]), ALU.mult)\
                                .then_inc(sem["rope_mul"], 1)
                        if slot == AD_ROPE[r] + 1:
                            dve.wait_ge(*upto("rope_mul", l, r + 1))
                            dve.wait_ge(*upto("rope_cos", l, r + 1))
                            rot = qk[0:ROPE, 2 * r:2 * r + 2]
                            dve.tensor_tensor(rot, rot, rope_t, ALU.add).then_inc(sem["rope_ready"], 1)
                    for p in range(4):
                        if slot == AD_SOFT[p]:
                            dve.wait_ge(*upto("score_mm", l, p + 1))
                            mxv = mx[:].rearrange("p (h t) -> p h t", t=TT)
                            link(dve.tensor_reduce(mxv[:, :, 1], two(M[0][:]), AX.X, ALU.max))
                            link(dve.tensor_reduce(mxv[:, :, 0], two(M[3][:, 0:2 * P]), AX.X, ALU.max))
                            dve.tensor_scalar(mx[:], mx[:], -(DH ** -0.5), None, ALU.mult)\
                                .then_inc(sem["nmax_ready"], 1)
                        if slot == AD_PT[p]:
                            dve.wait_ge(*upto("pt_mm", l, p + 1))
                            dve.tensor_copy(probsT[:, 3 * P:6 * P], M[3][:, 0:3 * P]).then_inc(sem["pt_v"], 1)
                            link(dve.reciprocal(rinv[:], rs[:]))
                        if slot == AD_O[p]:
                            dve.wait_ge(*upto("pv_mm", l, p + 1))
                            dve.tensor_tensor(four(ybuf[:, p * CB:(p + 1) * CB]), four(M[1][:]),
                                              rinv[:].unsqueeze(2).broadcast_to([P, 4, P]), ALU.mult)\
                                .then_inc(sem["attn_out"], 1)
                    if slot == AD_ATTN_NORM:
                        dve.wait_ge(*upto("squared", l, SQ_A))
                        dve.tensor_scalar(st[:, A_MS], ssq[:, 0], 1.0 / AW, EPS, ALU.mult, ALU.add)\
                            .then_inc(sem["attn_ms"], 1)
                    if slot == AD_ATTN_NORM + 1:
                        dve.wait_ge(*upto("attn_inv", l, 1))
                        for t in range(TT):
                            ins = dve.tensor_scalar(attn[:, :, t], attn[:, :, t], st[:, A_INV, t:t + 1], None,
                                                    ALU.mult)
                        ins.then_inc(sem["attn_ready"], 1)
                    for g in range(SG):
                        ms, inv = (S0_MS, S0_INV) if g == 0 else (S1_MS, S1_INV)
                        if slot == leaves(B_Z + g):
                            dve.wait_ge(*left(l, B_Z + g, 2))
                            dve.wait_ge(*upto("yoff_added", l, 2))
                            for t in range(TT):
                                ysg = ys[:, t, g * CB:(g + 1) * CB]
                                ins = dve.tensor_tensor(ysg, ysg, zs[:, t, g * CB:(g + 1) * CB], ALU.mult)
                            ins.then_inc(sem["gated"], 1)
                        if slot == leaves(B_Z + g) + 1:
                            dve.wait_ge(*upto("squared", l, SQ_S1 if g else SQ_S0))
                            dve.tensor_scalar(st[:, ms], ssq[:, 1 + g], 1.0 / CB, EPS, ALU.mult, ALU.add)\
                                .then_inc(sem["ssd_ms"], 1)
                        if slot == leaves(B_Z + g) + 2:
                            dve.wait_ge(*upto("ssd_inv", l, g + 1))
                            for t in range(TT):
                                ysg = ys[:, t, g * CB:(g + 1) * CB]
                                ins = dve.tensor_scalar(ysg, ysg, st[:, inv, t:t + 1], None, ALU.mult)
                            ins.then_inc(sem["ssd_ready"], 1)
                    for i in range(4):
                        if slot == leaves(B_OUT + i):
                            if i == 0:
                                dve.wait_ge(*upto("gain_landed", l, 16))
                            for t in range(TT):
                                cols = slice(i * CB, (i + 1) * CB)
                                dve.wait_ge(*upto("squared", l, SQ_S1 + 2 * i + t + 1))
                                if i == 3 and t == TT - 1:
                                    y_mean(SQ_Y0)
                                dve.tensor_tensor(y[:, t, cols], acc[(B_OUT + i) % 2][t][:], zg[:, cols], ALU.mult)\
                                    .then_inc(acc_free[(B_OUT + i) % 2], 1)
                    for j in range(4):
                        if slot == AD_SSDT[j]:
                            to_lo("ssdT", j + 1, 4 + j, SSDT_BANK[j], G_ATTN)
                        if slot == AD_ATTNT[j]:
                            to_lo("attnT", j + 1, j, ATTNT_BANK[j], G_ATTN)

                def up_pair(q, i):
                    for j in range(2):
                        b = l * NB + q * (2 * QB) + i * 2 + (B_MLP + j)
                        first = j == 0 and is_first(q, i)
                        for c in range(AHEAD, NC + AHEAD):
                            split = (lambda: split_lo(b, c)) if c < NC else (lambda: split_lo(b + 1, c - NC))
                            if first:
                                norm_turn(1, c, G_MLP, split)
                            else:
                                split()
                            if j == 1 and is_first(q, i) and c >= NC - 1:
                                dve.wait_ge(*upto("x_ready", l, 16))
                                n = c - (NC - 1)
                                dve.memset(ybuf[:, n * 2 * CB:(n + 1) * 2 * CB], 0.0).then_inc(sem["y_zero"], 1)
                        if first:
                            dve.wait_ge(*upto("squared", l, SQ_X1))
                            link(dve.tensor_reduce(st[:, X_SUM], sq[:], AX.X, ALU.add))
                            link(dve.tensor_scalar(st[:, X_MS], st[:, X_SUM], 1.0 / D, EPS, ALU.mult, ALU.add))
                            link(dve.scalar_tensor_tensor(st[:, X_EPS], st[:, X_MS], EPS, st[:, X_MS],
                                                          ALU.mult, ALU.mult))
                        for k in range(2):
                            n = q * (2 * QB) + i * 4 + (2 * j + k)
                            dve.wait_ge(*left(l, B_MLP + j, k + 1, q * QB + i))
                            dve.tensor_tensor(wk[:, 2 + k], wk[:, k], wk[:, k], ALU.mult)\
                                .then_inc(sem["u_sq"], 1)
                            dve.wait_ge(*upto("u_sq", l, n + 3))
                            dve.wait_ge(*upto("u_hi_ready", l, n + 1))
                            k0 = i * 8 + (4 * j + 2 * k)
                            uh, ul = (a[:, k0:k0 + 2] if type(i) is int else a[:, bass.ds(k0, 2)]
                                      for a in (u_hi, u_lo))
                            dve.tensor_tensor(ul.rearrange("p k s -> p (k s)"), wk[:, 2 + k],
                                              uh.rearrange("p k s -> p (k s)").bitcast(F32),
                                              ALU.subtract).then_inc(sem["u_ready"], 1)

                def down_pair(q, i):
                    for j in range(2):
                        b = l * NB + q * (2 * QB) + i * 2 + (B_MLP + QB + j)
                        for c in range(AHEAD, NC):
                            split_lo(b, c)
                        for c in range(AHEAD):
                            split_lo(b + 1, c)
                        last = type(q) is int
                        n = 2 * i + j
                        if not last:
                            dve.wait_ge(*upto("y_zero", l, 4))
                        for t in range(TT):
                            yp = y[:, t, n * CB:(n + 1) * CB] if last else \
                                y[:, t, bass.ds(i * (2 * CB) + j * CB, CB)]
                            if last and (n, t) == (QB - 1, 0):
                                dve.wait_ge(*upto("tile_done", l, 2))
                            else:
                                dve.wait_ge(sem["mm_done"], RING + chunk(b + 1, 0))
                            dve.tensor_tensor(yp, yp, acc[1 - j][t][:], ALU.add).then_inc(acc_free[1 - j], 1)
                        if last:
                            if n == 0:
                                dve.wait_ge(*upto("gain_landed", l, 32))
                            for t in range(TT):
                                dve.wait_ge(*upto("squared", l, SQ_X1 + 2 * n + t + 1))
                                yp = y[:, t, n * CB:(n + 1) * CB]
                                if n == QB - 1 and t == TT - 1:
                                    y_mean(SQ_Y1)
                                dve.tensor_tensor(yp, yp, zg[:, n * CB:(n + 1) * CB], ALU.mult)\
                                    .then_inc(sem["y_gained"], 1)

                up_pair(0, 0)
                up_pair(0, 1)
                with dve.Fori(0, QUARTERS - 1) as q:
                    with dve.Fori(0, QB // 2) as i:
                        down_pair(q, i)
                    with dve.Fori(0, QB // 2) as i:
                        up_pair(q + 1, i)
                down_pair(QUARTERS - 1, 0)
                down_pair(QUARTERS - 1, 1)
                for c in range(4):
                    update_x(1, c)
                assert links[0] == DVE_LINKS, links[0]


_INS = ["x", "positions", "pre_mix_norm", "post_mix_norm", "pre_mlp_norm", "post_mlp_norm", "w_in", "conv_w",
        "conv_b", "dt_bias", "a_log", "d_skip", "attn_out_norm", "ssd_out_norm", "w_out", "w_up", "w_down"]


def kernel(**inputs):
    import concourse.bacc as bacc
    from concourse.bass_utils import run_bass_kernel_spmd

    nc = bacc.Bacc("TRN2", target_bir_lowering=False, num_devices=1)
    arrays, args = {}, []
    for name in _INS:
        a = np.ascontiguousarray(inputs[name])
        arrays[f"in_{name}"] = a
        args.append(nc.dram_tensor(f"in_{name}", a.shape, mybir.dt.from_np(a.dtype), kind="ExternalInput").ap())
    args.append(nc.dram_tensor("out_0", (1, SEQ, D), F32, kind="ExternalOutput").ap())
    trunk(nc, *args)
    r = run_bass_kernel_spmd(nc, [arrays], core_ids=[0])
    return r.results[0]["out_0"]
```
